# Optimizing a Trainium2 kernel written in Bass

```python
import math
import jax, jax.numpy as jnp
from jax import lax
import numpy as np

D_MODEL = 2048
BATCH = 1
SEQ = 256
DEPTH = 1

N_META = 16
EPS = 1e-6
MLA_HEADS = 16
Q_LORA = 512
KV_LORA = 512
QK_NOPE = 128
QK_ROPE = 64
V_HEAD = 128
ROPE_THETA = 10000.0
Q_BLOCK = 128
SSM_WIDTH = 1024
SSM_GROUP = 16
SSM_GROUPS = SSM_WIDTH // SSM_GROUP
SSM_STATE = 64
DT_MIN = 1e-3
DT_MAX = 1e-1
N_BRANCH = 2
D_FF = -(-8 * D_MODEL // (3 * 256)) * 256
OFF_Q = Q_LORA
OFF_KV = OFF_Q + KV_LORA
OFF_KR = OFF_KV + QK_ROPE
OFF_U = OFF_KR + SSM_WIDTH
IN_WIDTH = OFF_U + N_BRANCH * D_MODEL


def rms_norm(x, g):
    xf = x.astype(jnp.float32)
    y = xf * lax.rsqrt(jnp.mean(xf * xf, axis=-1, keepdims=True) + EPS)
    return y.astype(x.dtype) * g.astype(x.dtype)

def rope_tables(length):
    half = QK_ROPE // 2
    freqs = ROPE_THETA ** (-jnp.arange(half, dtype=jnp.float32) / half)
    ang = jnp.arange(length, dtype=jnp.float32)[:, None] * freqs[None, :]
    return jnp.cos(ang), jnp.sin(ang)

def apply_rope(x, cos, sin):
    half = QK_ROPE // 2
    x1, x2 = x[..., :half], x[..., half:]
    c, s = cos.astype(x.dtype), sin.astype(x.dtype)
    return jnp.concatenate([x1 * c - x2 * s, x2 * c + x1 * s], axis=-1)

def mla_attention(q_nope, q_rope, k_nope, k_rope, v):
    length = q_nope.shape[1]
    scale = (QK_NOPE + QK_ROPE) ** -0.5
    outs = []
    for start in range(0, length, Q_BLOCK):
        end = min(start + Q_BLOCK, length)
        s = (jnp.einsum('bqhd,bkhd->bhqk', q_nope[:, start:end], k_nope[:, :end])
             + jnp.einsum('bqhr,bkr->bhqk', q_rope[:, start:end], k_rope[:, :end]))
        s = s.astype(jnp.float32) * scale
        q_pos = jnp.arange(start, end)[:, None]
        k_pos = jnp.arange(end)[None, :]
        s = jnp.where(k_pos <= q_pos, s, -jnp.inf)
        p = jax.nn.softmax(s, axis=-1).astype(v.dtype)
        outs.append(jnp.einsum('bhqk,bkhd->bqhd', p, v[:, :end]))
    return jnp.concatenate(outs, axis=1)

def s5_scan(u, lam_re, lam_im, log_step, b_re, b_im, c_re, c_im, d):
    f32 = jnp.float32
    step = jnp.exp(log_step.astype(f32))[:, None]
    lr, li = lam_re.astype(f32), lam_im.astype(f32)
    mag = jnp.exp(lr * step)
    ab_re, ab_im = mag * jnp.cos(li * step), mag * jnp.sin(li * step)
    den = lr * lr + li * li
    nr, ni = ab_re - 1.0, ab_im
    coef_re = (nr * lr + ni * li) / den
    coef_im = (ni * lr - nr * li) / den
    br, bi = b_re.astype(f32), b_im.astype(f32)
    bb_re = coef_re[..., None] * br - coef_im[..., None] * bi
    bb_im = coef_re[..., None] * bi + coef_im[..., None] * br
    uf = u.astype(f32)
    bu_re = jnp.einsum('blgp,gnp->blgn', uf, bb_re)
    bu_im = jnp.einsum('blgp,gnp->blgn', uf, bb_im)
    a_re = jnp.broadcast_to(ab_re, bu_re.shape)
    a_im = jnp.broadcast_to(ab_im, bu_im.shape)

    def combine(e1, e2):
        a1r, a1i, b1r, b1i = e1
        a2r, a2i, b2r, b2i = e2
        return (a2r * a1r - a2i * a1i,
                a2r * a1i + a2i * a1r,
                a2r * b1r - a2i * b1i + b2r,
                a2r * b1i + a2i * b1r + b2i)

    _, _, x_re, x_im = lax.associative_scan(combine, (a_re, a_im, bu_re, bu_im), axis=1)
    y = (jnp.einsum('blgn,gpn->blgp', x_re, c_re.astype(f32))
         - jnp.einsum('blgn,gpn->blgp', x_im, c_im.astype(f32))
         + d.astype(f32) * uf)
    return y

def first_inputs(seed: int = 0) -> dict:
    key = jax.random.key(seed)
    ks = jax.random.split(key, 32)
    f32 = jnp.float32
    nrm = lambda k, shape, scale: jax.random.normal(k, shape, f32) * scale
    gain = lambda k, shape: 1.0 + 0.02 * jax.random.normal(k, shape, f32)
    G, N, P = SSM_GROUPS, SSM_STATE, SSM_GROUP
    lam_re = -0.5 * jnp.exp(0.05 * jax.random.normal(ks[9], (DEPTH, G, N), f32))
    lam_im = jnp.broadcast_to(math.pi * jnp.arange(N, dtype=f32), (DEPTH, G, N))
    log_step = jax.random.uniform(ks[10], (DEPTH, G), f32, math.log(DT_MIN), math.log(DT_MAX))
    return {
        "x": nrm(ks[0], (BATCH, SEQ, D_MODEL), 1.0),
        "meta_tokens": nrm(ks[1], (N_META, D_MODEL), 1.0),
        "norm_mix": gain(ks[2], (DEPTH, D_MODEL)),
        "w_in": nrm(ks[3], (DEPTH, D_MODEL, IN_WIDTH), D_MODEL ** -0.5),
        "norm_q": gain(ks[4], (DEPTH, Q_LORA)),
        "w_q_up": nrm(ks[5], (DEPTH, Q_LORA, MLA_HEADS * (QK_NOPE + QK_ROPE)), Q_LORA ** -0.5),
        "norm_kv": gain(ks[6], (DEPTH, KV_LORA)),
        "w_kv_up": nrm(ks[7], (DEPTH, KV_LORA, MLA_HEADS * (QK_NOPE + V_HEAD)), KV_LORA ** -0.5),
        "w_attn_proj": nrm(ks[8], (DEPTH, MLA_HEADS * V_HEAD, D_MODEL), (MLA_HEADS * V_HEAD) ** -0.5),
        "ssm_lambda_re": lam_re,
        "ssm_lambda_im": lam_im,
        "ssm_log_step": log_step,
        "ssm_b_re": nrm(ks[11], (DEPTH, G, N, P), (2 * P) ** -0.5),
        "ssm_b_im": nrm(ks[12], (DEPTH, G, N, P), (2 * P) ** -0.5),
        "ssm_c_re": nrm(ks[13], (DEPTH, G, P, N), N ** -0.5),
        "ssm_c_im": nrm(ks[14], (DEPTH, G, P, N), N ** -0.5),
        "ssm_d": nrm(ks[15], (DEPTH, G, P), 1.0),
        "w_glu_val": nrm(ks[16], (DEPTH, SSM_WIDTH, D_MODEL), SSM_WIDTH ** -0.5),
        "w_glu_gate": nrm(ks[17], (DEPTH, SSM_WIDTH, D_MODEL), SSM_WIDTH ** -0.5),
        "w_out": nrm(ks[18], (DEPTH, D_MODEL, D_MODEL), D_MODEL ** -0.5),
        "norm_ffn": gain(ks[19], (DEPTH, D_MODEL)),
        "w_ffn_gate": nrm(ks[20], (DEPTH, D_MODEL, D_FF), D_MODEL ** -0.5),
        "w_ffn_up": nrm(ks[21], (DEPTH, D_MODEL, D_FF), D_MODEL ** -0.5),
        "w_ffn_down": nrm(ks[22], (DEPTH, D_FF, D_MODEL), D_FF ** -0.5),
        "norm_final": gain(ks[23], (D_MODEL,)),
    }

def first_block(x, meta_tokens, norm_mix, w_in, norm_q, w_q_up, norm_kv, w_kv_up, w_attn_proj,
              ssm_lambda_re, ssm_lambda_im, ssm_log_step, ssm_b_re, ssm_b_im, ssm_c_re, ssm_c_im,
              ssm_d, w_glu_val, w_glu_gate, w_out, norm_ffn, w_ffn_gate, w_ffn_up, w_ffn_down,
              norm_final):
    bsz = x.shape[0]
    meta = jnp.broadcast_to(meta_tokens[None].astype(x.dtype), (bsz, N_META, D_MODEL))
    h = jnp.concatenate([meta, x], axis=1)
    length = h.shape[1]
    cos, sin = rope_tables(length)
    for l in range(DEPTH):
        n = rms_norm(h, norm_mix[l])
        z = n @ w_in[l]
        q_lat, kv_lat, k_r, u, gates = jnp.split(z, [OFF_Q, OFF_KV, OFF_KR, OFF_U], axis=-1)
        q = (rms_norm(q_lat, norm_q[l]) @ w_q_up[l]).reshape(bsz, length, MLA_HEADS, QK_NOPE + QK_ROPE)
        kv = (rms_norm(kv_lat, norm_kv[l]) @ w_kv_up[l]).reshape(bsz, length, MLA_HEADS, QK_NOPE + V_HEAD)
        q_nope = q[..., :QK_NOPE]
        q_rope = apply_rope(q[..., QK_NOPE:], cos[:, None, :], sin[:, None, :])
        k_nope, v = kv[..., :QK_NOPE], kv[..., QK_NOPE:]
        k_rope = apply_rope(k_r, cos, sin)
        attn = mla_attention(q_nope, q_rope, k_nope, k_rope, v).reshape(bsz, length, MLA_HEADS * V_HEAD)
        attn_out = attn @ w_attn_proj[l]
        y = s5_scan(u.reshape(bsz, length, SSM_GROUPS, SSM_GROUP),
                    ssm_lambda_re[l], ssm_lambda_im[l], ssm_log_step[l],
                    ssm_b_re[l], ssm_b_im[l], ssm_c_re[l], ssm_c_im[l], ssm_d[l])
        y = jax.nn.gelu(y.reshape(bsz, length, SSM_WIDTH).astype(h.dtype))
        ssm_out = (y @ w_glu_val[l]) * jax.nn.sigmoid(y @ w_glu_gate[l])
        g = gates.reshape(bsz, length, N_BRANCH, D_MODEL)
        mixed = jax.nn.sigmoid(g[:, :, 0]) * attn_out + jax.nn.sigmoid(g[:, :, 1]) * ssm_out
        h = h + mixed @ w_out[l]
        m = rms_norm(h, norm_ffn[l])
        h = h + (jax.nn.silu(m @ w_ffn_gate[l]) * (m @ w_ffn_up[l])) @ w_ffn_down[l]
    out = rms_norm(h, norm_final)
    return out[:, N_META:]


DEPTH_2 = 2

CHUNK = 64
N_A_LAYERS = DEPTH_2 // 2
N_B_LAYERS = DEPTH_2 - N_A_LAYERS

A_INNER = 2 * D_MODEL
A_HEADS = 8
A_DV = A_INNER // A_HEADS
A_QK = A_INNER // 2
A_DK = A_QK // A_HEADS
CONV_W = 4
A_COLS = 2 * A_QK + 3 * A_INNER + 2 * A_HEADS
A_V0 = 2 * A_QK
A_O0 = A_V0 + A_INNER
A_Z0 = A_O0 + A_INNER
A_G0 = A_Z0 + A_INNER

B_HEADS = 16
B_DH = D_MODEL // B_HEADS
B_WIDTH = B_HEADS * B_DH
LEFT_CHUNKS = 8
BAND = (LEFT_CHUNKS + 1) * CHUNK
MAX_REL = 128


F32 = jnp.float32

def rmsnorm(x, g):
    xf = x.astype(F32)
    return xf * lax.rsqrt(jnp.mean(xf * xf, axis=-1, keepdims=True) + EPS) * g.astype(F32)

def modulate(hn, shift, scale):
    return hn * (1.0 + scale[:, None, :]) + shift[:, None, :]

def causal_conv(u, w, b):
    S = u.shape[1]
    up = jnp.pad(u, ((0, 0), (CONV_W - 1, 0), (0, 0)))
    out = b
    for j in range(CONV_W):
        out = out + up[:, j:j + S] * w[j]
    return out

def mlstm_chunkwise(q, k, v, li, lf):
    Bn, H, S, DK = q.shape
    DV = v.shape[-1]
    NC = S // CHUNK

    def to_chunks(a):
        return jnp.moveaxis(a.reshape(Bn, H, NC, CHUNK, *a.shape[3:]), 2, 0)

    qc, kc, vc, lic, lfc = (to_chunks(a) for a in (q, k * (DK ** -0.5), v, li, lf))
    causal = jnp.tril(jnp.ones((CHUNK, CHUNK), bool))

    def step(carry, inp):
        C, n, m = carry
        qi, ki, vi, lii, lfi = inp
        b = jnp.cumsum(lfi, axis=-1)
        dmat = b[..., :, None] - b[..., None, :] + lii[..., None, :]
        dmat = jnp.where(causal, dmat, -jnp.inf)
        inter = b + m[..., None]
        m_t = jnp.maximum(inter, jnp.max(dmat, axis=-1))
        w_intra = jnp.exp(dmat - m_t[..., None])
        w_inter = jnp.exp(inter - m_t)
        s = jnp.einsum('bhtd,bhsd->bhts', qi, ki) * w_intra
        num = (w_inter[..., None] * jnp.einsum('bhtd,bhde->bhte', qi, C)
               + jnp.einsum('bhts,bhse->bhte', s, vi))
        den = w_inter * jnp.einsum('bhtd,bhd->bht', qi, n) + jnp.sum(s, axis=-1)
        h = num / jnp.maximum(jnp.abs(den), jnp.exp(-m_t))[..., None]
        b_last = b[..., -1]
        g_s = b_last[..., None] - b + lii
        m_new = jnp.maximum(b_last + m, jnp.max(g_s, axis=-1))
        decay = jnp.exp(b_last + m - m_new)
        ws = jnp.exp(g_s - m_new[..., None])
        C_new = decay[..., None, None] * C + jnp.einsum('bhs,bhsd,bhse->bhde', ws, ki, vi)
        n_new = decay[..., None] * n + jnp.einsum('bhs,bhsd->bhd', ws, ki)
        return (C_new, n_new, m_new), h

    init = (jnp.zeros((Bn, H, DK, DV), F32), jnp.zeros((Bn, H, DK), F32), jnp.zeros((Bn, H), F32))
    _, hs = lax.scan(step, init, (qc, kc, vc, lic, lfc))
    return jnp.moveaxis(hs, 0, 2).reshape(Bn, H, S, DV)

def mlstm_mixer(h, w_in, conv_w, conv_b, gate_b, g_head, w_out):
    Bn, S, _ = h.shape
    proj = h @ w_in
    qk = jax.nn.silu(causal_conv(proj[..., :A_V0].astype(F32), conv_w.astype(F32), conv_b.astype(F32)))
    v = proj[..., A_V0:A_O0]
    o = proj[..., A_O0:A_Z0]
    z = proj[..., A_Z0:A_G0]
    gates = proj[..., A_G0:].astype(F32) + gate_b.astype(F32)

    def heads(a, d):
        return a.astype(F32).reshape(Bn, S, A_HEADS, d).transpose(0, 2, 1, 3)

    li = gates[..., :A_HEADS].transpose(0, 2, 1)
    lf = jax.nn.log_sigmoid(gates[..., A_HEADS:]).transpose(0, 2, 1)
    ht = mlstm_chunkwise(heads(qk[..., :A_QK], A_DK), heads(qk[..., A_QK:], A_DK), heads(v, A_DV), li, lf)
    ht = rmsnorm(ht.transpose(0, 2, 1, 3), g_head.reshape(A_HEADS, A_DV)).reshape(Bn, S, A_INNER)
    y = jax.nn.sigmoid(o.astype(F32)) * ht * jax.nn.silu(z.astype(F32))
    return y.astype(h.dtype) @ w_out

def chunk_band_attention(q, k, v, rel_table):
    Bn, S, H, Dh = q.shape
    NC = S // CHUNK
    pad = LEFT_CHUNKS * CHUNK
    q = q.astype(F32)
    kp = jnp.pad(k.astype(F32), ((0, 0), (pad, 0), (0, 0), (0, 0)))
    vp = jnp.pad(v.astype(F32), ((0, 0), (pad, 0), (0, 0), (0, 0)))
    qc = jnp.moveaxis(q.reshape(Bn, NC, CHUNK, H, Dh), 1, 0)
    r = jnp.arange(CHUNK)[:, None]
    idx = jnp.arange(BAND)[None, :]
    bucket = jnp.clip(pad + r - idx, -MAX_REL, MAX_REL) + MAX_REL
    bias = rel_table.astype(F32)[:, bucket]
    key_off = jnp.arange(BAND) - pad
    scale = Dh ** -0.5

    def one_chunk(args):
        ci, qi = args
        start = ci * CHUNK
        kb = lax.dynamic_slice_in_dim(kp, start, BAND, axis=1)
        vb = lax.dynamic_slice_in_dim(vp, start, BAND, axis=1)
        s = jnp.einsum('blhd,bkhd->bhlk', qi, kb) * scale + bias
        s = jnp.where((start + key_off) >= 0, s, -jnp.inf)
        p = jax.nn.softmax(s, axis=-1)
        return jnp.einsum('bhlk,bkhd->blhd', p, vb)

    out = lax.map(one_chunk, (jnp.arange(NC), qc))
    return jnp.moveaxis(out, 0, 1).reshape(Bn, S, H, Dh)

def band_attention_mixer(h, k, v, w_in, rel_table, w_out):
    Bn, S, _ = h.shape
    qz = h @ w_in
    q = qz[..., :B_WIDTH].reshape(Bn, S, B_HEADS, B_DH)
    z = qz[..., B_WIDTH:]
    o = chunk_band_attention(q, k, v, rel_table)
    y = o.reshape(Bn, S, B_WIDTH) * jax.nn.silu(z.astype(F32))
    return y.astype(h.dtype) @ w_out

def second_inputs(seed: int = 0) -> dict:
    key = jax.random.key(seed)
    ks = jax.random.split(key, 24)

    def nrm(k, shape, fan):
        return jax.random.normal(k, shape, F32) * (fan ** -0.5)

    def small(k, shape, s):
        return jax.random.normal(k, shape, F32) * s

    x = jax.random.normal(ks[0], (BATCH, SEQ, D_MODEL), F32)
    c = jax.random.normal(ks[1], (BATCH, D_MODEL), F32)
    ada_w = 0.5 * nrm(ks[2], (DEPTH_2, D_MODEL, 3 * D_MODEL), D_MODEL)
    ada_b = small(ks[3], (DEPTH_2, 3 * D_MODEL), 0.02)
    g_pre = 1.0 + small(ks[4], (DEPTH_2, D_MODEL), 0.05)
    g_post = 1.0 + small(ks[5], (DEPTH_2, D_MODEL), 0.05)
    a_w_in = nrm(ks[6], (N_A_LAYERS, D_MODEL, A_COLS), D_MODEL)
    a_conv_w = nrm(ks[7], (N_A_LAYERS, CONV_W, 2 * A_QK), CONV_W)
    a_conv_b = small(ks[8], (N_A_LAYERS, 2 * A_QK), 0.02)
    i_bias = small(ks[9], (N_A_LAYERS, A_HEADS), 0.1)
    f_bias = jnp.linspace(3.0, 6.0, A_HEADS, dtype=F32)[None, :] + small(ks[10], (N_A_LAYERS, A_HEADS), 0.1)
    a_gate_b = jnp.concatenate([i_bias, f_bias], axis=-1)
    a_g_head = 1.0 + small(ks[11], (N_A_LAYERS, A_INNER), 0.05)
    a_w_out = nrm(ks[12], (N_A_LAYERS, A_INNER, D_MODEL), A_INNER)
    kv_ada_w = 0.5 * nrm(ks[13], (D_MODEL, 2 * D_MODEL), D_MODEL)
    kv_ada_b = small(ks[14], (2 * D_MODEL,), 0.02)
    kv_g = 1.0 + small(ks[15], (D_MODEL,), 0.05)
    kv_w = nrm(ks[16], (D_MODEL, 2 * B_WIDTH), D_MODEL)
    b_w_in = nrm(ks[17], (N_B_LAYERS, D_MODEL, 2 * B_WIDTH), D_MODEL)
    b_rel = small(ks[18], (N_B_LAYERS, B_HEADS, 2 * MAX_REL + 1), 0.5)
    b_w_out = nrm(ks[19], (N_B_LAYERS, B_WIDTH, D_MODEL), B_WIDTH)
    return {"x": x, "c": c, "ada_w": ada_w, "ada_b": ada_b, "g_pre": g_pre, "g_post": g_post,
            "a_w_in": a_w_in, "a_conv_w": a_conv_w, "a_conv_b": a_conv_b, "a_gate_b": a_gate_b,
            "a_g_head": a_g_head, "a_w_out": a_w_out, "kv_ada_w": kv_ada_w, "kv_ada_b": kv_ada_b,
            "kv_g": kv_g, "kv_w": kv_w, "b_w_in": b_w_in, "b_rel": b_rel, "b_w_out": b_w_out}

def second_block(x, c, ada_w, ada_b, g_pre, g_post, a_w_in, a_conv_w, a_conv_b, a_gate_b, a_g_head,
              a_w_out, kv_ada_w, kv_ada_b, kv_g, kv_w, b_w_in, b_rel, b_w_out):
    Bn, S, _ = x.shape
    sc = jax.nn.silu(c.astype(F32))
    k_sh = None
    v_sh = None
    for l in range(DEPTH_2):
        mod = sc @ ada_w[l].astype(F32) + ada_b[l].astype(F32)
        shift, scale, gate = mod[:, :D_MODEL], mod[:, D_MODEL:2 * D_MODEL], mod[:, 2 * D_MODEL:]
        h = modulate(rmsnorm(x, g_pre[l]), shift, scale).astype(x.dtype)
        if l < N_A_LAYERS:
            y = mlstm_mixer(h, a_w_in[l], a_conv_w[l], a_conv_b[l], a_gate_b[l], a_g_head[l], a_w_out[l])
        else:
            if l == N_A_LAYERS:
                kmod = sc @ kv_ada_w.astype(F32) + kv_ada_b.astype(F32)
                hkv = modulate(rmsnorm(x, kv_g), kmod[:, :D_MODEL], kmod[:, D_MODEL:]).astype(x.dtype)
                kv = hkv @ kv_w
                k_sh = kv[..., :B_WIDTH].reshape(Bn, S, B_HEADS, B_DH)
                v_sh = kv[..., B_WIDTH:].reshape(Bn, S, B_HEADS, B_DH)
            j = l - N_A_LAYERS
            y = band_attention_mixer(h, k_sh, v_sh, b_w_in[j], b_rel[j], b_w_out[j])
        x = (x.astype(F32) + gate[:, None, :] * rmsnorm(y, g_post[l])).astype(x.dtype)
    return x


def setup_inputs(seed=0):
    out = dict(first_inputs(seed))
    for name, value in second_inputs(seed + 1).items():
        if name != "x":
            out[name + "_2"] = value
    return out


def reference(
    x, meta_tokens, norm_mix, w_in, norm_q, w_q_up, norm_kv, w_kv_up, w_attn_proj,
    ssm_lambda_re, ssm_lambda_im, ssm_log_step, ssm_b_re, ssm_b_im, ssm_c_re, ssm_c_im, ssm_d,
    w_glu_val, w_glu_gate, w_out, norm_ffn, w_ffn_gate, w_ffn_up, w_ffn_down, norm_final, c_2,
    ada_w_2, ada_b_2, g_pre_2, g_post_2, a_w_in_2, a_conv_w_2, a_conv_b_2, a_gate_b_2,
    a_g_head_2, a_w_out_2, kv_ada_w_2, kv_ada_b_2, kv_g_2, kv_w_2, b_w_in_2, b_rel_2, b_w_out_2,
):
    x = first_block(
        x, meta_tokens, norm_mix, w_in, norm_q, w_q_up, norm_kv, w_kv_up, w_attn_proj,
        ssm_lambda_re, ssm_lambda_im, ssm_log_step, ssm_b_re, ssm_b_im, ssm_c_re, ssm_c_im,
        ssm_d, w_glu_val, w_glu_gate, w_out, norm_ffn, w_ffn_gate, w_ffn_up, w_ffn_down,
        norm_final,
    )
    return second_block(
        x, c_2, ada_w_2, ada_b_2, g_pre_2, g_post_2, a_w_in_2, a_conv_w_2, a_conv_b_2,
        a_gate_b_2, a_g_head_2, a_w_out_2, kv_ada_w_2, kv_ada_b_2, kv_g_2, kv_w_2, b_w_in_2,
        b_rel_2, b_w_out_2,
    )


_drawn_inputs = setup_inputs


def setup_inputs(seed=0):
    import zlib

    import numpy as np

    out = dict(_drawn_inputs(seed))
    spreads = {}
    factors = {'norm_mix': 8.0,
     'norm_q': 8.0,
     'norm_kv': 8.0,
     'ssm_lambda_re': 64.0,
     'ssm_lambda_im': 3.053,
     'ssm_log_step': 3.114,
     'ssm_b_re': 13.011,
     'ssm_b_im': 13.928,
     'ssm_c_re': 13.099,
     'ssm_c_im': 13.391,
     'norm_ffn': 3.763,
     'norm_final': 2.687,
     'g_post_2': 2.718,
     'a_conv_b_2': 23.653,
     'a_g_head_2': 9.995,
     'kv_ada_b_2': 3.659,
     'kv_g_2': 5.295}
    for name, (base, spread) in spreads.items():
        noise = np.random.default_rng([zlib.crc32(name.encode()), seed]).standard_normal(out[name].shape)
        drawn = base * np.exp(spread * noise) if base else spread * noise
        out[name] = __import__('jax').numpy.asarray(drawn.astype(out[name].dtype))
    for name, factor in factors.items():
        out[name] = (out[name] * factor).astype(out[name].dtype)
    return out
```

```python
from contextlib import ExitStack

import concourse.bass as bass
from concourse import mybir

F32 = mybir.dt.float32
I32 = mybir.dt.int32
ALU = mybir.AluOpType
ACT = mybir.ActivationFunctionType
AX = mybir.AxisListType.X

P = 128
D = 2048
DB = D // P
SEQ = 256
META = 16
LEN = SEQ + META
EPS = 1e-6
NEG = -1e30

SLOTS = 8
KT = 4
COLS = 512
MB = COLS // P

HEADS = 16
LORA = 512
NOPE, ROPE, VH = 128, 64, 128
G, N, C = 64, 64, 16
SSM_W = G * C
OFF_KR = 2 * LORA
OFF_U = OFF_KR + ROPE
OFF_G = OFF_U + SSM_W
FF = 5632

A_INNER, A_QK, A_HEADS, CONV = 4096, 2048, 8, 4
A_DK, A_DV = A_QK // A_HEADS, A_INNER // A_HEADS
A_V0, A_O0, A_Z0, A_G0 = 2 * A_QK, 2 * A_QK + A_INNER, 2 * A_QK + 2 * A_INNER, 2 * A_QK + 3 * A_INNER
CHUNK, MAX_REL = 64, 128

VECTOR_ROWS = {
    "a_conv_w_2": (0, 0, 128),
    "ada_b_2": (1, 0, 96), "kv_ada_b_2": (1, 96, 32),
    "g_pre_2": (2, 0, 32), "g_post_2": (2, 32, 32), "norm_mix": (2, 64, 16), "norm_ffn": (2, 80, 16),
    "norm_final": (2, 96, 16), "kv_g_2": (2, 112, 16),
    "a_conv_b_2": (3, 0, 32), "a_g_head_2": (3, 32, 32), "c_2": (3, 64, 16), "norm_q": (3, 80, 4),
    "norm_kv": (3, 84, 4), "ssm_d": (3, 88, 8),
}
VECTOR_TILE_ROWS = (128, 128, 128, 96)

CONST = {"identity": (0, 128), "cos": (128, LEN), "sin": (128 + LEN, LEN), "causal": (128 + 2 * LEN, LEN),
         "after": (128 + 3 * LEN, SEQ)}
CONST_COLS = 128 + 3 * LEN + SEQ


class Phase:

    def __init__(self, base, iters, upi, source, tail=0):
        assert upi % SLOTS == 0
        self.base, self.iters, self.upi, self.source, self.tail = base, iters, upi, source, tail
        self.end = base + iters * upi + tail

    def slot(self, j):
        return (self.base + j) % SLOTS

    def uses(self, it, j):
        return (self.base + j) // SLOTS + it * (self.upi // SLOTS) + 1


def plan_units(w):
    phases, flat = {}, []

    def block(m, row, col, cols=COLS):
        rows = m[bass.ds(row, KT * P), :] if not isinstance(row, int) else m[row:row + KT * P, :]
        part = rows[:, bass.ds(col, cols)] if not isinstance(col, int) else rows[:, col:col + cols]
        return part.rearrange("(k p) n -> p k n", p=P)

    def add(name, iters, upi, source, tail=0):
        ph = phases[name] = Phase(len(flat), iters, upi, source, tail)
        for n in range(iters * upi + tail):
            flat.append((source, n // upi, n % upi))
        assert len(flat) == ph.end

    def slabs(m, first, k_units, per=2):
        return lambda it, j: block(m, (j % k_units) * KT * P, first + it * per * COLS + (j // k_units) * COLS)

    def pair(m0, c0, m1, c1, k_units, per=1):
        def source(it, j):
            s = j // k_units
            m, c = ((m0, c0), (m1, c1))[s % 2]
            return block(m, (j % k_units) * KT * P, c + it * per * COLS + (s // 2) * COLS)
        return source

    add("latents", 1, 8, slabs(w["w_in"], 0, 4))
    add("u", 1, 8, slabs(w["w_in"], OFF_U, 4))
    add("q_up", 1, 8, lambda it, j: block(w["w_q_up"], 0, j * 2 * (NOPE + ROPE), 2 * (NOPE + ROPE)))
    add("kv_up", 1, 8, lambda it, j: block(w["w_kv_up"], 0, j * COLS))
    add("attn_proj", 2, 8, slabs(w["w_attn_proj"], 0, 4))
    add("glu", 2, 8, pair(w["w_glu_val"], 0, w["w_glu_gate"], 0, 2, 2))
    add("mix_gates", 4, 8, pair(w["w_in"], OFF_G, w["w_in"], OFF_G + D, 4))
    add("w_out", 2, 8, slabs(w["w_out"], 0, 4))
    add("ffn_up", FF // COLS, 8, pair(w["w_ffn_gate"], 0, w["w_ffn_up"], 0, 4))
    add("ffn_down", 5, 8, lambda it, j: block(w["w_ffn_down"], it * 2 * KT * P + (j // 4) * KT * P, (j % 4) * COLS), 4)
    add("ada0", 6, 8, slabs(w["ada_w_0"], 0, 4))
    add("a_qk", 4, 8, slabs(w["a_w_in_2"], 0, 4))
    add("a_v", 4, 8, slabs(w["a_w_in_2"], A_V0, 4))
    add("a_oz", 8, 8, pair(w["a_w_in_2"], A_O0, w["a_w_in_2"], A_Z0, 4))
    add("a_out", 2, 16, slabs(w["a_w_out_2"], 0, 8))
    add("ada1", 6, 8, slabs(w["ada_w_1"], 0, 4))
    add("kv_ada", 4, 8, slabs(w["kv_ada_w_2"], 0, 4))
    add("b_k", 2, 8, slabs(w["kv_w_2"], 0, 4))
    add("b_v", 2, 8, slabs(w["kv_w_2"], D, 4))
    add("b_q", 2, 8, slabs(w["b_w_in_2"], 0, 4))
    add("b_z", 2, 8, slabs(w["b_w_in_2"], D, 4))
    add("b_out", 2, 8, slabs(w["b_w_out_2"], 0, 4))
    return phases, flat


class Step:

    def __init__(self, sem):
        self.sem, self.value = sem, 0

    def tick(self, instruction):
        self.value += 1
        instruction.then_inc(self.sem, 1)
        return self.value


def build(nc, w, out):
    with ExitStack() as ctx:
        names = [0]

        def sem(name):
            return ctx.enter_context(nc.semaphore(name))

        def sbuf(stack, name, shape, dtype=F32):
            names[0] += 1
            return stack.enter_context(nc.sbuf_tensor(f"{name}_{names[0]}", shape, dtype))

        phases, flat = plan_units(w)

        ring = sbuf(ctx, "ring", [P, SLOTS, KT, COLS])
        hT = sbuf(ctx, "hT", [P, DB, LEN])
        xT = hT[:, :, META:LEN]
        cols = sbuf(ctx, "cols", [P, 4 * P])
        const = sbuf(ctx, "const", [P, CONST_COLS])
        ones = sbuf(ctx, "ones", [P, P])
        eps = sbuf(ctx, "eps", [P, 1])
        rms = sbuf(ctx, "rms", [P, LEN])
        PS = ctx.enter_context(nc.psum_tensor("PS", [P, 8, 512], F32))

        unit_loaded = [sem(f"unit_loaded{i}") for i in range(SLOTS)]
        slot_read = [sem(f"slot_read{i}") for i in range(SLOTS)]
        banks_free = [sem(f"banks_free{i}") for i in range(2)]
        freed = [0, 0]
        half_done = sem("half_done")
        halves = [0]
        vec = Step(sem("vector_step"))
        act = Step(sem("scalar_step"))
        ten = Step(sem("tensor_step"))
        pool = Step(sem("pool_step"))
        small_loaded = sem("small_loaded")
        small = [0]
        stored = sem("stored")

        def const_of(name):
            first, n = CONST[name]
            return const[:, first:first + n]

        ident, cosT, sinT = const_of("identity"), const_of("cos"), const_of("sin")
        causal, after = const_of("causal"), const_of("after")

        def col(name, i, n=1):
            tile, row, rows = VECTOR_ROWS[name]
            assert i + n <= rows
            return cols[:, tile * P + row + i:tile * P + row + i + n]

        def load_small(eng, dst, src):
            small[0] += 16
            eng.dma_start(dst, src).then_inc(small_loaded, 16)

        def load_unit(sp, n):
            source, it, j = flat[n]
            if n >= SLOTS:
                sp.wait_ge(slot_read[n % SLOTS], n // SLOTS)
            src = source(it, j)
            sp.dma_start(ring[:, n % SLOTS, :, 0:src.shape[2]], src).then_inc(unit_loaded[n % SLOTS], 16)

        def stream(sp, ph):
            for n in range(ph.base + SLOTS, ph.base + ph.upi):
                load_unit(sp, n)
            if ph.iters > 1:
                with sp.Fori(1, ph.iters) as it:
                    for j in range(ph.upi):
                        s = ph.slot(j)
                        sp.wait_ge(slot_read[s], ph.uses(it, j) - 1)
                        sp.dma_start(ring[:, s], ph.source(it, j)).then_inc(unit_loaded[s], 16)
            for n in range(max(ph.base + ph.upi * ph.iters, ph.base + SLOTS), min(ph.end + SLOTS, len(flat))):
                load_unit(sp, n)

        def multiply(pe, ph, it, k_units, moving, free_per_slab, slabs):
            for s in range(slabs):
                half = s % 2
                need = freed[half] + free_per_slab * (it * (slabs // 2) + s // 2)
                if not isinstance(it, int) or need > 0:
                    pe.wait_ge(banks_free[half], need)
                for ku in range(k_units):
                    j = s * k_units + ku
                    slot = ph.slot(j)
                    pe.wait_ge(unit_loaded[slot], 16 * ph.uses(it, j))
                    for kt in range(KT):
                        rhs = moving(ku * KT + kt)
                        for m in range(MB):
                            mm = nc.tensor.matmul(
                                PS[:, 4 * half + m, 0:rhs.shape[1]], ring[:, slot, kt, m * P:(m + 1) * P], rhs,
                                start=(ku == 0 and kt == 0), stop=(ku == k_units - 1 and kt == KT - 1))
                    mm.then_inc(slot_read[slot], 1)

        def wait_slab(eng, ph, it, s, k_units):
            j = (s + 1) * k_units - 1
            eng.wait_ge(slot_read[ph.slot(j)], ph.uses(it, j))

        def rounds(eng, ph, body):
            if ph.iters == 1:
                body(0)
            else:
                with eng.Fori(0, ph.iters) as it:
                    body(it)

        def project(name, k_units, moving, width, on_vector, slabs=2):
            ph = phases[name]
            with nc.Block() as block:
                @block.sync
                def _(sp):
                    stream(sp, ph)

                @block.tensor
                def _(pe):
                    rounds(pe, ph, lambda it: multiply(pe, ph, it, k_units, moving, 1, slabs))

                @block.vector
                def _(dve):
                    def body(it):
                        for s in range(slabs):
                            wait_slab(dve, ph, it, s, k_units)
                            half = s % 2
                            on_vector(it, s, PS[:, 4 * half:4 * half + 4, 0:width]).then_inc(banks_free[half], 1)
                    rounds(dve, ph, body)
            for half in range(2):
                freed[half] += ph.iters * slabs // 2

        def project_pair(name, k_units, moving, gate_half, on_vector, slabs=2, both=False):
            ph = phases[name]
            pairs = slabs // 2
            gates_ready, gates_used = sem(f"{name}_gates_ready"), sem(f"{name}_gates_used")
            with ExitStack() as scope:
                gates = sbuf(scope, "gates", [P, 2, MB, SEQ])
                with nc.Block() as block:
                    @block.sync
                    def _(sp):
                        stream(sp, ph)

                    @block.tensor
                    def _(pe):
                        rounds(pe, ph, lambda it: multiply(pe, ph, it, k_units, moving, 1, slabs))

                    @block.scalar
                    def _(a):
                        a.sem_inc(gates_used, 1)
                        def body(it):
                            for q in range(pairs):
                                wait_slab(a, ph, it, 2 * q + 1, k_units)
                                a.wait_ge(gates_used, it * pairs + q + 1)
                                for g in ((0, 1) if both else (gate_half,)):
                                    last = nc.scalar.activation(gates[:, g], PS[:, 4 * g:4 * g + 4, 0:SEQ], ACT.Sigmoid)
                                last.then_inc(gates_ready, 1)
                        rounds(a, ph, body)

                    @block.vector
                    def _(dve):
                        def body(it):
                            for q in range(pairs):
                                dve.wait_ge(gates_ready, it * pairs + q + 1)
                                on_vector(dve, it, q, PS[:, 0:4, 0:SEQ], PS[:, 4:8, 0:SEQ], gates, gates_used)
                        rounds(dve, ph, body)
            for half in range(2):
                freed[half] += ph.iters * pairs

        def inverse_rms(src, blocks, width, squares):
            with nc.Block() as block:
                squared, summed = act.value + 2, ten.value + 1
                half = (blocks + 1) // 2

                @block.scalar
                def _(a):
                    for k0 in (0, half):
                        act.tick(nc.scalar.activation(squares[:, k0:k0 + half, 0:width], src[:, k0:k0 + half], ACT.Square))
                    a.wait_ge(ten.sem, summed)
                    act.tick(nc.scalar.activation(rms[:, 0:width], PS[:, 0, 0:width], ACT.Sqrt,
                                                  scale=1.0 / (blocks * P), bias=eps[:, 0:1]))

                @block.tensor
                def _(pe):
                    for k in range(blocks):
                        pe.wait_ge(act.sem, squared - 1 if k < half else squared)
                        mm = nc.tensor.matmul(PS[:, 0, 0:width], ones[:], squares[:, k, 0:width],
                                              start=(k == 0), stop=(k == blocks - 1))
                    ten.tick(mm)

                @block.vector
                def _(dve):
                    dve.wait_ge(act.sem, squared + 1)
                    vec.tick(nc.vector.reciprocal(rms[:, 0:width], rms[:, 0:width]))

        def scale_tokens(dst, src, blocks, width, gain, shift=None):
            with nc.Block() as block:
                base = vec.value

                @block.vector
                def _(dve):
                    for k in range(blocks):
                        vec.tick(nc.vector.scalar_tensor_tensor(dst[:, k], src[:, k], gain[:, k:k + 1], rms[:, 0:width],
                                                                ALU.mult, ALU.mult))

                @block.scalar
                def _(a):
                    if shift is not None:
                        for k in range(blocks):
                            a.wait_ge(vec.sem, base + k + 1)
                            act.tick(nc.scalar.activation(dst[:, k], dst[:, k], ACT.Identity, bias=shift[:, k:k + 1]))

        def small_ops(ops):
            with nc.Block() as block:
                @block.vector
                def _(dve):
                    for op in ops:
                        dve.wait_ge(vec.sem, vec.tick(op()))

        def attention(name, heads, scores_of, keys_of, bias_of, scale, v, o):
            items = 2 * heads
            scored, turned, valued = (sem(f"{name}_{x}") for x in ("scored", "turned", "valued"))
            biased, shifted, exped, normed = (sem(f"{name}_{x}") for x in ("biased", "shifted", "exped", "normed"))
            copied, kept, dve_step = (sem(f"{name}_{x}") for x in ("copied", "kept", "maxed"))
            with ExitStack() as scope:
                S = sbuf(scope, "S", [P, 2, LEN])
                Pr = sbuf(scope, "Pr", [P, 2, LEN])
                PT = sbuf(scope, "PT", [P, 2, 3, P])
                mx = sbuf(scope, "mx", [P, 2, 4])
                with nc.Block() as block:
                    @block.tensor
                    def _(pe):
                        for n in range(items + 2):
                            if n < items:
                                if n >= 3:
                                    pe.wait_ge(biased, n - 2)
                                pairs = scores_of(n)
                                for i, (lhsT, rhs) in enumerate(pairs):
                                    mm = nc.tensor.matmul(PS[:, n % 3, 0:keys_of(n)], lhsT, rhs,
                                                          start=(i == 0), stop=(i == len(pairs) - 1))
                                mm.then_inc(scored, 1)
                            t = n - 1
                            if 0 <= t < items:
                                pe.wait_ge(normed, t + 1)
                                if t >= 2:
                                    pe.wait_ge(copied, t - 1)
                                for k0 in range(0, keys_of(t), P):
                                    kn = min(P, keys_of(t) - k0)
                                    mm = nc.tensor.transpose(PS[0:kn, 3 + t % 2, k0:k0 + P], Pr[:, t % 2, k0:k0 + kn], ident)
                                mm.then_inc(turned, 1)
                            r = n - 2
                            if 0 <= r < items:
                                pe.wait_ge(copied, r + 1)
                                if r >= 2:
                                    pe.wait_ge(kept, r - 1)
                                kts = -(-keys_of(r) // P)
                                for kt in range(kts):
                                    kn = min(P, keys_of(r) - kt * P)
                                    mm = nc.tensor.matmul(PS[:, 5 + r % 2, 0:P], v[0:kn, kt, (r // 2) * P:(r // 2 + 1) * P],
                                                          PT[0:kn, r % 2, kt], start=(kt == 0), stop=(kt == kts - 1))
                                mm.then_inc(valued, 1)

                    @block.vector
                    def _(dve):
                        chain = 0
                        for n in range(items + 2):
                            if n < items:
                                nk, b = keys_of(n), n % 2
                                dve.wait_ge(scored, n + 1)
                                if n >= 2:
                                    dve.wait_ge(exped, n - 1)
                                nc.vector.scalar_tensor_tensor(S[:, b, 0:nk], PS[:, n % 3, 0:nk], scale, bias_of(n),
                                                               ALU.mult, ALU.add).then_inc(biased, 1)
                                dve.wait_ge(biased, n + 1)
                                nc.vector.reduce_max(mx[:, b, 0:1], S[:, b, 0:nk], AX).then_inc(dve_step, 1)
                                chain += 1
                                dve.wait_ge(dve_step, chain)
                                nc.vector.tensor_scalar(mx[:, b, 1:2], mx[:, b, 0:1], -1.0, None, ALU.mult).then_inc(shifted, 1)
                            t = n - 1
                            if 0 <= t < items:
                                nk, b = keys_of(t), t % 2
                                dve.wait_ge(exped, t + 1)
                                nc.vector.reciprocal(mx[:, b, 3:4], mx[:, b, 2:3]).then_inc(dve_step, 1)
                                chain += 1
                                dve.wait_ge(dve_step, chain)
                                nc.vector.tensor_scalar(Pr[:, b, 0:nk], Pr[:, b, 0:nk], mx[:, b, 3:4], None,
                                                        ALU.mult).then_inc(normed, 1)
                            r = n - 2
                            if 0 <= r < items:
                                dve.wait_ge(valued, r + 1)
                                nc.vector.tensor_copy(o[:, r // 2, (r % 2) * P:(r % 2 + 1) * P],
                                                      PS[:, 5 + r % 2, 0:P]).then_inc(kept, 1)

                    @block.scalar
                    def _(a):
                        for n in range(items + 1):
                            if n < items:
                                nk, b = keys_of(n), n % 2
                                a.wait_ge(shifted, n + 1)
                                if n >= 2:
                                    a.wait_ge(turned, n - 1)
                                nc.scalar.activation(Pr[:, b, 0:nk], S[:, b, 0:nk], ACT.Exp, bias=mx[:, b, 1:2],
                                                     accum_out=mx[:, b, 2:3]).then_inc(exped, 1)
                            t = n - 1
                            if 0 <= t < items:
                                a.wait_ge(turned, t + 1)
                                if t >= 2:
                                    a.wait_ge(valued, t - 1)
                                nk, b = keys_of(t), t % 2
                                full, rest = nk // P, nk % P
                                last = nc.scalar.copy(PT[:, b, 0:full], PS[:, 3 + b, 0:full * P].rearrange("p (k q) -> p k q", q=P))
                                if rest:
                                    last = nc.scalar.copy(PT[0:rest, b, full], PS[0:rest, 3 + b, full * P:(full + 1) * P])
                                last.then_inc(copied, 1)

        with ExitStack() as scope:
            x_rows = sbuf(scope, "x_rows", [P, 2, D])
            meta_rows = sbuf(scope, "meta_rows", [META, D])
            vec_rows = sbuf(scope, "vec_rows", [P, 4, P])
            with nc.Block() as block:
                turned, copied = sem("input_turned"), sem("input_copied")

                @block.sync
                def _(sp):
                    load_small(sp, const[:], w["shape_constants"])
                    for name, (tile, row, rows) in VECTOR_ROWS.items():
                        load_small(sp, vec_rows[row:row + rows, tile], w[name + "_rows"])
                    load_small(sp, x_rows[:], w["x"].rearrange("(t p) d -> p t d", p=P))
                    load_small(sp, meta_rows[:], w["meta_tokens"])
                    for n in range(SLOTS):
                        load_unit(sp, n)

                @block.gpsimd
                def _(g):
                    nc.gpsimd.memset(ones[:], 1.0)
                    nc.gpsimd.memset(eps[:], EPS)

                groups = [("vector", None)] + [("x", i) for i in range(8)] + [("meta", None)]
                places = [cols[:, 0:3 * P].rearrange("p (a b) -> p a b", b=P)]
                n_small = 16 * (3 + len(VECTOR_ROWS))

                @block.tensor
                def _(pe):
                    pe.wait_ge(small_loaded, n_small)
                    for n, (kind, i) in enumerate(groups):
                        if n >= 4:
                            pe.wait_ge(copied, n - 3)
                        if kind == "vector":
                            for t in range(4):
                                r = VECTOR_TILE_ROWS[t]
                                mm = nc.tensor.transpose(PS[:, 0, t * P:t * P + r], vec_rows[0:r, t], ident[0:r, 0:r])
                        elif kind == "x":
                            for q in range(4):
                                k = (i % 4) * 4 + q
                                mm = nc.tensor.transpose(PS[:, n % 4, q * P:(q + 1) * P],
                                                         x_rows[:, i // 4, k * P:(k + 1) * P], ident)
                        else:
                            for k in range(DB):
                                mm = nc.tensor.transpose(PS[:, n % 4, k * META:(k + 1) * META],
                                                         meta_rows[:, k * P:(k + 1) * P], ident[0:META, 0:META])
                        mm.then_inc(turned, 1)

                @block.vector
                def _(dve):
                    for n, (kind, i) in enumerate(groups):
                        dve.wait_ge(turned, n + 1)
                        if kind == "vector":
                            nc.vector.tensor_copy(cols[:, 0:480], PS[:, 0, 0:480]).then_inc(copied, 1)
                        elif kind == "x":
                            nc.vector.tensor_copy(
                                hT[:, (i % 4) * 4:(i % 4) * 4 + 4, META + (i // 4) * P:META + (i // 4 + 1) * P],
                                PS[:, n % 4, :].rearrange("p (k t) -> p k t", k=4)).then_inc(copied, 1)
                        else:
                            nc.vector.tensor_copy(hT[:, :, 0:META],
                                                  PS[:, n % 4, 0:DB * META].rearrange("p (k t) -> p k t", k=DB)).then_inc(copied, 1)

        with ExitStack() as one:
            nT = sbuf(one, "nT", [P, DB, LEN])
            kT = sbuf(one, "kT", [P, HEADS, LEN])
            attn_out = kT[:, :, 0:SEQ]
            uT = sbuf(one, "uT", [P, SSM_W // P, LEN])
            inverse_rms(hT, DB, LEN, nT)
            scale_tokens(nT, hT, DB, LEN, col("norm_mix", 0, DB))

            with ExitStack() as scope:
                latent = sbuf(scope, "latent", [P, 8, LEN])
                k_rope = sbuf(scope, "k_rope", [P, LEN])
                qT = sbuf(scope, "qT", [P, HEADS, SEQ])
                q_rope = sbuf(scope, "q_rope", [P, HEADS // 2, SEQ])
                swapped = sbuf(scope, "swapped", [P, 2, LEN])

                project("latents", 4, lambda k: nT[:, k, :], LEN,
                        lambda it, s, ps: nc.vector.tensor_copy(latent[:, 4 * s:4 * s + 4], ps))
                project("u", 4, lambda k: nT[:, k, :], LEN,
                        lambda it, s, ps: nc.vector.tensor_copy(uT[:, 4 * s:4 * s + 4], ps))

                def rotate(dve, dst, ps, first, width):
                    for q, r in ((0, 1), (1, 0), (2, 3), (3, 2)):
                        last = nc.vector.tensor_copy(swapped[32 * q:32 * q + 32, 0, 0:width], ps[32 * r:32 * r + 32])
                        vec.tick(last)
                    dve.wait_ge(vec.sem, vec.value)
                    vec.tick(nc.vector.tensor_tensor(swapped[:, 0, 0:width], swapped[:, 0, 0:width],
                                                     sinT[:, first:first + width], ALU.mult))
                    last = nc.vector.tensor_tensor(swapped[:, 1, 0:width], ps, cosT[:, first:first + width], ALU.mult)
                    dve.wait_ge(vec.sem, vec.tick(last))
                    last = nc.vector.tensor_tensor(dst, swapped[:, 0, 0:width], swapped[:, 1, 0:width], ALU.add)
                    dve.wait_ge(vec.sem, vec.tick(last))

                with ExitStack() as kr, nc.Block() as block:
                    w_kr = sbuf(kr, "w_kr", [P, DB, 2, ROPE])
                    kr_done = ten.value + 1
                    kr_loaded = small[0] + 32

                    @block.sync
                    def _(sp):
                        for half in range(2):
                            load_small(sp, w_kr[:, :, half], w["w_in"][:, OFF_KR:OFF_U].rearrange("(k p) n -> p k n", p=P))

                    @block.tensor
                    def _(pe):
                        pe.wait_ge(small_loaded, kr_loaded)
                        for k in range(DB):
                            mm = nc.tensor.matmul(PS[:, 0, 0:LEN], w_kr[:, k].rearrange("p a b -> p (a b)"), nT[:, k],
                                                  start=(k == 0), stop=(k == DB - 1))
                        ten.tick(mm)

                    @block.vector
                    def _(dve):
                        dve.wait_ge(ten.sem, kr_done)
                        rotate(dve, k_rope[:], PS[:, 0, 0:LEN], 0, LEN)

                for part, gain in ((latent[:, 0:4], "norm_q"), (latent[:, 4:8], "norm_kv")):
                    inverse_rms(part, 4, LEN, kT)
                    scale_tokens(part, part, 4, LEN, col(gain, 0, 4))

                ph = phases["q_up"]
                with nc.Block() as block:
                    q_free, q_rope_free = sem("q_free"), sem("q_rope_free")

                    @block.sync
                    def _(sp):
                        stream(sp, ph)

                    @block.tensor
                    def _(pe):
                        for j in range(8):
                            slot, half = ph.slot(j), j % 2
                            if j >= 2:
                                pe.wait_ge(q_free, j - 1)
                                pe.wait_ge(q_rope_free, j - 1)
                            pe.wait_ge(unit_loaded[slot], 16 * ph.uses(0, j))
                            for m in range(3):
                                for kt in range(KT):
                                    mm = nc.tensor.matmul(PS[:, 4 * half + m, 0:SEQ], ring[:, slot, kt, m * P:(m + 1) * P],
                                                          latent[:, kt, META:LEN],
                                                          start=(kt == 0), stop=(kt == KT - 1))
                            mm.then_inc(slot_read[slot], 1)

                    @block.scalar
                    def _(a):
                        for j in range(8):
                            half = j % 2
                            a.wait_ge(slot_read[ph.slot(j)], ph.uses(0, j))
                            nc.scalar.copy(qT[:, 2 * j:2 * j + 2], PS[:, 4 * half:4 * half + 2, 0:SEQ]).then_inc(q_free, 1)

                    @block.vector
                    def _(dve):
                        for j in range(8):
                            half = j % 2
                            dve.wait_ge(slot_read[ph.slot(j)], ph.uses(0, j))
                            rotate(dve, q_rope[:, j], PS[:, 4 * half + 2, 0:SEQ], META, SEQ)
                            dve.sem_inc(q_rope_free, 1)

                v = sbuf(scope, "v", [P, 3, D])
                ph_kv = phases["kv_up"]
                with nc.Block() as block:
                    k_free, v_free = sem("k_free"), sem("v_free")
                    token_tiles = ((0, P), (P, P), (2 * P, META))

                    @block.sync
                    def _(sp):
                        stream(sp, ph_kv)

                    @block.tensor
                    def _(pe):
                        for j in range(8):
                            slot, half = ph_kv.slot(j), j % 2
                            if j >= 2:
                                pe.wait_ge(k_free, j - 1)
                                pe.wait_ge(v_free, j - 1)
                            pe.wait_ge(unit_loaded[slot], 16 * ph_kv.uses(0, j))
                            pairs = ring[:, slot].rearrange("p k (h c) -> p k h c", h=2)
                            for m in range(2):
                                for kt in range(KT):
                                    nc.tensor.matmul(PS[:, 4 * half + m, 0:LEN], pairs[:, kt, m, 0:NOPE], latent[:, 4 + kt],
                                                     start=(kt == 0), stop=(kt == KT - 1))
                            for t, (t0, tn) in enumerate(token_tiles):
                                dst = PS[0:tn, 4 * half + 2 + t // 2, (t % 2) * 256:(t % 2) * 256 + 256]
                                for kt in range(KT):
                                    mm = nc.tensor.matmul(dst, latent[:, 4 + kt, t0:t0 + tn], pairs[:, kt, :, NOPE:],
                                                          start=(kt == 0), stop=(kt == KT - 1))
                            mm.then_inc(slot_read[slot], 1)

                    @block.scalar
                    def _(a):
                        for j in range(8):
                            half = j % 2
                            a.wait_ge(slot_read[ph_kv.slot(j)], ph_kv.uses(0, j))
                            nc.scalar.copy(kT[:, 2 * j:2 * j + 2], PS[:, 4 * half:4 * half + 2, 0:LEN]).then_inc(k_free, 1)

                    @block.vector
                    def _(dve):
                        for j in range(8):
                            half = j % 2
                            dve.wait_ge(slot_read[ph_kv.slot(j)], ph_kv.uses(0, j))
                            nc.vector.tensor_copy(v[0:META, 2, j * 256:(j + 1) * 256], PS[0:META, 4 * half + 3, 0:256])
                            nc.vector.tensor_copy(v[:, 0:2, j * 256:(j + 1) * 256],
                                                  PS[:, 4 * half + 2, :].rearrange("p (t c) -> p t c", t=2)).then_inc(v_free, 1)

                def mla_keys(n):
                    return META + P * (n % 2 + 1)

                def mla_scores(n):
                    h, b = n // 2, n % 2
                    r = 64 * (h % 2)
                    nk = mla_keys(n)
                    return [(qT[:, h, b * P:(b + 1) * P], kT[:, h, 0:nk]),
                            (q_rope[r:r + 64, h // 2, b * P:(b + 1) * P], k_rope[r:r + 64, 0:nk])]

                attention("mla", HEADS, mla_scores, mla_keys, lambda n: causal[:, LEN - mla_keys(n):LEN],
                          (NOPE + ROPE) ** -0.5, v, qT)
                project("attn_proj", 4, lambda k: qT[:, k, :], SEQ,
                        lambda it, s, ps: nc.vector.tensor_copy(attn_out[:, bass.ds(it * 8 + 4 * s, 4)], ps))

            TILES = G // 2
            UB = SSM_W // P
            with ExitStack() as scope:
                y = uT[:, :, META:LEN]
                BT = sbuf(scope, "BT", [P, UB, 2, P])
                CT = sbuf(scope, "CT", [P, UB, 2, P])
                mag = sbuf(scope, "mag", [P, TILES])
                powers = sbuf(scope, "powers", [P, 2, 9, TILES])
                with ExitStack() as prep:
                    row = sbuf(prep, "row", [TILES, 16, P])
                    steps = sbuf(prep, "steps", [TILES, 2])
                    turns = sbuf(prep, "turns", [TILES, P], I32)
                    b_in = sbuf(prep, "b_in", [P, 2, TILES, C])
                    c_in = sbuf(prep, "c_in", [P, 2, UB, P])
                    coef = sbuf(prep, "coef", [P, 2, TILES])
                    prod = sbuf(prep, "prod", [P, 4, TILES, C])
                    b_pad = sbuf(prep, "b_pad", [P, 2, TILES, 2 * C])
                    LR, LI, ST, ANG, MAG, SIN, COS, NR, T0, T1, DEN, CR, CI, HALF = range(14)
                    halfpi = 1.5707963267948966
                    two_pi_hi, two_pi_lo = 6.28125, 0.0019353071795864769
                    with nc.Block() as block:
                        base = small[0]
                        c_loaded = sem("ssm_c_loaded")
                        zeroed = pool.value + 2

                        @block.gpsimd
                        def _(g):
                            pool.tick(nc.gpsimd.memset(c_in[:], 0.0))
                            pool.tick(nc.gpsimd.memset(b_pad[:], 0.0))

                        @block.sync
                        def _(sp):
                            load_small(sp, row[:, LR], w["ssm_lambda_re"].rearrange("(r c) n -> r (c n)", c=2))
                            load_small(sp, row[:, LI], w["ssm_lambda_im"].rearrange("(r c) n -> r (c n)", c=2))
                            load_small(sp, steps[:], w["ssm_log_step"].rearrange("(r c) -> r c", c=2))
                            for i, name in enumerate(("ssm_b_re", "ssm_b_im")):
                                load_small(sp, b_in[:, i], w[name].rearrange("(t c) n p -> (c n) t p", c=2))
                            sp.wait_ge(pool.sem, zeroed)
                            for i, name in enumerate(("ssm_c_re", "ssm_c_im")):
                                src = w[name].rearrange("(j g) p n -> g p j n", g=8)
                                for g8 in range(8):
                                    sp.dma_start(c_in[16 * g8:16 * g8 + 16, i, :, 64 * (g8 % 2):64 * (g8 % 2) + 64],
                                                 src[g8]).then_inc(c_loaded, 16)
                        in_loaded = base + 16 * 5
                        stepped, phased, ready = sem("ssm_stepped"), sem("ssm_phased"), sem("ssm_ready")
                        turned, copied, padded = sem("ssm_turned"), sem("ssm_copied"), sem("ssm_padded")

                        @block.scalar
                        def _(a):
                            a.wait_ge(small_loaded, in_loaded)
                            nc.scalar.activation(steps[:], steps[:], ACT.Exp).then_inc(stepped, 1)
                            a.wait_ge(phased, 1)
                            act.tick(nc.scalar.activation(row[:, MAG], row[:, T0], ACT.Exp))
                            act.tick(nc.scalar.activation(row[:, SIN], row[:, ANG], ACT.Sin))
                            nc.scalar.activation(row[:, HALF], row[:, ANG], ACT.Sin, scale=0.5).then_inc(stepped, 1)
                            for n in range(8):
                                a.wait_ge(turned, 2 + n)
                                src = PS[:, 1 + n % 2, :]
                                nc.scalar.copy(BT[:, n], src[:, 0:256].rearrange("p (a b) -> p a b", a=2))
                                nc.scalar.copy(CT[:, n, 0], src[:, 256:384])
                                nc.scalar.mul(CT[:, n, 1], src[:, 384:512], -1.0).then_inc(copied, 1)

                        @block.vector
                        def _(dve):
                            def link(instruction):
                                dve.wait_ge(vec.sem, vec.tick(instruction))

                            def tt(o, i0, i1, op):
                                link(nc.vector.tensor_tensor(o, i0, i1, op))

                            dve.wait_ge(stepped, 1)
                            for c2 in range(2):
                                link(nc.vector.tensor_copy(row[:, ST, c2 * N:(c2 + 1) * N], steps[:, c2:c2 + 1].to_broadcast([TILES, N])))
                            tt(row[:, T0], row[:, LR], row[:, ST], ALU.mult)
                            tt(row[:, ANG], row[:, LI], row[:, ST], ALU.mult)
                            link(nc.vector.tensor_scalar(turns[:], row[:, ANG], 1.0 / 6.283185307179586, None, ALU.mult))
                            link(nc.vector.tensor_copy(row[:, T1], turns[:]))
                            for part in (two_pi_hi, two_pi_lo):
                                link(nc.vector.scalar_tensor_tensor(row[:, ANG], row[:, T1], -part, row[:, ANG], ALU.mult, ALU.add))
                            link(nc.vector.tensor_scalar(row[:, T1], row[:, ANG], 3.1415925, 6.283185307179586, ALU.is_gt, ALU.mult))
                            tt(row[:, ANG], row[:, ANG], row[:, T1], ALU.subtract)
                            link(nc.vector.tensor_scalar(row[:, T1], row[:, ANG], -3.1415925, 6.283185307179586, ALU.is_lt, ALU.mult))
                            tt(row[:, ANG], row[:, ANG], row[:, T1], ALU.add)
                            link(nc.vector.tensor_scalar(row[:, ANG], row[:, ANG], 3.1415925, -3.1415925, ALU.min, ALU.max))
                            dve.sem_inc(phased, 1)
                            dve.wait_ge(stepped, 2)
                            tt(row[:, T1], row[:, HALF], row[:, HALF], ALU.mult)
                            link(nc.vector.tensor_scalar(row[:, COS], row[:, T1], -2.0, 1.0, ALU.mult, ALU.add))
                            tt(row[:, T0], row[:, MAG], row[:, COS], ALU.mult)
                            link(nc.vector.tensor_scalar(row[:, NR], row[:, T0], -1.0, None, ALU.add))
                            tt(row[:, T0], row[:, MAG], row[:, SIN], ALU.mult)
                            tt(row[:, T1], row[:, LR], row[:, LR], ALU.mult)
                            tt(row[:, DEN], row[:, LI], row[:, LI], ALU.mult)
                            tt(row[:, DEN], row[:, DEN], row[:, T1], ALU.add)
                            link(nc.vector.reciprocal(row[:, DEN], row[:, DEN]))
                            tt(row[:, CR], row[:, NR], row[:, LR], ALU.mult)
                            tt(row[:, T1], row[:, T0], row[:, LI], ALU.mult)
                            tt(row[:, CR], row[:, CR], row[:, T1], ALU.add)
                            tt(row[:, CR], row[:, CR], row[:, DEN], ALU.mult)
                            tt(row[:, CI], row[:, T0], row[:, LR], ALU.mult)
                            tt(row[:, T1], row[:, NR], row[:, LI], ALU.mult)
                            tt(row[:, CI], row[:, CI], row[:, T1], ALU.subtract)
                            tt(row[:, CI], row[:, CI], row[:, DEN], ALU.mult)
                            dve.sem_inc(ready, 1)
                            dve.wait_ge(turned, 1)
                            vec.tick(nc.vector.tensor_copy(mag[:], PS[:, 0, 0:32]))
                            vec.tick(nc.vector.tensor_copy(powers[:, :, 0], PS[:, 0, 32:96].rearrange("p (a t) -> p a t", a=2)))
                            link(nc.vector.tensor_copy(coef[:], PS[:, 0, 96:160].rearrange("p (a t) -> p a t", a=2)))
                            bc = [coef[:, i].unsqueeze(2).to_broadcast([P, TILES, C]) for i in range(2)]
                            tt(prod[:, 0], b_in[:, 0], bc[0], ALU.mult)
                            tt(prod[:, 1], b_in[:, 1], bc[1], ALU.mult)
                            tt(prod[:, 2], b_in[:, 1], bc[0], ALU.mult)
                            tt(prod[:, 3], b_in[:, 0], bc[1], ALU.mult)
                            dve.wait_ge(pool.sem, zeroed)
                            for hf in range(2):
                                r = slice(64 * hf, 64 * hf + 64)
                                c = slice(C * hf, C * hf + C)
                                vec.tick(nc.vector.tensor_tensor(b_pad[r, 0, :, c], prod[r, 0], prod[r, 1], ALU.subtract))
                                link(nc.vector.tensor_tensor(b_pad[r, 1, :, c], prod[r, 2], prod[r, 3], ALU.add))
                            dve.sem_inc(padded, 1)
                            for k in range(8):
                                re, im = powers[:, 0, k], powers[:, 1, k]
                                re2, im2 = powers[:, 0, k + 1], powers[:, 1, k + 1]
                                t0, t1 = prod[:, 0, :, 0], prod[:, 0, :, 1]
                                tt(t0, re, re, ALU.mult)
                                tt(t1, im, im, ALU.mult)
                                tt(re2, t0, t1, ALU.subtract)
                                tt(t0, re, im, ALU.mult)
                                link(nc.vector.tensor_scalar(im2, t0, 2.0, None, ALU.mult))

                        @block.tensor
                        def _(pe):
                            pe.wait_ge(ready, 1)
                            for i, r in enumerate((MAG, COS, SIN, CR, CI)):
                                mm = nc.tensor.transpose(PS[:, 0, 32 * i:32 * i + 32], row[:, r], ident[0:TILES, 0:TILES])
                            mm.then_inc(turned, 1)
                            pe.wait_ge(padded, 1)
                            pe.wait_ge(c_loaded, 16 * 16)
                            for n in range(8):
                                if n >= 2:
                                    pe.wait_ge(copied, n - 1)
                                for i in range(2):
                                    nc.tensor.transpose(PS[:, 1 + n % 2, i * P:(i + 1) * P],
                                                        b_pad[:, i, 4 * n:4 * n + 4].rearrange("p t c -> p (t c)"), ident)
                                for i in range(2):
                                    mm = nc.tensor.transpose(PS[:, 1 + n % 2, (2 + i) * P:(3 + i) * P], c_in[:, i, n], ident)
                                mm.then_inc(turned, 1)

                with ExitStack() as run:
                    E = sbuf(run, "E", [P, 2, 2, 4, LEN])
                    bu = sbuf(run, "bu", [P, 2, 2, 4, LEN])
                    z = sbuf(run, "z", [P, 2, 4, LEN])
                    xs = sbuf(run, "xs", [P, 2, 4, LEN])
                    tmp = sbuf(run, "tmp", [P, 2, 4, P])
                    driven, drive_copied, tabled, rotated = (sem(f"ssm_{x}") for x in ("driven", "drive_copied", "tabled", "rotated"))
                    stated, summed, ykept, pstep = (sem(f"ssm_{x}") for x in ("stated", "summed", "ykept", "pstep"))
                    with nc.Block() as block:
                        @block.tensor
                        def _(pe):
                            def drive(j):
                                for part in range(2):
                                    n = 2 * j + part
                                    if n >= 1:
                                        pe.wait_ge(drive_copied, n)
                                    for q in range(4):
                                        r = slice(32 * q, 32 * q + 32)
                                        mm = nc.tensor.matmul(PS[:, q, 0:LEN], BT[r, j, part], uT[r, j], start=True, stop=True)
                                    mm.then_inc(driven, 1)

                            drive(0)
                            for j in range(UB):
                                if j + 1 < UB:
                                    drive(j + 1)
                                pe.wait_ge(stated, j + 1)
                                if j >= 2:
                                    pe.wait_ge(ykept, j - 1)
                                for q in range(4):
                                    r = slice(32 * q, 32 * q + 32)
                                    for part in range(2):
                                        mm = nc.tensor.matmul(PS[r, 4 + j % 2, 0:SEQ], CT[:, j, part, r], xs[:, part, q, META:LEN],
                                                              start=(part == 0), stop=(part == 1))
                                mm.then_inc(summed, 1)

                        @block.scalar
                        def _(a):
                            for j in range(UB):
                                for part in range(2):
                                    a.wait_ge(driven, 2 * j + part + 1)
                                    if j >= 2:
                                        a.wait_ge(rotated, j - 1)
                                    nc.scalar.copy(bu[:, j % 2, part], PS[:, 0:4, 0:LEN]).then_inc(drive_copied, 1)

                        @block.gpsimd
                        def _(g):
                            steps_done = 0

                            def link(instruction):
                                nonlocal steps_done
                                steps_done += 1
                                instruction.then_inc(pstep, 1)
                                g.wait_ge(pstep, steps_done)

                            for j in range(UB):
                                if j >= 2:
                                    g.wait_ge(stated, j - 1)
                                e = E[:, j % 2]
                                link(nc.gpsimd.memset(e[:, 0, :, 0:1], 1.0))
                                link(nc.gpsimd.memset(e[:, 1, :, 0:1], 0.0))
                                for k in range(9):
                                    L = 2 ** k
                                    m = min(L, LEN - L)
                                    pre, pim = (powers[:, i, k, 4 * j:4 * j + 4].unsqueeze(2).to_broadcast([P, 4, min(m, P)]) for i in range(2))
                                    for o in range(0, m, P):
                                        mm_ = min(P, m - o)
                                        pr, pi = pre[:, :, 0:mm_], pim[:, :, 0:mm_]
                                        lo_re, lo_im = e[:, 0, :, o:o + mm_], e[:, 1, :, o:o + mm_]
                                        hi_re, hi_im = e[:, 0, :, L + o:L + o + mm_], e[:, 1, :, L + o:L + o + mm_]
                                        ta, tb = tmp[:, 0, :, 0:mm_], tmp[:, 1, :, 0:mm_]
                                        link(nc.gpsimd.tensor_tensor(hi_re, lo_re, pr, ALU.mult))
                                        link(nc.gpsimd.tensor_tensor(ta, lo_im, pi, ALU.mult))
                                        link(nc.gpsimd.tensor_tensor(hi_re, hi_re, ta, ALU.subtract))
                                        link(nc.gpsimd.tensor_tensor(hi_im, lo_im, pr, ALU.mult))
                                        link(nc.gpsimd.tensor_tensor(tb, lo_re, pi, ALU.mult))
                                        link(nc.gpsimd.tensor_tensor(hi_im, hi_im, tb, ALU.add))
                                g.sem_inc(tabled, 1)

                        @block.vector
                        def _(dve):
                            def tt(o, i0, i1, op):
                                vec.tick(nc.vector.tensor_tensor(o, i0, i1, op))

                            def link():
                                dve.wait_ge(vec.sem, vec.value)

                            for j in range(UB):
                                dve.wait_ge(drive_copied, 2 * j + 2)
                                dve.wait_ge(tabled, j + 1)
                                cs, sn = E[:, j % 2, 0], E[:, j % 2, 1]
                                bre, bim = bu[:, j % 2, 0], bu[:, j % 2, 1]
                                if j >= 1:
                                    dve.wait_ge(summed, j)
                                tt(z[:, 0], cs, bre, ALU.mult)
                                tt(xs[:, 0], sn, bim, ALU.mult)
                                tt(z[:, 1], cs, bim, ALU.mult)
                                tt(xs[:, 1], sn, bre, ALU.mult)
                                link()
                                tt(z[:, 0], z[:, 0], xs[:, 0], ALU.add)
                                tt(z[:, 1], z[:, 1], xs[:, 1], ALU.subtract)
                                link()
                                dve.sem_inc(rotated, 1)
                                for part in range(2):
                                    for q in range(4):
                                        vec.tick(nc.vector.tensor_tensor_scan(
                                            xs[:, part, q], mag[:, 4 * j + q:4 * j + q + 1].to_broadcast([P, LEN]), z[:, part, q],
                                            0.0, ALU.mult, ALU.add))
                                link()
                                tt(z[:, 0], cs, xs[:, 0], ALU.mult)
                                tt(z[:, 1], sn, xs[:, 0], ALU.mult)
                                tt(bre, sn, xs[:, 1], ALU.mult)
                                tt(bim, cs, xs[:, 1], ALU.mult)
                                link()
                                tt(xs[:, 0], z[:, 0], bre, ALU.subtract)
                                tt(xs[:, 1], z[:, 1], bim, ALU.add)
                                link()
                                dve.sem_inc(stated, 1)
                                dve.wait_ge(summed, j + 1)
                                nc.vector.scalar_tensor_tensor(y[:, j], uT[:, j, META:LEN], col("ssm_d", j), PS[:, 4 + j % 2, 0:SEQ],
                                                               ALU.mult, ALU.add).then_inc(ykept, 1)
                with nc.Block() as block:
                    @block.scalar
                    def _(a):
                        act.tick(nc.scalar.activation(y, y, ACT.Gelu_apprx_tanh))

                ssm_out = sbuf(scope, "ssm_out", [P, DB, SEQ])

                def glu(dve, it, q, even, odd, gates, used):
                    nc.vector.tensor_tensor(ssm_out[:, bass.ds(it * 8 + 4 * q, 4)], even, gates[:, 1], ALU.mult).then_inc(banks_free[0], 1)
                    dve.sem_inc(banks_free[1], 1)
                    dve.wait_ge(banks_free[0], freed[0] + it * 2 + q + 1)
                    dve.sem_inc(used, 1)
                project_pair("glu", 2, lambda k: y[:, k, :], 1, glu, slabs=4)

                def mix(dve, it, q, even, odd, gates, used):
                    a_part, s_part = attn_out[:, bass.ds(it * 4, 4)], ssm_out[:, bass.ds(it * 4, 4)]
                    nc.vector.tensor_tensor(a_part, a_part, gates[:, 0], ALU.mult).then_inc(banks_free[0], 1)
                    nc.vector.tensor_tensor(s_part, s_part, gates[:, 1], ALU.mult).then_inc(banks_free[1], 1)
                    dve.wait_ge(banks_free[0], freed[0] + it + 1)
                    dve.wait_ge(banks_free[1], freed[1] + it + 1)
                    nc.vector.tensor_tensor(a_part, a_part, s_part, ALU.add).then_inc(used, 1)
                project_pair("mix_gates", 4, lambda k: nT[:, k, META:LEN], None, mix, both=True)

            def residual(it, s, ps):
                part = hT[:, bass.ds(it * 8 + 4 * s, 4), META:LEN]
                return nc.vector.tensor_tensor(part, part, ps, ALU.add)
            project("w_out", 4, lambda k: attn_out[:, k, :], SEQ, residual)

        with ExitStack() as scope:
            mT = sbuf(scope, "mT", [P, DB, SEQ])
            hid = sbuf(scope, "hid", [P, FF // P, SEQ])
            inverse_rms(xT, DB, SEQ, mT)
            scale_tokens(mT, xT, DB, SEQ, col("norm_ffn", 0, DB))

            def swiglu(dve, it, q, even, odd, gates, used):
                nc.vector.tensor_tensor(gates[:, 1], even, gates[:, 0], ALU.mult).then_inc(banks_free[0], 1)
                dve.wait_ge(banks_free[0], freed[0] + it + 1)
                nc.vector.tensor_tensor(hid[:, bass.ds(it * 4, 4)], odd, gates[:, 1], ALU.mult).then_inc(banks_free[1], 1)
                dve.wait_ge(banks_free[1], freed[1] + it + 1)
                dve.sem_inc(used, 1)
            project_pair("ffn_up", 4, lambda k: mT[:, k, :], 0, swiglu)

            ph_down = phases["ffn_down"]
            with nc.Block() as block:
                down_done = ten.value + 1

                @block.sync
                def _(sp):
                    stream(sp, ph_down)

                @block.tensor
                def _(pe):
                    def group(it, j, first, last):
                        slot = ph_down.slot(j)
                        pe.wait_ge(unit_loaded[slot], 16 * ph_down.uses(it, j))
                        for kt in range(KT):
                            rhs = hid[:, it * 2 * KT + (j // 4) * KT + kt, :] if isinstance(it, int) else \
                                hid[:, bass.ds(it * 2 * KT + (j // 4) * KT + kt, 1), :].rearrange("p a t -> p (a t)")
                            for m in range(MB):
                                M = 4 * (j % 4) + m
                                mm = nc.tensor.matmul(PS[:, M // 2, (M % 2) * SEQ:(M % 2 + 1) * SEQ],
                                                      ring[:, slot, kt, m * P:(m + 1) * P], rhs,
                                                      start=(first and kt == 0 and M % 2 == 0), stop=(last and kt == KT - 1),
                                                      skip_group_check=True)
                        mm.then_inc(slot_read[slot], 1)
                        return mm
                    for j in range(8):
                        group(0, j, j < 4, False)
                    with pe.Fori(1, ph_down.iters) as it:
                        for j in range(8):
                            group(it, j, False, False)
                    for j in range(4):
                        group(5, j, False, True)

                @block.vector
                def _(dve):
                    last = ph_down.slot(3)
                    dve.wait_ge(slot_read[last], ph_down.uses(5, 3))
                    vec.tick(nc.vector.tensor_tensor(xT, xT, PS[:, :, :].rearrange("p b (m t) -> p (b m) t", m=2), ALU.add))

            inverse_rms(xT, DB, SEQ, mT)
            scale_tokens(xT, xT, DB, SEQ, col("norm_final", 0, DB))

        with ExitStack() as two:
            c_silu = sbuf(two, "c_silu", [P, DB])
            mods = sbuf(two, "mods", [P, 3, 48])
            gains = sbuf(two, "gains", [P, DB])
            with nc.Block() as block:
                done = act.value + 1

                @block.scalar
                def _(a):
                    act.tick(nc.scalar.activation(c_silu[:], col("c_2", 0, DB), ACT.Sigmoid))

                @block.vector
                def _(dve):
                    dve.wait_ge(act.sem, done)
                    vec.tick(nc.vector.tensor_tensor(c_silu[:], c_silu[:], col("c_2", 0, DB), ALU.mult))

            def modulation(name, dst, bias, first_bias):
                ph = phases[name]
                with nc.Block() as block:
                    @block.sync
                    def _(sp):
                        stream(sp, ph)

                    @block.tensor
                    def _(pe):
                        with pe.Fori(0, ph.iters) as it:
                            for s in range(2):
                                pe.wait_ge(banks_free[s], freed[s] + it)
                                for ku in range(4):
                                    j = 4 * s + ku
                                    slot = ph.slot(j)
                                    pe.wait_ge(unit_loaded[slot], 16 * ph.uses(it, j))
                                    for kt in range(KT):
                                        k = ku * KT + kt
                                        for m in range(MB):
                                            mm = nc.tensor.matmul(PS[:, 4 * s, m:m + 1], ring[:, slot, kt, m * P:(m + 1) * P],
                                                                  c_silu[:, k:k + 1], start=(k == 0 and m == 0), stop=(k == DB - 1),
                                                                  skip_group_check=True)
                                    mm.then_inc(slot_read[slot], 1)

                    @block.vector
                    def _(dve):
                        tile, row_, _n = VECTOR_ROWS[bias]
                        first = tile * P + row_ + first_bias
                        with dve.Fori(0, ph.iters) as it:
                            for s in range(2):
                                wait_slab(dve, ph, it, s, 4)
                                nc.vector.tensor_tensor(dst[:, bass.ds(it * 8 + 4 * s, 4)], PS[:, 4 * s, 0:MB],
                                                        cols[:, bass.ds(it * 8 + 4 * s + first, 4)], ALU.add).then_inc(banks_free[s], 1)
                for s in range(2):
                    freed[s] += ph.iters

            def modulated(dst, gain, mod):
                small_ops([lambda: nc.vector.scalar_tensor_tensor(gains[:], mod[:, DB:2 * DB], 1.0, gain, ALU.add, ALU.mult)])
                scale_tokens(dst, xT, DB, SEQ, gains, mod[:, 0:DB])

            def post_norm(y_out, gain, gate, squares):
                inverse_rms(y_out, DB, SEQ, squares)
                small_ops([lambda: nc.vector.tensor_tensor(gains[:], gain, gate, ALU.mult)])
                scale_tokens(y_out, y_out, DB, SEQ, gains)
                small_ops([lambda: nc.vector.tensor_tensor(xT, xT, y_out[:], ALU.add)])

            modulation("ada0", mods[:, 0], "ada_b_2", 0)
            with ExitStack() as scope:
                qk = sbuf(scope, "qk", [P, 2 * A_QK // P, SEQ])
                heads_view = qk[:].rearrange("p (r h e) t -> p r h e t", r=2, e=2)
                with ExitStack() as inner:
                    hn = sbuf(inner, "hn", [P, DB, SEQ])
                    with ExitStack() as proj:
                        gate_rows = sbuf(proj, "gate_rows", [A_HEADS, 8, SEQ])
                        pick = sbuf(proj, "pick", [A_HEADS, A_HEADS * P])
                        va = sbuf(proj, "va", [P, 2, A_INNER])
                        w_g = sbuf(proj, "w_g", [P, DB, 2 * A_HEADS])
                        b_g = sbuf(proj, "b_g", [A_HEADS, 2])
                        inverse_rms(xT, DB, SEQ, hn)
                        modulated(hn, col("g_pre_2", 0, DB), mods[:, 0])

                        project("a_qk", 4, lambda k: hn[:, k, :], SEQ,
                                lambda it, s, ps: nc.vector.tensor_copy(qk[:, bass.ds(it * 8 + 4 * s, 4)], ps))

                        ph_v = phases["a_v"]
                        with ExitStack() as conv:
                            acc = sbuf(conv, "acc", [P, MB, SEQ])
                            term = sbuf(conv, "term", [P, MB, SEQ])
                            with nc.Block() as block:
                                @block.sync
                                def _(sp):
                                    stream(sp, ph_v)

                                values_by_token(nc, block, ph_v, ring, PS, hn, unit_loaded, slot_read, banks_free, freed, va)

                                @block.vector
                                def _(dve):
                                    def link(instruction):
                                        dve.wait_ge(vec.sem, vec.tick(instruction))

                                    def taps(j, b):
                                        t0 = 32 * j + b * MB
                                        return cols[:, t0:t0 + MB].unsqueeze(2)

                                    for b in range(2 * A_QK // COLS):
                                        part = qk[:, b * MB:(b + 1) * MB]
                                        link(nc.vector.tensor_tensor(acc[:], part, taps(CONV - 1, b).to_broadcast([P, MB, SEQ]), ALU.mult))
                                        link(nc.vector.tensor_tensor(acc[:], acc[:], col("a_conv_b_2", b * MB, MB).unsqueeze(2).to_broadcast([P, MB, SEQ]), ALU.add))
                                        for back in range(1, CONV):
                                            n = SEQ - back
                                            link(nc.vector.tensor_tensor(term[:, :, 0:n], part[:, :, 0:n],
                                                                         taps(CONV - 1 - back, b).to_broadcast([P, MB, n]), ALU.mult))
                                            link(nc.vector.tensor_tensor(acc[:, :, back:SEQ], acc[:, :, back:SEQ], term[:, :, 0:n], ALU.add))
                                        link(nc.vector.tensor_copy(part, acc[:]))
                            for s in range(2):
                                freed[s] += ph_v.iters
                            with nc.Block() as block:
                                base_a, base_v = act.value, vec.value

                                @block.scalar
                                def _(a):
                                    for b in range(8):
                                        if b >= 2:
                                            a.wait_ge(vec.sem, base_v + b - 1)
                                        act.tick(nc.scalar.activation((acc, term)[b % 2][:], qk[:, b * MB:(b + 1) * MB], ACT.Sigmoid))

                                @block.vector
                                def _(dve):
                                    for b in range(8):
                                        dve.wait_ge(act.sem, base_a + b + 1)
                                        part = qk[:, b * MB:(b + 1) * MB]
                                        vec.tick(nc.vector.tensor_tensor(part, part, (acc, term)[b % 2][:], ALU.mult))

                        with nc.Block() as block:
                            gates_in = small[0] + 48
                            gated = ten.value + 1
                            a0, v0 = act.value, vec.value

                            @block.sync
                            def _(sp):
                                load_small(sp, w_g[:], w["a_w_in_2"][:, A_G0:A_G0 + 2 * A_HEADS].rearrange("(k p) n -> p k n", p=P))
                                load_small(sp, pick[:], w["head_pick"])
                                load_small(sp, b_g[:], w["a_gate_b_2"])

                            @block.tensor
                            def _(pe):
                                pe.wait_ge(small_loaded, gates_in)
                                for g in range(2):
                                    for k in range(DB):
                                        mm = nc.tensor.matmul(PS[0:A_HEADS, g, 0:SEQ], w_g[:, k, g * A_HEADS:(g + 1) * A_HEADS],
                                                              hn[:, k], start=(k == 0), stop=(k == DB - 1))
                                ten.tick(mm)

                            I, FG_, ABS, CUM, A_, MM, EN, ZERO = range(8)

                            @block.scalar
                            def _(a):
                                a.wait_ge(vec.sem, v0 + 3)
                                for fn, dst, src, kw in ((ACT.Abs, ABS, FG_, {}), (ACT.Exp, ABS, ABS, {"scale": -1.0}),
                                                         (ACT.Ln, ABS, ABS, {"bias": ones[0:A_HEADS, 0:1]})):
                                    n = act.tick(nc.scalar.activation(gate_rows[:, dst], gate_rows[:, src], fn, **kw))
                                    a.wait_ge(act.sem, n)
                                a.wait_ge(vec.sem, v0 + 9)
                                act.tick(nc.scalar.activation(gate_rows[:, EN], gate_rows[:, EN], ACT.Exp, scale=-1.0))

                            @block.vector
                            def _(dve):
                                def link(instruction):
                                    dve.wait_ge(vec.sem, vec.tick(instruction))
                                dve.wait_ge(ten.sem, gated)
                                link(nc.vector.memset(gate_rows[:, ZERO], 0.0))
                                link(nc.vector.tensor_scalar(gate_rows[:, I], PS[0:A_HEADS, 0, 0:SEQ], b_g[:, 0:1], None, ALU.add))
                                link(nc.vector.tensor_scalar(gate_rows[:, FG_], PS[0:A_HEADS, 1, 0:SEQ], b_g[:, 1:2], None, ALU.add))
                                dve.wait_ge(act.sem, a0 + 3)
                                link(nc.vector.tensor_scalar(gate_rows[:, FG_], gate_rows[:, FG_], 0.0, None, ALU.min))
                                link(nc.vector.tensor_tensor(gate_rows[:, FG_], gate_rows[:, FG_], gate_rows[:, ABS], ALU.subtract))
                                link(nc.vector.tensor_tensor_scan(gate_rows[:, CUM], ones[0:A_HEADS, 0:1].to_broadcast([A_HEADS, SEQ]),
                                                                  gate_rows[:, FG_], 0.0, ALU.mult, ALU.add))
                                link(nc.vector.tensor_tensor(gate_rows[:, A_], gate_rows[:, I], gate_rows[:, CUM], ALU.subtract))
                                link(nc.vector.tensor_tensor_scan(gate_rows[:, MM], gate_rows[:, A_], gate_rows[:, ZERO], 0.0, ALU.max, ALU.max))
                                link(nc.vector.tensor_tensor(gate_rows[:, EN], gate_rows[:, CUM], gate_rows[:, MM], ALU.add))

                        mlstm_heads(nc, sem, sbuf, PS, gate_rows, qk, va, ident, ones, after, pick)

                    with ExitStack() as hs:
                        rms_head = sbuf(hs, "rms_head", [P, A_HEADS, SEQ])
                        sq = sbuf(hs, "sq", [P, 2, 4, SEQ])
                        squared, hsum, sq_used = sem("head_squared"), sem("head_summed"), sem("head_rooted")
                        with nc.Block() as block:
                            @block.gpsimd
                            def _(g):
                                for h in range(A_HEADS):
                                    if h >= 2:
                                        g.wait_ge(hsum, h - 1)
                                    for r in range(2):
                                        src = heads_view[:, r, h]
                                        last = nc.gpsimd.tensor_tensor(sq[:, h % 2, 2 * r:2 * r + 2], src, src, ALU.mult)
                                        last.then_inc(squared, 1)

                            @block.tensor
                            def _(pe):
                                for h in range(A_HEADS):
                                    pe.wait_ge(squared, 2 * h + 2)
                                    if h >= 4:
                                        pe.wait_ge(sq_used, h - 3)
                                    for e in range(4):
                                        mm = nc.tensor.matmul(PS[:, h % 4, 0:SEQ], ones[:], sq[:, h % 2, e], start=(e == 0), stop=(e == 3))
                                    mm.then_inc(hsum, 1)

                            @block.scalar
                            def _(a):
                                for h in range(A_HEADS):
                                    a.wait_ge(hsum, h + 1)
                                    nc.scalar.activation(rms_head[:, h], PS[:, h % 4, 0:SEQ], ACT.Sqrt, scale=1.0 / A_DV,
                                                         bias=eps[:, 0:1]).then_inc(sq_used, 1)

                            @block.vector
                            def _(dve):
                                def link():
                                    dve.wait_ge(vec.sem, vec.value)
                                for h in range(A_HEADS):
                                    dve.wait_ge(sq_used, h + 1)
                                    vec.tick(nc.vector.reciprocal(rms_head[:, h], rms_head[:, h]))
                                    link()
                                    for e in range(4):
                                        ht = heads_view[:, e // 2, h, e % 2]
                                        vec.tick(nc.vector.scalar_tensor_tensor(ht, ht, col("a_g_head_2", 4 * h + e), rms_head[:, h], ALU.mult, ALU.mult))

                    def output_gate(dve, it, q, even, odd, gates, used):
                        nc.vector.tensor_tensor(gates[:, 1], odd, gates[:, 1], ALU.mult).then_inc(banks_free[1], 1)
                        dve.wait_ge(banks_free[1], freed[1] + it + 1)
                        nc.vector.tensor_tensor(gates[:, 0], gates[:, 0], gates[:, 1], ALU.mult).then_inc(banks_free[0], 1)
                        dve.wait_ge(banks_free[0], freed[0] + it + 1)
                        ht = qk[:].rearrange("p (r b) t -> p r b t", r=2)[:, :, bass.ds(it * 2, 2)]
                        nc.vector.tensor_tensor(ht, ht, gates[:, 0].rearrange("p (r e) t -> p r e t", r=2), ALU.mult).then_inc(used, 1)
                    project_pair("a_oz", 4, lambda k: hn[:, k, :], None, output_gate, both=True)
                y_out = sbuf(scope, "y_out", [P, DB, SEQ])
                room = sbuf(scope, "room", [P, DB, SEQ])
                project("a_out", 8, lambda k: heads_view[:, k % 4 // 2, k // 4, k % 2], SEQ,
                        lambda it, s, ps: nc.vector.tensor_copy(y_out[:, bass.ds(it * 8 + 4 * s, 4)], ps))
                post_norm(y_out, col("g_post_2", 0, DB), mods[:, 0, 2 * DB:3 * DB], room)

            modulation("ada1", mods[:, 1], "ada_b_2", 3 * DB)
            modulation("kv_ada", mods[:, 2], "kv_ada_b_2", 0)
            with ExitStack() as scope:
                hn = sbuf(scope, "hn", [P, DB, SEQ])
                kb = sbuf(scope, "kb", [P, DB, SEQ])
                vb = sbuf(scope, "vb", [P, 2, D])
                qb = sbuf(scope, "qb", [P, DB, SEQ])
                zb = sbuf(scope, "zb", [P, DB, SEQ])
                bias = sbuf(scope, "bias", [P, HEADS, SEQ])
                rel = sbuf(scope, "rel", [HEADS, 2 * MAX_REL + 1])
                drawn = sbuf(scope, "drawn", [HEADS, 3 * P])

                with nc.Block() as block:
                    rel_loaded, made = small[0] + 16, vec.value + 2
                    spread_done = small[0] + 48

                    @block.sync
                    def _(sp):
                        load_small(sp, rel[:], w["b_rel_2"])
                        sp.wait_ge(vec.sem, made)
                        load_small(sp, w["rel_scratch"], drawn[:])
                        sp.wait_ge(small_loaded, rel_loaded + 16)
                        scratch = w["rel_scratch"]
                        load_small(sp, bias[:], bass.AP(tensor=scratch.tensor, offset=scratch.offset,
                                                        ap=[[1, P], [3 * P, HEADS], [1, SEQ]]))

                    @block.vector
                    def _(dve):
                        dve.wait_ge(small_loaded, rel_loaded)
                        vec.tick(nc.vector.tensor_copy(drawn[:, 2 * P:3 * P], rel[:, 2 * MAX_REL:2 * MAX_REL + 1].to_broadcast([HEADS, P])))
                        vec.tick(nc.vector.tensor_copy(drawn[:, 0:2 * P], rel[:, 1:2 * MAX_REL + 1]))
                        dve.wait_ge(small_loaded, spread_done)
                        vec.tick(nc.vector.memset(bias[0:CHUNK, :, 0:CHUNK], NEG))

                inverse_rms(xT, DB, SEQ, hn)
                modulated(hn, col("kv_g_2", 0, DB), mods[:, 2])
                project("b_k", 4, lambda k: hn[:, k, :], SEQ,
                        lambda it, s, ps: nc.vector.tensor_copy(kb[:, bass.ds(it * 8 + 4 * s, 4)], ps))
                ph_v = phases["b_v"]
                with nc.Block() as block:
                    @block.sync
                    def _(sp):
                        stream(sp, ph_v)

                    values_by_token(nc, block, ph_v, ring, PS, hn, unit_loaded, slot_read, banks_free, freed, vb)
                for s in range(2):
                    freed[s] += ph_v.iters
                modulated(hn, col("g_pre_2", DB, DB), mods[:, 1])
                project("b_q", 4, lambda k: hn[:, k, :], SEQ,
                        lambda it, s, ps: nc.vector.tensor_copy(qb[:, bass.ds(it * 8 + 4 * s, 4)], ps))
                project("b_z", 4, lambda k: hn[:, k, :], SEQ,
                        lambda it, s, ps: nc.vector.tensor_copy(zb[:, bass.ds(it * 8 + 4 * s, 4)], ps))

                def band_keys(n):
                    return P * (n % 2 + 1)

                attention("band", HEADS, lambda n: [(qb[:, n // 2, (n % 2) * P:(n % 2 + 1) * P], kb[:, n // 2, 0:band_keys(n)])],
                          band_keys, lambda n: bias[:, n // 2, 0:band_keys(n)][:, ::-1], P ** -0.5, vb, qb)
                with nc.Block() as block:
                    base_a = act.value

                    @block.scalar
                    def _(a):
                        act.tick(nc.scalar.activation(hn[:], zb[:], ACT.Sigmoid))

                    @block.vector
                    def _(dve):
                        n = vec.tick(nc.vector.tensor_tensor(qb[:], qb[:], zb[:], ALU.mult))
                        dve.wait_ge(vec.sem, n)
                        dve.wait_ge(act.sem, base_a + 1)
                        vec.tick(nc.vector.tensor_tensor(qb[:], qb[:], hn[:], ALU.mult))
                project("b_out", 4, lambda k: qb[:, k, :], SEQ,
                        lambda it, s, ps: nc.vector.tensor_copy(kb[:, bass.ds(it * 8 + 4 * s, 4)], ps))
                post_norm(kb, col("g_post_2", DB, DB), mods[:, 1, 2 * DB:3 * DB], hn)

        with ExitStack() as scope:
            rows_out = sbuf(scope, "rows_out", [P, 2, D])
            turned, copied = sem("output_turned"), sem("output_copied")
            with nc.Block() as block:
                @block.tensor
                def _(pe):
                    for n in range(8):
                        if n >= 4:
                            pe.wait_ge(copied, n - 3)
                        for q in range(4):
                            k, t = (n % 4) * 4 + q, n // 4
                            mm = nc.tensor.transpose(PS[:, n % 4, q * P:(q + 1) * P], xT[:, k, t * P:(t + 1) * P], ident)
                        mm.then_inc(turned, 1)

                @block.vector
                def _(dve):
                    for n in range(8):
                        dve.wait_ge(turned, n + 1)
                        nc.vector.tensor_copy(rows_out[:, n // 4, (n % 4) * COLS:(n % 4 + 1) * COLS], PS[:, n % 4, :]).then_inc(copied, 1)

                @block.sync
                def _(sp):
                    for t in range(2):
                        sp.wait_ge(copied, 4 * t + 4)
                        sp.dma_start(out[t * P:(t + 1) * P, :], rows_out[:, t]).then_inc(stored, 16)
                    sp.wait_ge(stored, 32)


def values_by_token(nc, block, ph, ring, PS, hn, unit_loaded, slot_read, banks_free, freed, v):
    @block.tensor
    def _(pe):
        with pe.Fori(0, ph.iters) as it:
            for s in range(2):
                pe.wait_ge(banks_free[s], freed[s] + it)
                for ku in range(4):
                    j = 4 * s + ku
                    slot = ph.slot(j)
                    pe.wait_ge(unit_loaded[slot], 16 * ph.uses(it, j))
                    for kt in range(KT):
                        k = ku * KT + kt
                        for t in range(2):
                            mm = nc.tensor.matmul(PS[:, 4 * s + t, :], hn[:, k, t * P:(t + 1) * P], ring[:, slot, kt],
                                                  start=(k == 0), stop=(k == DB - 1))
                    mm.then_inc(slot_read[slot], 1)

    @block.scalar
    def _(a):
        with a.Fori(0, ph.iters) as it:
            for s in range(2):
                j = 4 * s + 3
                a.wait_ge(slot_read[ph.slot(j)], ph.uses(it, j))
                nc.scalar.copy(v[:, :, bass.ds(it * 2 * COLS + s * COLS, COLS)], PS[:, 4 * s:4 * s + 2, :]).then_inc(banks_free[s], 1)


def mlstm_heads(nc, sem, sbuf, PS, gate_rows, qk, va, ident, ones, after, head_pick):
    I, FG_, ABS, CUM, A_, MM, EN, ZERO = range(8)
    QB = A_DK // P
    W0 = SEQ + P
    with ExitStack() as scope:
        a_cols = sbuf(scope, "a_cols", [P, 2, A_HEADS])
        wt = sbuf(scope, "wt", [P, 2, W0])
        st = sbuf(scope, "st", [P, 2, W0])
        den = sbuf(scope, "den", [P, 2, SEQ])
        spread, scored, a_turned, a_kept = (sem(f"mlstm_{x}") for x in ("spread", "scored", "a_turned", "a_kept"))
        masked, exped, weighted, valued = (sem(f"mlstm_{x}") for x in ("masked", "exped", "weighted", "valued"))
        absed, kept, dstep = (sem(f"mlstm_{x}") for x in ("absed", "kept", "dstep"))
        with nc.Block() as block:
            @block.tensor
            def _(pe):
                for b in range(2):
                    mm = nc.tensor.transpose(PS[:, 7, 8 * b:8 * b + 8], gate_rows[:, A_, b * P:(b + 1) * P], ident[0:A_HEADS, 0:A_HEADS])
                mm.then_inc(a_turned, 1)

                def front(h):
                    if h >= 2:
                        pe.wait_ge(kept, h - 1)
                    for i, r in enumerate((MM, EN)):
                        mm = nc.tensor.matmul(PS[:, h % 2, i * SEQ:(i + 1) * SEQ], head_pick[0:A_HEADS, h * P:(h + 1) * P],
                                              gate_rows[:, r], start=True, stop=True)
                    mm.then_inc(spread, 1)
                    for b in range(2):
                        dst = PS[:, 2 + h % 2, b * SEQ:b * SEQ + SEQ - b * P]
                        for i in range(QB):
                            mm = nc.tensor.matmul(dst, qk[:, A_QK // P + QB * h + i, b * P:(b + 1) * P], qk[:, QB * h + i, b * P:SEQ],
                                                  start=(i == 0), stop=(i == QB - 1))
                    mm.then_inc(scored, 1)

                front(0)
                for h in range(A_HEADS):
                    if h + 1 < A_HEADS:
                        front(h + 1)
                    pe.wait_ge(weighted, h + 1)
                    if h >= 1:
                        pe.wait_ge(kept, h)
                    for e in range(5):
                        dst = PS[:, 4 + e // 2, (e % 2) * SEQ:(e % 2 + 1) * SEQ]
                        for b in range(2):
                            lhsT = va[:, b, h * A_DV + e * P:h * A_DV + (e + 1) * P] if e < 4 else ones[:]
                            mm = nc.tensor.matmul(dst[:, b * P:SEQ], lhsT, st[:, h % 2, b * SEQ:b * SEQ + SEQ - b * P],
                                                  start=(b == 0), stop=(b == 1))
                    mm.then_inc(valued, 1)

            @block.scalar
            def _(a):
                a.wait_ge(a_kept, 1)
                for h in range(A_HEADS):
                    a.wait_ge(masked, h + 1)
                    nc.scalar.activation(wt[:, h % 2, 0:SEQ], wt[:, h % 2, 0:SEQ], ACT.Exp, scale=-1.0, bias=a_cols[:, 0, h:h + 1])
                    nc.scalar.activation(wt[:, h % 2, SEQ:W0], wt[:, h % 2, SEQ:W0], ACT.Exp, scale=-1.0,
                                         bias=a_cols[:, 1, h:h + 1]).then_inc(exped, 1)
                    if h >= 1:
                        denominator(nc, a, h - 1, valued, absed, kept, den, PS)
                denominator(nc, a, A_HEADS - 1, valued, absed, kept, den, PS)

            @block.vector
            def _(dve):
                steps = 0

                def link(instruction):
                    nonlocal steps
                    steps += 1
                    instruction.then_inc(dstep, 1)
                    dve.wait_ge(dstep, steps)

                def mask(h):
                    dve.wait_ge(spread, h + 1)
                    b = h % 2
                    nc.vector.tensor_tensor(wt[:, b, 0:SEQ], PS[:, b, 0:SEQ], after, ALU.add)
                    nc.vector.tensor_tensor(wt[:, b, SEQ:W0], PS[:, b, P:SEQ], after[:, 0:P], ALU.add).then_inc(masked, 1)

                dve.wait_ge(a_turned, 1)
                nc.vector.tensor_copy(a_cols[:], PS[:, 7, 0:16].rearrange("p (b h) -> p b h", b=2)).then_inc(a_kept, 1)
                mask(0)
                for h in range(A_HEADS):
                    b = h % 2
                    dve.wait_ge(scored, h + 1)
                    dve.wait_ge(exped, h + 1)
                    nc.vector.scalar_tensor_tensor(st[:, b], PS[:, 2 + b, 0:W0], A_DK ** -0.5, wt[:, b], ALU.mult, ALU.mult).then_inc(weighted, 1)
                    if h + 1 < A_HEADS:
                        mask(h + 1)
                    dve.wait_ge(absed, h + 1)
                    link(nc.vector.tensor_tensor(den[:, b], den[:, b], PS[:, b, SEQ:2 * SEQ], ALU.max))
                    link(nc.vector.reciprocal(den[:, b], den[:, b]))
                    for r in range(2):
                        dst = qk[:, r * (A_QK // P) + QB * h:r * (A_QK // P) + QB * h + QB]
                        last = nc.vector.tensor_tensor(dst, PS[:, 4 + r, :].rearrange("p (e t) -> p e t", e=2),
                                                       den[:, b].unsqueeze(1).to_broadcast([P, 2, SEQ]), ALU.mult)
                    last.then_inc(kept, 1)


def denominator(nc, a, h, valued, absed, kept, den, PS):
    a.wait_ge(valued, h + 1)
    nc.scalar.activation(den[:, h % 2], PS[:, 6, 0:SEQ], ACT.Abs).then_inc(absed, 1)


def shape_constants():
    import numpy as np
    a = np.zeros((P, CONST_COLS), np.float32)

    def put(name, value):
        first, n = CONST[name]
        a[:value.shape[0], first:first + n] = value

    put("identity", np.eye(P, dtype=np.float32))
    half = ROPE // 2
    freqs = np.float32(10000.0) ** (-np.arange(half, dtype=np.float32) / np.float32(half))
    ang = np.arange(LEN, dtype=np.float32)[None, :] * freqs[:, None]
    put("cos", np.tile(np.cos(ang), (4, 1)))
    put("sin", np.tile(np.concatenate([-np.sin(ang), np.sin(ang)]), (2, 1)))
    p = np.arange(P)[:, None]
    put("causal", np.where(np.arange(LEN)[None, :] <= P + META + p, 0.0, NEG))
    put("after", np.where(np.arange(SEQ)[None, :] < p, -NEG, 0.0))
    return a


_MATRICES = ["w_in", "w_kv_up", "w_attn_proj", "w_glu_val", "w_glu_gate", "w_out", "w_ffn_gate", "w_ffn_up",
             "w_ffn_down", "a_w_in_2", "a_w_out_2", "b_w_in_2", "b_w_out_2"]


def kernel(**inputs):
    import numpy as np
    import concourse.bacc as bacc
    from concourse.bass_utils import run_bass_kernel_spmd as run

    nc = bacc.Bacc("TRN2", target_bir_lowering=False, num_devices=1)
    arrays, w = {}, {}

    def give(name, a):
        a = np.ascontiguousarray(a)
        arrays[f"in_{name}"] = a
        w[name] = nc.dram_tensor(f"in_{name}", a.shape, F32, kind="ExternalInput").ap()

    for name in _MATRICES:
        give(name, np.asarray(inputs[name])[0])
    q_up = np.asarray(inputs["w_q_up"])[0].reshape(LORA, HEADS // 2, 2, NOPE + ROPE)
    give("w_q_up", np.concatenate([q_up[..., :NOPE].reshape(LORA, HEADS // 2, -1),
                                   q_up[..., NOPE:].reshape(LORA, HEADS // 2, -1)], axis=2).reshape(LORA, -1))
    for l in range(2):
        give(f"ada_w_{l}", np.asarray(inputs["ada_w_2"])[l])
    for name in ("kv_ada_w_2", "kv_w_2", "meta_tokens"):
        give(name, inputs[name])
    for name in ("ssm_lambda_re", "ssm_lambda_im", "ssm_log_step", "ssm_b_re", "ssm_b_im", "ssm_c_re", "ssm_c_im",
                 "b_rel_2", "x"):
        give(name, np.asarray(inputs[name])[0])
    give("a_gate_b_2", np.asarray(inputs["a_gate_b_2"])[0].reshape(2, A_HEADS).T)
    for name in VECTOR_ROWS:
        give(name + "_rows", np.asarray(inputs[name]).reshape(-1, P))
    give("shape_constants", shape_constants())
    give("head_pick", np.kron(np.eye(A_HEADS), np.ones((1, P))).astype(np.float32))
    w["rel_scratch"] = nc.dram_tensor("rel_scratch", (HEADS, 3 * P), F32, kind="Internal").ap()
    out = nc.dram_tensor("out_x", (SEQ, D), F32, kind="ExternalOutput").ap()
    build(nc, w, out)
    r = run(nc, [arrays], core_ids=[0])
    return r.results[0]["out_x"].reshape(1, SEQ, D)
```

```python
from contextlib import ExitStack

import concourse.bass as bass
from concourse import mybir

F32 = mybir.dt.float32
F32R = mybir.dt.float32r
I32 = mybir.dt.int32
ALU = mybir.AluOpType
ACT = mybir.ActivationFunctionType
AX = mybir.AxisListType.X

P = 128
D = 2048
DB = D // P
SEQ = 256
META = 16
LEN = SEQ + META
EPS = 1e-6
NEG = -1e30

SLOTS = 4
KT = 4
COLS = 512
MB = COLS // P

HEADS = 16
LORA = 512
NOPE, ROPE, VH = 128, 64, 128
G, N, C = 64, 64, 16
SSM_W = G * C
OFF_KR = 2 * LORA
OFF_U = OFF_KR + ROPE
OFF_G = OFF_U + SSM_W
FF = 5632

FF_PARTS = ((0, 6), (6, 5))

A_INNER, A_QK, A_HEADS, CONV = 4096, 2048, 8, 4
A_DK, A_DV = A_QK // A_HEADS, A_INNER // A_HEADS
I, FG_, ABS, CUM, MM = range(5)
A_, ZERO, EN = I, FG_, ABS
A_V0, A_O0, A_Z0, A_G0 = 2 * A_QK, 2 * A_QK + A_INNER, 2 * A_QK + 2 * A_INNER, 2 * A_QK + 3 * A_INNER
CHUNK, MAX_REL = 64, 128

VECTOR_ROWS = {
    "a_conv_w_2": (0, 0, 128),
    "ada_b_2": (1, 0, 96), "kv_ada_b_2": (1, 96, 32),
    "g_pre_2": (2, 0, 32), "g_post_2": (2, 32, 32), "norm_mix": (2, 64, 16), "norm_ffn": (2, 80, 16),
    "norm_final": (2, 96, 16), "kv_g_2": (2, 112, 16),
    "a_conv_b_2": (3, 0, 32), "a_g_head_2": (3, 32, 32), "c_2": (3, 64, 16), "norm_q": (3, 80, 4),
    "norm_kv": (3, 84, 4), "ssm_d": (3, 88, 8),
}
VECTOR_TILE_ROWS = (128, 128, 128, 96)

CONST = {"identity": (0, 128), "after": (128, SEQ)}
CONST_COLS = 128 + SEQ
CONST_ONE = {"cos": (0, LEN), "sin": (LEN, LEN), "causal": (2 * LEN, LEN)}


class Phase:

    def __init__(self, base, iters, upi, source, extra, splits):
        self.base, self.iters, self.upi, self.source, self.extra, self.splits = base, iters, upi, source, extra, splits
        self.raw = upi + upi // 2 if extra is not None else upi
        assert iters == 1 or self.raw % SLOTS == 0
        self.end = base + iters * self.raw

    def place(self, j):
        return j + j // 2 if self.extra is not None else j

    def slot_at(self, r):
        return (self.base + r) % SLOTS

    def uses_at(self, it, r):
        return (self.base + r) // SLOTS + it * (self.raw // SLOTS) + 1

    def slot(self, j):
        return self.slot_at(self.place(j))

    def uses(self, it, j):
        return self.uses_at(it, self.place(j))

    def fills(self, it, j):
        return (self.splits + j) // 2 + it * (self.upi // 2) + 1


def plan_units(w):
    phases, flat = {}, []

    def block(m, row, col, cols=COLS):
        rows = m[bass.ds(row, KT * P), :] if not isinstance(row, int) else m[row:row + KT * P, :]
        part = rows[:, bass.ds(col, cols)] if not isinstance(col, int) else rows[:, col:col + cols]
        return part.rearrange("(k p) n -> p k n", p=P)

    splits = [0]

    def add(name, iters, upi, source, extra=None, split=True):
        ph = phases[name] = Phase(len(flat), iters, upi, source, extra, splits[0] if split else None)
        for it in range(iters):
            for r in range(ph.raw):
                flat.append((lambda it, r, ph=ph: round_unit(ph, it, r), it, r))
        assert len(flat) == ph.end
        if split:
            splits[0] += iters * upi

    def round_unit(ph, it, r):
        if ph.extra is None:
            return ph.source(it, r)
        if r % 3 == 2:
            return block(w["ada_all"], (r // 3) % 4 * KT * P, (it + ph.extra + r // 12) * COLS)
        return ph.source(it, r - r // 3)

    plan_units.round_unit = round_unit

    def slabs(m, first, k_units, per=2):
        return lambda it, j: block(m, (j % k_units) * KT * P, first + it * per * COLS + (j // k_units) * COLS)

    def pair(m0, c0, m1, c1, k_units, per=1):
        def source(it, j):
            s = j // k_units
            m, c = ((m0, c0), (m1, c1))[s % 2]
            return block(m, (j % k_units) * KT * P, c + it * per * COLS + (s // 2) * COLS)
        return source

    add("latents", 1, 8, slabs(w["w_in"], 0, 4))
    add("u", 1, 8, slabs(w["w_in"], OFF_U, 4), extra=0)
    add("q_up", 1, 8, lambda it, j: block(w["w_q_up"], 0, j * 2 * (NOPE + ROPE), 2 * (NOPE + ROPE)), split=False)
    add("kv_up", 1, 8, lambda it, j: block(w["w_kv_up"], 0, j * COLS), split=False)
    add("attn_proj", 2, 8, slabs(w["w_attn_proj"], 0, 4), extra=1)
    add("glu", 2, 8, pair(w["w_glu_gate"], 0, w["w_glu_val"], 0, 2, 2))
    add("mix_gates", 4, 8, pair(w["w_in"], OFF_G, w["w_in"], OFF_G + D, 4), extra=3)
    add("w_out", 2, 8, slabs(w["w_out"], 0, 4), extra=7)
    for part, (first, n) in enumerate(FF_PARTS):
        add(f"ffn_up{part}", n, 8, pair(w["w_ffn_gate"], first * COLS, w["w_ffn_up"], first * COLS, 4), extra=9 + first)
        add(f"ffn_down{part}", 1, 4 * n,
            lambda it, j, first=first: block(w["w_ffn_down"], (first + j // 4) * KT * P, (j % 4) * COLS))
    add("a_qk", 4, 8, slabs(w["a_w_in_2"], 0, 4), extra=20)
    add("a_v", 4, 8, slabs(w["a_w_in_2"], A_V0, 4))
    add("a_oz", 8, 8, pair(w["a_w_in_2"], A_O0, w["a_w_in_2"], A_Z0, 4), extra=24)
    add("a_out", 2, 16, slabs(w["a_w_out_2"], 0, 8))
    add("b_k", 2, 8, slabs(w["kv_w_2"], 0, 4))
    add("b_v", 2, 8, slabs(w["kv_w_2"], D, 4))
    add("b_q", 2, 8, slabs(w["b_w_in_2"], 0, 4))
    add("b_z", 2, 8, slabs(w["b_w_in_2"], D, 4))
    add("b_out", 2, 8, slabs(w["b_w_out_2"], 0, 4))
    return phases, flat


class Step:

    def __init__(self, sem):
        self.sem, self.value = sem, 0

    def tick(self, instruction):
        self.value += 1
        instruction.then_inc(self.sem, 1)
        return self.value


def build(nc, w, out):
    with ExitStack() as ctx:
        names = [0]

        def sem(name):
            return ctx.enter_context(nc.semaphore(name))

        def sbuf(stack, name, shape, dtype=F32):
            names[0] += 1
            return stack.enter_context(nc.sbuf_tensor(f"{name}_{names[0]}", shape, dtype))

        phases, flat = plan_units(w)

        ring = sbuf(ctx, "ring", [P, SLOTS, KT, COLS])
        w_hi = sbuf(ctx, "w_hi", [P, 2, KT, COLS], F32R)
        w_lo = sbuf(ctx, "w_lo", [P, 2, KT, COLS], F32R)
        hT = sbuf(ctx, "hT", [P, DB, LEN])
        xT = hT[:, :, META:LEN]
        cols = sbuf(ctx, "cols", [P, 4 * P])
        const = sbuf(ctx, "const", [P, CONST_COLS])
        ones = sbuf(ctx, "ones", [P, P])
        eps = sbuf(ctx, "eps", [P, 1])
        mods = sbuf(ctx, "mods", [P, P])
        c_silu = sbuf(ctx, "c_silu", [P, DB])
        mod_room = sbuf(ctx, "mod_room", [P, 2, COLS])
        mod_acc, mod_sum = mod_room[:, 0], mod_room[:, 1]
        rms = sbuf(ctx, "rms", [P, LEN])
        PS = ctx.enter_context(nc.psum_tensor("PS", [P, 8, 512], F32))

        unit_loaded = [sem(f"unit_loaded{i}") for i in range(SLOTS)]
        slot_read = [sem(f"slot_read{i}") for i in range(SLOTS)]
        hi_ready = [sem(f"hi_ready{i}") for i in range(4)]
        parts_read = [sem(f"parts_read{i}") for i in range(4)]
        mod_step = sem("mod_step")
        mod_reduced = sem("mod_reduced")
        mod_seen = sem("mod_seen")
        mod_kept = sem("mod_kept")
        banks_free = [sem(f"banks_free{i}") for i in range(2)]
        freed = [0, 0]
        vec = Step(sem("vector_step"))
        act = Step(sem("scalar_step"))
        ten = Step(sem("tensor_step"))
        pool = Step(sem("pool_step"))
        small_loaded = sem("small_loaded")
        small = [0]
        stored = sem("stored")

        def const_of(name):
            first, n = CONST[name]
            return const[:, first:first + n]

        ident, after = const_of("identity"), const_of("after")

        def col(name, i, n=1):
            tile, row, rows = VECTOR_ROWS[name]
            assert i + n <= rows
            return cols[:, tile * P + row + i:tile * P + row + i + n]

        def load_small(eng, dst, src):
            small[0] += 16
            eng.dma_start(dst, src).then_inc(small_loaded, 16)

        def load_unit(sp, n):
            source, it, j = flat[n]
            if n >= SLOTS:
                sp.wait_ge(slot_read[n % SLOTS], 2 * (n // SLOTS))
            src = source(it, j)
            sp.dma_start(ring[:, n % SLOTS, :, 0:src.shape[2]], src).then_inc(unit_loaded[n % SLOTS], 16)

        def stream(sp, ph):
            first = ph.base + SLOTS
            if ph.iters > 1:
                for n in range(first, ph.base + ph.raw):
                    load_unit(sp, n)
                with sp.Fori(1, ph.iters) as it:
                    for r in range(ph.raw):
                        s = ph.slot_at(r)
                        sp.wait_ge(slot_read[s], 2 * ph.uses_at(it, r) - 2)
                        sp.dma_start(ring[:, s], plan_units.round_unit(ph, it, r)).then_inc(unit_loaded[s], 16)
                first = ph.end
            for n in range(first, min(ph.end + SLOTS, len(flat))):
                load_unit(sp, n)

        def split_hi(a, ph, it, j):
            slot, b = ph.slot(j), j % 2
            a.wait_ge(unit_loaded[slot], 16 * ph.uses(it, j))
            for half in range(2):
                if not isinstance(it, int) or ph.fills(it, j) > 1:
                    a.wait_ge(parts_read[2 * b + half], ph.fills(it, j) - 1)
                k = slice(half * KT // 2, (half + 1) * KT // 2)
                nc.scalar.copy(w_hi[:, b, k], ring[:, slot, k]).then_inc(hi_ready[2 * b + half], 1)

        def split_lo(dve, ph, it, j):
            slot, b = ph.slot(j), j % 2
            for half in range(2):
                dve.wait_ge(hi_ready[2 * b + half], ph.fills(it, j))
                k = slice(half * KT // 2, (half + 1) * KT // 2)
                nc.vector.tensor_tensor(w_lo[:, b, k], ring[:, slot, k], w_hi[:, b, k].bitcast(F32), ALU.subtract).then_inc(slot_read[slot], 1)

        def wait_parts(pe, ph, it, j, kt):
            if kt % 2 == 0:
                pe.wait_ge(slot_read[ph.slot(j)], 2 * ph.uses(it, j) - 1 + kt // 2)

        def release_parts(mm, j, kt):
            if kt % 2 == 1:
                mm.then_inc(parts_read[2 * (j % 2) + kt // 2], 1)

        def prime(ph):
            with nc.Block() as block:
                @block.scalar
                def _(a):
                    for j in range(2):
                        split_hi(a, ph, 0, j)

                @block.vector
                def _(dve):
                    for j in range(2):
                        split_lo(dve, ph, 0, j)

        def mod_unit(dve, ph, it, i):
            r = 3 * i + 2
            slot = ph.slot_at(r)
            done = 16 * (it + ph.extra)
            dve.wait_ge(unit_loaded[slot], 16 * ph.uses_at(it, r))
            for kt in range(KT):
                k = i * KT + kt
                if k == 0:
                    if ph.extra > 0:
                        dve.wait_ge(mod_reduced, it + ph.extra)
                    last = nc.vector.tensor_scalar(mod_acc, ring[:, slot, kt], c_silu[:, k:k + 1], None, ALU.mult)
                else:
                    dve.wait_ge(mod_step, done + k)
                    last = nc.vector.scalar_tensor_tensor(mod_acc, ring[:, slot, kt], c_silu[:, k:k + 1], mod_acc,
                                                          ALU.mult, ALU.add)
                last.then_inc(mod_step, 1)
            dve.wait_ge(mod_step, done + (i + 1) * KT)
            dve.sem_inc(slot_read[slot], 2)

        def mod_reduce(g, ph, it):
            m = it + ph.extra
            g.wait_ge(mod_step, 16 * m + 16)
            if ph.extra > 0:
                g.wait_ge(mod_kept, 3 * m)
            g.sem_inc(mod_seen, 1)
            nc.gpsimd.partition_all_reduce(mod_sum, mod_acc, P, bass.bass_isa.ReduceOp.add).then_inc(mod_reduced, 1)

        def mod_keep(dve, ph, it):
            m = it + ph.extra
            dve.wait_ge(mod_reduced, m + 1)
            picked = mod_sum.rearrange("p (i c) -> p i c", i=MB)
            nc.vector.tensor_tensor(picked, picked, ident.unsqueeze(1).to_broadcast([P, MB, P]), ALU.mult).then_inc(mod_kept, 1)
            dve.wait_ge(mod_kept, 3 * m + 1)
            part = mods[:, m * MB:(m + 1) * MB] if isinstance(m, int) else mods[:, bass.ds(m * MB, MB)]
            nc.vector.reduce_sum(part, picked, AX).then_inc(mod_kept, 1)
            dve.wait_ge(mod_kept, 3 * m + 2)
            bias = cols[:, P + m * MB:P + (m + 1) * MB] if isinstance(m, int) else cols[:, bass.ds(m * MB + P, MB)]
            nc.vector.tensor_tensor(part, part, bias, ALU.add).then_inc(mod_kept, 1)

        def modulation_part(dve, ph, it, j):
            if ph.extra is not None and j % 2 == 0:
                mod_unit(dve, ph, it, j // 2 - 1)
            if ph.extra is not None and j == ph.upi + 1:
                mod_keep(dve, ph, it)

        def three_products(dst, b, kt, cols_of, x, start, stop):
            for i, (part, xi) in enumerate(((w_hi, 0), (w_hi, 1), (w_lo, 0))):
                mm = nc.tensor.matmul(dst, part[:, b, kt, cols_of], x[:, xi], start=(start and i == 0),
                                      stop=(stop and i == 2), skip_group_check=True)
            return mm

        def multiply(pe, ph, it, k_units, moving, free_per_slab, slabs):
            for s in range(slabs):
                half = s % 2
                need = freed[half] + free_per_slab * (it * (slabs // 2) + s // 2)
                if not isinstance(it, int) or need > 0:
                    pe.wait_ge(banks_free[half], need)
                for ku in range(k_units):
                    j = s * k_units + ku
                    for kt in range(KT):
                        wait_parts(pe, ph, it, j, kt)
                        x = moving(ku * KT + kt)
                        for m in range(MB):
                            mm = three_products(PS[:, 4 * half + m, 0:x.shape[2]], j % 2, kt, slice(m * P, (m + 1) * P), x,
                                                ku == 0 and kt == 0, ku == k_units - 1 and kt == KT - 1)
                        release_parts(mm, j, kt)

        def wait_slab(eng, ph, it, s, k_units):
            j = (s + 1) * k_units - 1
            eng.wait_ge(parts_read[2 * (j % 2) + 1], ph.fills(it, j))

        def rounds(eng, ph, body, static=False):
            if ph.iters == 1 or static:
                for it in range(ph.iters):
                    body(it)
            else:
                with eng.Fori(0, ph.iters) as it:
                    body(it)

        def split_round(eng, split, ph, it, k_units, evacuate, last, between=None):
            for j in range(2, ph.upi + 2):
                if between is not None:
                    between(it, j)
                if j < ph.upi or not last:
                    split(eng, ph, it, j)
                if (j - 1) % k_units == 0 and evacuate is not None:
                    evacuate(it, (j - 1) // k_units - 1)

        def project(name, k_units, moving, width, on_vector, slabs=2, static=False, follows=True):
            ph = phases[name]

            def ends(it):
                return not follows and it == ph.iters - 1

            with nc.Block() as block:
                @block.sync
                def _(sp):
                    stream(sp, ph)

                @block.tensor
                def _(pe):
                    rounds(pe, ph, lambda it: multiply(pe, ph, it, k_units, moving, 1, slabs), static)

                @block.scalar
                def _(a):
                    rounds(a, ph, lambda it: split_round(a, split_hi, ph, it, k_units, None, ends(it)), static)

                @block.vector
                def _(dve):
                    def evacuate(it, s):
                        wait_slab(dve, ph, it, s, k_units)
                        half = s % 2
                        on_vector(it, s, PS[:, 4 * half:4 * half + 4, 0:width]).then_inc(banks_free[half], 1)

                    def between(it, j):
                        modulation_part(dve, ph, it, j)

                    def body(it):
                        split_round(dve, split_lo, ph, it, k_units, evacuate, ends(it), between)
                    rounds(dve, ph, body, static)

                if ph.extra is not None:
                    @block.gpsimd
                    def _(g):
                        rounds(g, ph, lambda it: mod_reduce(g, ph, it), static)
            for half in range(2):
                freed[half] += ph.iters * slabs // 2

        def project_pair(name, k_units, moving, on_scalar, on_vector, slabs=2, on_pool=None):
            ph = phases[name]
            ready, taken = sem(f"{name}_ready"), sem(f"{name}_taken")
            with nc.Block() as block:
                @block.sync
                def _(sp):
                    stream(sp, ph)

                @block.tensor
                def _(pe):
                    rounds(pe, ph, lambda it: multiply(pe, ph, it, k_units, moving, 1, slabs))

                @block.scalar
                def _(a):
                    a.sem_inc(taken, 1)
                    def evacuate(it, s):
                        wait_slab(a, ph, it, s, k_units)
                        on_scalar(a, it, s, ready, taken)
                    rounds(a, ph, lambda it: split_round(a, split_hi, ph, it, k_units, evacuate, False))

                @block.vector
                def _(dve):
                    def evacuate(it, s):
                        wait_slab(dve, ph, it, s, k_units)
                        on_vector(dve, it, s, ready, taken)

                    def between(it, j):
                        modulation_part(dve, ph, it, j)

                    def body(it):
                        split_round(dve, split_lo, ph, it, k_units, evacuate, False, between)
                    rounds(dve, ph, body)

                @block.gpsimd
                def _(g):
                    def body(it):
                        if ph.extra is not None:
                            mod_reduce(g, ph, it)
                        if on_pool is not None:
                            on_pool(g, it, taken)
                    if on_pool is not None or ph.extra is not None:
                        rounds(g, ph, body)
            for half in range(2):
                freed[half] += ph.iters * slabs // 2

        def values_by_token(ph, block, x, v):
            @block.tensor
            def _(pe):
                with pe.Fori(0, ph.iters) as it:
                    for s in range(2):
                        pe.wait_ge(banks_free[s], freed[s] + it)
                        for ku in range(4):
                            j = 4 * s + ku
                            for kt in range(KT):
                                wait_parts(pe, ph, it, j, kt)
                                k = ku * KT + kt
                                for t in range(2):
                                    for i, (xi, part) in enumerate(((0, w_hi), (0, w_lo), (1, w_hi))):
                                        mm = nc.tensor.matmul(PS[:, 4 * s + t, :], x[:, k, xi, t * P:(t + 1) * P], part[:, j % 2, kt],
                                                              start=(k == 0 and i == 0), stop=(k == DB - 1 and i == 2))
                                release_parts(mm, j, kt)

            @block.scalar
            def _(a):
                with a.Fori(0, ph.iters) as it:
                    def evacuate(it, s):
                        wait_slab(a, ph, it, s, 4)
                        nc.scalar.copy(v[:, :, bass.ds(it * 2 * COLS + s * COLS, COLS)], PS[:, 4 * s:4 * s + 2, :]).then_inc(banks_free[s], 1)
                    split_round(a, split_hi, ph, it, 4, evacuate, False)

        def inverse_rms(src, blocks, width, squares):
            with nc.Block() as block:
                squared, summed = act.value + 2, ten.value + 1
                half = (blocks + 1) // 2

                @block.scalar
                def _(a):
                    for k0 in (0, half):
                        act.tick(nc.scalar.activation(squares[:, k0:k0 + half, 0:width], src[:, k0:k0 + half], ACT.Square))
                    a.wait_ge(ten.sem, summed)
                    act.tick(nc.scalar.activation(rms[:, 0:width], PS[:, 0, 0:width], ACT.Sqrt,
                                                  scale=1.0 / (blocks * P), bias=eps[:, 0:1]))

                @block.tensor
                def _(pe):
                    for k in range(blocks):
                        pe.wait_ge(act.sem, squared - 1 if k < half else squared)
                        mm = nc.tensor.matmul(PS[:, 0, 0:width], ones[:], squares[:, k, 0:width],
                                              start=(k == 0), stop=(k == blocks - 1))
                    ten.tick(mm)

                @block.vector
                def _(dve):
                    dve.wait_ge(act.sem, squared + 1)
                    vec.tick(nc.vector.reciprocal(rms[:, 0:width], rms[:, 0:width]))

        def scale_tokens(dst, src, blocks, width, gain):
            with nc.Block() as block:
                @block.vector
                def _(dve):
                    for k in range(blocks):
                        vec.tick(nc.vector.scalar_tensor_tensor(dst[:, k], src[:, k], gain[:, k:k + 1], rms[:, 0:width],
                                                                ALU.mult, ALU.mult))

        def scale_and_split(dst, src, blocks, width, gain, shift=None):
            with ExitStack() as scope:
                whole = sbuf(scope, "whole", [P, 2, MB, width])
                with nc.Block() as block:
                    v0, a0, g0 = vec.value, act.value, pool.value
                    per = MB + (1 if shift is not None else 0)

                    @block.vector
                    def _(dve):
                        for q in range(blocks // MB):
                            if q >= 2:
                                dve.wait_ge(pool.sem, g0 + q - 1)
                            for i in range(MB):
                                k = q * MB + i
                                n = vec.tick(nc.vector.scalar_tensor_tensor(whole[:, q % 2, i], src[:, k], gain[:, k:k + 1],
                                                                            rms[:, 0:width], ALU.mult, ALU.mult))
                            if shift is not None:
                                dve.wait_ge(vec.sem, n)
                                vec.tick(nc.vector.tensor_tensor(
                                    whole[:, q % 2], whole[:, q % 2],
                                    shift[:, q * MB:(q + 1) * MB].unsqueeze(2).to_broadcast([P, MB, width]), ALU.add))

                    @block.scalar
                    def _(a):
                        for q in range(blocks // MB):
                            a.wait_ge(vec.sem, v0 + per * (q + 1))
                            act.tick(nc.scalar.copy(dst[:, q * MB:(q + 1) * MB, 0], whole[:, q % 2]))

                    @block.gpsimd
                    def _(g):
                        for q in range(blocks // MB):
                            g.wait_ge(act.sem, a0 + q + 1)
                            part = dst[:, q * MB:(q + 1) * MB]
                            pool.tick(nc.gpsimd.tensor_tensor(part[:, :, 1], whole[:, q % 2], part[:, :, 0].bitcast(F32), ALU.subtract))

        def split_blocks(groups):
            with nc.Block() as block:
                a0 = act.value

                @block.scalar
                def _(a):
                    for hi, lo, src in groups:
                        act.tick(nc.scalar.copy(hi, src))

                @block.vector
                def _(dve):
                    for n, (hi, lo, src) in enumerate(groups):
                        if n % 3 != 1:
                            dve.wait_ge(act.sem, a0 + n + 1)
                            vec.tick(nc.vector.tensor_tensor(lo, src, hi.bitcast(F32), ALU.subtract))

                @block.gpsimd
                def _(g):
                    for n, (hi, lo, src) in enumerate(groups):
                        if n % 3 == 1:
                            g.wait_ge(act.sem, a0 + n + 1)
                            pool.tick(nc.gpsimd.tensor_tensor(lo, src, hi.bitcast(F32), ALU.subtract))

        def split_activations(dst, src, blocks, step=2):
            split_blocks([(dst[:, k:k + step, 0], dst[:, k:k + step, 1], src[:, k:k + step]) for k in range(0, blocks, step)])

        def small_ops(ops):
            with nc.Block() as block:
                @block.vector
                def _(dve):
                    for op in ops:
                        dve.wait_ge(vec.sem, vec.tick(op()))

        def attention(name, heads, scores_of, keys_of, bias_of, scale, v, o):
            items = 2 * heads
            TURN, VALUE, KEEP = 2, 3, 4
            scored, turned, valued = (sem(f"{name}_{x}") for x in ("scored", "turned", "valued"))
            biased, shifted, exped, normed = (sem(f"{name}_{x}") for x in ("biased", "shifted", "exped", "normed"))
            copied, kept, dve_step = (sem(f"{name}_{x}") for x in ("copied", "kept", "maxed"))
            with ExitStack() as scope:
                S = sbuf(scope, "S", [P, 2, LEN])
                Pr = sbuf(scope, "Pr", [P, 3, LEN])
                PT = sbuf(scope, "PT", [P, 2, 3, P])
                mx = sbuf(scope, "mx", [P, 3, 4])
                with nc.Block() as block:
                    @block.tensor
                    def _(pe):
                        for n in range(items + VALUE):
                            if n < items:
                                if n >= 3:
                                    pe.wait_ge(biased, n - 2)
                                pairs = scores_of(n)
                                for i, (lhsT, rhs) in enumerate(pairs):
                                    mm = nc.tensor.matmul(PS[:, n % 3, 0:keys_of(n)], lhsT, rhs,
                                                          start=(i == 0), stop=(i == len(pairs) - 1))
                                mm.then_inc(scored, 1)
                            t = n - TURN
                            if 0 <= t < items:
                                pe.wait_ge(normed, t + 1)
                                if t >= 2:
                                    pe.wait_ge(copied, t - 1)
                                for k0 in range(0, keys_of(t), P):
                                    kn = min(P, keys_of(t) - k0)
                                    mm = nc.tensor.transpose(PS[0:kn, 3 + t % 2, k0:k0 + P], Pr[:, t % 3, k0:k0 + kn], ident)
                                mm.then_inc(turned, 1)
                            r = n - VALUE
                            if 0 <= r < items:
                                pe.wait_ge(copied, r + 1)
                                if r >= 2:
                                    pe.wait_ge(kept, r - 1)
                                kts = -(-keys_of(r) // P)
                                for kt in range(kts):
                                    kn = min(P, keys_of(r) - kt * P)
                                    mm = nc.tensor.matmul(PS[:, 5 + r % 2, 0:P], v[0:kn, kt, (r // 2) * P:(r // 2 + 1) * P],
                                                          PT[0:kn, r % 2, kt], start=(kt == 0), stop=(kt == kts - 1))
                                mm.then_inc(valued, 1)

                    @block.vector
                    def _(dve):
                        chain = 0
                        for n in range(items + KEEP):
                            if n < items:
                                nk, b = keys_of(n), n % 2
                                dve.wait_ge(scored, n + 1)
                                if n >= 2:
                                    dve.wait_ge(exped, n - 1)
                                if n >= 3:
                                    dve.wait_ge(normed, n - 2)
                                nc.vector.scalar_tensor_tensor(S[:, b, 0:nk], PS[:, n % 3, 0:nk], scale, bias_of(n),
                                                               ALU.mult, ALU.add).then_inc(biased, 1)
                                dve.wait_ge(biased, n + 1)
                                nc.vector.reduce_max(mx[:, n % 3, 0:1], S[:, b, 0:nk], AX).then_inc(dve_step, 1)
                                chain += 1
                                dve.wait_ge(dve_step, chain)
                                nc.vector.tensor_scalar(mx[:, n % 3, 1:2], mx[:, n % 3, 0:1], -1.0, None, ALU.mult).then_inc(shifted, 1)
                            t = n - 1
                            if 0 <= t < items:
                                nk, b = keys_of(t), t % 3
                                dve.wait_ge(exped, t + 1)
                                nc.vector.reciprocal(mx[:, b, 3:4], mx[:, b, 2:3]).then_inc(dve_step, 1)
                                chain += 1
                                dve.wait_ge(dve_step, chain)
                                nc.vector.tensor_scalar(Pr[:, b, 0:nk], Pr[:, b, 0:nk], mx[:, b, 3:4], None,
                                                        ALU.mult).then_inc(normed, 1)
                            r = n - KEEP
                            if 0 <= r < items:
                                dve.wait_ge(valued, r + 1)
                                nc.vector.tensor_copy(o[:, r // 2, (r % 2) * P:(r % 2 + 1) * P],
                                                      PS[:, 5 + r % 2, 0:P]).then_inc(kept, 1)

                    @block.scalar
                    def _(a):
                        for n in range(items + TURN):
                            if n < items:
                                nk, b = keys_of(n), n % 3
                                a.wait_ge(shifted, n + 1)
                                if n >= 3:
                                    a.wait_ge(turned, n - 2)
                                nc.scalar.activation(Pr[:, b, 0:nk], S[:, n % 2, 0:nk], ACT.Exp, bias=mx[:, b, 1:2],
                                                     accum_out=mx[:, b, 2:3]).then_inc(exped, 1)
                            t = n - TURN
                            if 0 <= t < items:
                                a.wait_ge(turned, t + 1)
                                if t >= 2:
                                    a.wait_ge(valued, t - 1)
                                nk, b = keys_of(t), t % 2
                                full, rest = nk // P, nk % P
                                last = nc.scalar.copy(PT[:, b, 0:full], PS[:, 3 + b, 0:full * P].rearrange("p (k q) -> p k q", q=P))
                                if rest:
                                    last = nc.scalar.copy(PT[0:rest, b, full], PS[0:rest, 3 + b, full * P:(full + 1) * P])
                                last.then_inc(copied, 1)

        with ExitStack() as scope:
            x_rows = sbuf(scope, "x_rows", [P, 2, D])
            meta_rows = sbuf(scope, "meta_rows", [META, D])
            vec_rows = sbuf(scope, "vec_rows", [P, 4, P])
            with nc.Block() as block:
                turned, copied = sem("input_turned"), sem("input_copied")

                @block.sync
                def _(sp):
                    load_small(sp, const[:], w["shape_constants"])
                    for name, (tile, row, rows) in VECTOR_ROWS.items():
                        load_small(sp, vec_rows[row:row + rows, tile], w[name + "_rows"])
                    load_small(sp, x_rows[:], w["x"].rearrange("(t p) d -> p t d", p=P))
                    load_small(sp, meta_rows[:], w["meta_tokens"])
                    for n in range(SLOTS):
                        load_unit(sp, n)

                @block.gpsimd
                def _(g):
                    nc.gpsimd.memset(ones[:], 1.0)
                    nc.gpsimd.memset(eps[:], EPS)

                @block.scalar
                def _(a):
                    a.wait_ge(copied, 1)
                    n = act.tick(nc.scalar.activation(c_silu[:], col("c_2", 0, DB), ACT.Sigmoid))

                groups = [("vector", None)] + [("x", i) for i in range(8)] + [("meta", None)]
                n_small = 16 * (3 + len(VECTOR_ROWS))

                @block.tensor
                def _(pe):
                    pe.wait_ge(small_loaded, n_small)
                    for n, (kind, i) in enumerate(groups):
                        if n >= 4:
                            pe.wait_ge(copied, n - 3)
                        if kind == "vector":
                            for t in range(4):
                                r = VECTOR_TILE_ROWS[t]
                                mm = nc.tensor.transpose(PS[:, 0, t * P:t * P + r], vec_rows[0:r, t], ident[0:r, 0:r])
                        elif kind == "x":
                            for q in range(4):
                                k = (i % 4) * 4 + q
                                mm = nc.tensor.transpose(PS[:, n % 4, q * P:(q + 1) * P],
                                                         x_rows[:, i // 4, k * P:(k + 1) * P], ident)
                        else:
                            for k in range(DB):
                                mm = nc.tensor.transpose(PS[:, n % 4, k * META:(k + 1) * META],
                                                         meta_rows[:, k * P:(k + 1) * P], ident[0:META, 0:META])
                        mm.then_inc(turned, 1)

                @block.vector
                def _(dve):
                    for n, (kind, i) in enumerate(groups):
                        dve.wait_ge(turned, n + 1)
                        if kind == "vector":
                            nc.vector.tensor_copy(cols[:, 0:480], PS[:, 0, 0:480]).then_inc(copied, 1)
                        elif kind == "x":
                            nc.vector.tensor_copy(
                                hT[:, (i % 4) * 4:(i % 4) * 4 + 4, META + (i // 4) * P:META + (i // 4 + 1) * P],
                                PS[:, n % 4, :].rearrange("p (k t) -> p k t", k=4)).then_inc(copied, 1)
                        else:
                            nc.vector.tensor_copy(hT[:, :, 0:META],
                                                  PS[:, n % 4, 0:DB * META].rearrange("p (k t) -> p k t", k=DB)).then_inc(copied, 1)

        small_ops([lambda: nc.vector.tensor_tensor(c_silu[:], c_silu[:], col("c_2", 0, DB), ALU.mult)])
        prime(phases["latents"])

        with ExitStack() as one:
            const_one = sbuf(one, "const_one", [P, 3 * LEN])
            cosT, sinT, causal = (const_one[:, first:first + n] for first, n in CONST_ONE.values())
            kT = sbuf(one, "kT", [P, HEADS, LEN])
            attn_out = kT[:, :, 0:SEQ]
            uT = sbuf(one, "uT", [P, SSM_W // P, LEN])
            with ExitStack() as scope:
                latent = sbuf(scope, "latent", [P, 8, LEN])
                k_rope = sbuf(scope, "k_rope", [P, LEN])
                qT = sbuf(scope, "qT", [P, HEADS, SEQ])
                swapped = sbuf(scope, "swapped", [P, 2, LEN])
                with nc.Block() as block:
                    @block.sync
                    def _(sp):
                        load_small(sp, const_one[:], w["shape_constants_one"])
                        sp.wait_ge(small_loaded, small[0])

                def rotate(dve, dst, ps, first, width):
                    for q, r in ((0, 1), (1, 0), (2, 3), (3, 2)):
                        last = nc.vector.tensor_copy(swapped[32 * q:32 * q + 32, 0, 0:width], ps[32 * r:32 * r + 32])
                        vec.tick(last)
                    dve.wait_ge(vec.sem, vec.value)
                    vec.tick(nc.vector.tensor_tensor(swapped[:, 0, 0:width], swapped[:, 0, 0:width],
                                                     sinT[:, first:first + width], ALU.mult))
                    last = nc.vector.tensor_tensor(swapped[:, 1, 0:width], ps, cosT[:, first:first + width], ALU.mult)
                    dve.wait_ge(vec.sem, vec.tick(last))
                    last = nc.vector.tensor_tensor(dst, swapped[:, 0, 0:width], swapped[:, 1, 0:width], ALU.add)
                    dve.wait_ge(vec.sem, vec.tick(last))

                with ExitStack() as normed:
                    nT = sbuf(normed, "nT", [P, DB, 2, LEN], F32R)
                    w_kr = sbuf(normed, "w_kr", [P, DB, 2, ROPE])
                    inverse_rms(hT, DB, LEN, kT)
                    scale_and_split(nT, hT, DB, LEN, col("norm_mix", 0, DB))
                    project("latents", 4, lambda k: nT[:, k], LEN,
                            lambda it, s, ps: nc.vector.tensor_copy(latent[:, 4 * s:4 * s + 4], ps))
                    project("u", 4, lambda k: nT[:, k], LEN,
                            lambda it, s, ps: nc.vector.tensor_copy(uT[:, 4 * s:4 * s + 4], ps), follows=False)

                    with nc.Block() as block:
                        kr_done = ten.value + 1
                        kr_loaded = small[0] + 32

                        @block.sync
                        def _(sp):
                            for half in range(2):
                                load_small(sp, w_kr[:, :, half], w["w_in"][:, OFF_KR:OFF_U].rearrange("(k p) n -> p k n", p=P))

                        @block.tensor
                        def _(pe):
                            pe.wait_ge(small_loaded, kr_loaded)
                            for k in range(DB):
                                for part in range(2):
                                    mm = nc.tensor.matmul(PS[:, 0, 0:LEN], w_kr[:, k].rearrange("p a b -> p (a b)"),
                                                          nT[:, k, part].bitcast(F32), start=(k == 0 and part == 0),
                                                          stop=(k == DB - 1 and part == 1))
                            ten.tick(mm)

                        @block.vector
                        def _(dve):
                            dve.wait_ge(ten.sem, kr_done)
                            rotate(dve, k_rope[:], PS[:, 0, 0:LEN], 0, LEN)

                heads_done = scope.enter_context(ExitStack())
                q_rope = sbuf(heads_done, "q_rope", [P, HEADS // 2, SEQ])
                for part, gain in ((latent[:, 0:4], "norm_q"), (latent[:, 4:8], "norm_kv")):
                    inverse_rms(part, 4, LEN, kT)
                    scale_tokens(part, part, 4, LEN, col(gain, 0, 4))

                ph = phases["q_up"]
                with nc.Block() as block:
                    q_free, q_rope_free = sem("q_free"), sem("q_rope_free")

                    @block.sync
                    def _(sp):
                        stream(sp, ph)

                    @block.tensor
                    def _(pe):
                        for j in range(8):
                            slot, half = ph.slot(j), j % 2
                            if j >= 2:
                                pe.wait_ge(q_free, j - 1)
                                pe.wait_ge(q_rope_free, j - 1)
                            pe.wait_ge(unit_loaded[slot], 16 * ph.uses(0, j))
                            for m in range(3):
                                for kt in range(KT):
                                    mm = nc.tensor.matmul(PS[:, 4 * half + m, 0:SEQ], ring[:, slot, kt, m * P:(m + 1) * P],
                                                          latent[:, kt, META:LEN],
                                                          start=(kt == 0), stop=(kt == KT - 1))
                            mm.then_inc(slot_read[slot], 2)

                    @block.scalar
                    def _(a):
                        for j in range(8):
                            half = j % 2
                            a.wait_ge(slot_read[ph.slot(j)], 2 * ph.uses(0, j))
                            nc.scalar.copy(qT[:, 2 * j:2 * j + 2], PS[:, 4 * half:4 * half + 2, 0:SEQ]).then_inc(q_free, 1)

                    @block.vector
                    def _(dve):
                        for j in range(8):
                            half = j % 2
                            dve.wait_ge(slot_read[ph.slot(j)], 2 * ph.uses(0, j))
                            rotate(dve, q_rope[:, j], PS[:, 4 * half + 2, 0:SEQ], META, SEQ)
                            dve.sem_inc(q_rope_free, 1)

                v = sbuf(heads_done, "v", [P, 3, D])
                ph_kv = phases["kv_up"]
                with nc.Block() as block:
                    k_free, v_free = sem("k_free"), sem("v_free")
                    token_tiles = ((0, P), (P, P), (2 * P, META))

                    @block.sync
                    def _(sp):
                        stream(sp, ph_kv)

                    @block.tensor
                    def _(pe):
                        for j in range(8):
                            slot, half = ph_kv.slot(j), j % 2
                            if j >= 2:
                                pe.wait_ge(k_free, j - 1)
                                pe.wait_ge(v_free, j - 1)
                            pe.wait_ge(unit_loaded[slot], 16 * ph_kv.uses(0, j))
                            pairs = ring[:, slot].rearrange("p k (h c) -> p k h c", h=2)
                            for m in range(2):
                                for kt in range(KT):
                                    nc.tensor.matmul(PS[:, 4 * half + m, 0:LEN], pairs[:, kt, m, 0:NOPE], latent[:, 4 + kt],
                                                     start=(kt == 0), stop=(kt == KT - 1))
                            for t, (t0, tn) in enumerate(token_tiles):
                                dst = PS[0:tn, 4 * half + 2 + t // 2, (t % 2) * 256:(t % 2) * 256 + 256]
                                for kt in range(KT):
                                    mm = nc.tensor.matmul(dst, latent[:, 4 + kt, t0:t0 + tn], pairs[:, kt, :, NOPE:],
                                                          start=(kt == 0), stop=(kt == KT - 1))
                            mm.then_inc(slot_read[slot], 2)

                    @block.scalar
                    def _(a):
                        for j in range(8):
                            half = j % 2
                            a.wait_ge(slot_read[ph_kv.slot(j)], 2 * ph_kv.uses(0, j))
                            nc.scalar.copy(kT[:, 2 * j:2 * j + 2], PS[:, 4 * half:4 * half + 2, 0:LEN]).then_inc(k_free, 1)

                    @block.vector
                    def _(dve):
                        for j in range(8):
                            half = j % 2
                            dve.wait_ge(slot_read[ph_kv.slot(j)], 2 * ph_kv.uses(0, j))
                            nc.vector.tensor_copy(v[0:META, 2, j * 256:(j + 1) * 256], PS[0:META, 4 * half + 3, 0:256])
                            nc.vector.tensor_copy(v[:, 0:2, j * 256:(j + 1) * 256],
                                                  PS[:, 4 * half + 2, :].rearrange("p (t c) -> p t c", t=2)).then_inc(v_free, 1)

                def mla_keys(n):
                    return META + P * (n % 2 + 1)

                def mla_scores(n):
                    h, b = n // 2, n % 2
                    r = 64 * (h % 2)
                    nk = mla_keys(n)
                    return [(qT[:, h, b * P:(b + 1) * P], kT[:, h, 0:nk]),
                            (q_rope[r:r + 64, h // 2, b * P:(b + 1) * P], k_rope[r:r + 64, 0:nk])]

                attention("mla", HEADS, mla_scores, mla_keys, lambda n: causal[:, LEN - mla_keys(n):LEN],
                          (NOPE + ROPE) ** -0.5, v, qT)
                heads_done.close()
                prime(phases["attn_proj"])
                o_parts = sbuf(scope, "o_parts", [P, HEADS, 2, SEQ], F32R)
                split_activations(o_parts, qT, HEADS)
                project("attn_proj", 4, lambda k: o_parts[:, k], SEQ,
                        lambda it, s, ps: nc.vector.tensor_copy(attn_out[:, bass.ds(it * 8 + 4 * s, 4)], ps))

            TILES = G // 2
            UB = SSM_W // P
            with ExitStack() as scope:
                y = uT[:, :, META:LEN]
                BT = sbuf(scope, "BT", [P, UB, 2, P])
                CT = sbuf(scope, "CT", [P, UB, 2, P])
                mag = sbuf(scope, "mag", [P, TILES])
                powers = sbuf(scope, "powers", [P, 2, 9, TILES])
                with ExitStack() as prep:
                    row = sbuf(prep, "row", [TILES, 16, P])
                    steps = sbuf(prep, "steps", [TILES, 2])
                    turns = sbuf(prep, "turns", [TILES, P], I32)
                    b_in = sbuf(prep, "b_in", [P, 2, TILES, C])
                    c_in = sbuf(prep, "c_in", [P, 2, UB, P])
                    coef = sbuf(prep, "coef", [P, 2, TILES])
                    prod = sbuf(prep, "prod", [P, 4, TILES, C])
                    b_pad = sbuf(prep, "b_pad", [P, 2, TILES, 2 * C])
                    LR, LI, ST, ANG, MAG, SIN, COS, NR, T0, T1, DEN, CR, CI, HALF = range(14)
                    halfpi = 1.5707963267948966
                    two_pi_hi, two_pi_lo = 6.28125, 0.0019353071795864769
                    with nc.Block() as block:
                        base = small[0]
                        c_loaded = sem("ssm_c_loaded")
                        zeroed = pool.value + 2

                        @block.gpsimd
                        def _(g):
                            pool.tick(nc.gpsimd.memset(c_in[:], 0.0))
                            pool.tick(nc.gpsimd.memset(b_pad[:], 0.0))

                        @block.sync
                        def _(sp):
                            load_small(sp, row[:, LR], w["ssm_lambda_re"].rearrange("(r c) n -> r (c n)", c=2))
                            load_small(sp, row[:, LI], w["ssm_lambda_im"].rearrange("(r c) n -> r (c n)", c=2))
                            load_small(sp, steps[:], w["ssm_log_step"].rearrange("(r c) -> r c", c=2))
                            for i, name in enumerate(("ssm_b_re", "ssm_b_im")):
                                load_small(sp, b_in[:, i], w[name].rearrange("(t c) n p -> (c n) t p", c=2))
                            sp.wait_ge(pool.sem, zeroed)
                            for i, name in enumerate(("ssm_c_re", "ssm_c_im")):
                                src = w[name].rearrange("(j g) p n -> g p j n", g=8)
                                for g8 in range(8):
                                    sp.dma_start(c_in[16 * g8:16 * g8 + 16, i, :, 64 * (g8 % 2):64 * (g8 % 2) + 64],
                                                 src[g8]).then_inc(c_loaded, 16)
                        in_loaded = base + 16 * 5
                        stepped, phased, ready = sem("ssm_stepped"), sem("ssm_phased"), sem("ssm_ready")
                        turned, copied, padded = sem("ssm_turned"), sem("ssm_copied"), sem("ssm_padded")

                        @block.scalar
                        def _(a):
                            a.wait_ge(small_loaded, in_loaded)
                            nc.scalar.activation(steps[:], steps[:], ACT.Exp).then_inc(stepped, 1)
                            a.wait_ge(phased, 1)
                            act.tick(nc.scalar.activation(row[:, MAG], row[:, T0], ACT.Exp))
                            act.tick(nc.scalar.activation(row[:, SIN], row[:, ANG], ACT.Sin))
                            nc.scalar.activation(row[:, HALF], row[:, ANG], ACT.Sin, scale=0.5).then_inc(stepped, 1)
                            for n in range(8):
                                a.wait_ge(turned, 2 + n)
                                src = PS[:, 1 + n % 2, :]
                                nc.scalar.copy(BT[:, n], src[:, 0:256].rearrange("p (a b) -> p a b", a=2))
                                nc.scalar.copy(CT[:, n, 0], src[:, 256:384])
                                nc.scalar.mul(CT[:, n, 1], src[:, 384:512], -1.0).then_inc(copied, 1)

                        @block.vector
                        def _(dve):
                            def link(instruction):
                                dve.wait_ge(vec.sem, vec.tick(instruction))

                            def tt(o, i0, i1, op):
                                link(nc.vector.tensor_tensor(o, i0, i1, op))

                            dve.wait_ge(stepped, 1)
                            for c2 in range(2):
                                link(nc.vector.tensor_copy(row[:, ST, c2 * N:(c2 + 1) * N], steps[:, c2:c2 + 1].to_broadcast([TILES, N])))
                            tt(row[:, T0], row[:, LR], row[:, ST], ALU.mult)
                            tt(row[:, ANG], row[:, LI], row[:, ST], ALU.mult)
                            link(nc.vector.tensor_scalar(turns[:], row[:, ANG], 1.0 / 6.283185307179586, None, ALU.mult))
                            link(nc.vector.tensor_copy(row[:, T1], turns[:]))
                            for part in (two_pi_hi, two_pi_lo):
                                link(nc.vector.scalar_tensor_tensor(row[:, ANG], row[:, T1], -part, row[:, ANG], ALU.mult, ALU.add))
                            link(nc.vector.tensor_scalar(row[:, T1], row[:, ANG], 3.1415925, 6.283185307179586, ALU.is_gt, ALU.mult))
                            tt(row[:, ANG], row[:, ANG], row[:, T1], ALU.subtract)
                            link(nc.vector.tensor_scalar(row[:, T1], row[:, ANG], -3.1415925, 6.283185307179586, ALU.is_lt, ALU.mult))
                            tt(row[:, ANG], row[:, ANG], row[:, T1], ALU.add)
                            link(nc.vector.tensor_scalar(row[:, ANG], row[:, ANG], 3.1415925, -3.1415925, ALU.min, ALU.max))
                            dve.sem_inc(phased, 1)
                            dve.wait_ge(stepped, 2)
                            tt(row[:, T1], row[:, HALF], row[:, HALF], ALU.mult)
                            link(nc.vector.tensor_scalar(row[:, COS], row[:, T1], -2.0, 1.0, ALU.mult, ALU.add))
                            tt(row[:, T0], row[:, MAG], row[:, COS], ALU.mult)
                            link(nc.vector.tensor_scalar(row[:, NR], row[:, T0], -1.0, None, ALU.add))
                            tt(row[:, T0], row[:, MAG], row[:, SIN], ALU.mult)
                            tt(row[:, T1], row[:, LR], row[:, LR], ALU.mult)
                            tt(row[:, DEN], row[:, LI], row[:, LI], ALU.mult)
                            tt(row[:, DEN], row[:, DEN], row[:, T1], ALU.add)
                            link(nc.vector.reciprocal(row[:, DEN], row[:, DEN]))
                            tt(row[:, CR], row[:, NR], row[:, LR], ALU.mult)
                            tt(row[:, T1], row[:, T0], row[:, LI], ALU.mult)
                            tt(row[:, CR], row[:, CR], row[:, T1], ALU.add)
                            tt(row[:, CR], row[:, CR], row[:, DEN], ALU.mult)
                            tt(row[:, CI], row[:, T0], row[:, LR], ALU.mult)
                            tt(row[:, T1], row[:, NR], row[:, LI], ALU.mult)
                            tt(row[:, CI], row[:, CI], row[:, T1], ALU.subtract)
                            tt(row[:, CI], row[:, CI], row[:, DEN], ALU.mult)
                            dve.sem_inc(ready, 1)
                            dve.wait_ge(turned, 1)
                            vec.tick(nc.vector.tensor_copy(mag[:], PS[:, 0, 0:32]))
                            vec.tick(nc.vector.tensor_copy(powers[:, :, 0], PS[:, 0, 32:96].rearrange("p (a t) -> p a t", a=2)))
                            link(nc.vector.tensor_copy(coef[:], PS[:, 0, 96:160].rearrange("p (a t) -> p a t", a=2)))
                            bc = [coef[:, i].unsqueeze(2).to_broadcast([P, TILES, C]) for i in range(2)]
                            tt(prod[:, 0], b_in[:, 0], bc[0], ALU.mult)
                            tt(prod[:, 1], b_in[:, 1], bc[1], ALU.mult)
                            tt(prod[:, 2], b_in[:, 1], bc[0], ALU.mult)
                            tt(prod[:, 3], b_in[:, 0], bc[1], ALU.mult)
                            dve.wait_ge(pool.sem, zeroed)
                            for hf in range(2):
                                r = slice(64 * hf, 64 * hf + 64)
                                c = slice(C * hf, C * hf + C)
                                vec.tick(nc.vector.tensor_tensor(b_pad[r, 0, :, c], prod[r, 0], prod[r, 1], ALU.subtract))
                                link(nc.vector.tensor_tensor(b_pad[r, 1, :, c], prod[r, 2], prod[r, 3], ALU.add))
                            dve.sem_inc(padded, 1)
                            for k in range(8):
                                re, im = powers[:, 0, k], powers[:, 1, k]
                                re2, im2 = powers[:, 0, k + 1], powers[:, 1, k + 1]
                                t0, t1 = prod[:, 0, :, 0], prod[:, 0, :, 1]
                                tt(t0, re, re, ALU.mult)
                                tt(t1, im, im, ALU.mult)
                                tt(re2, t0, t1, ALU.subtract)
                                tt(t0, re, im, ALU.mult)
                                link(nc.vector.tensor_scalar(im2, t0, 2.0, None, ALU.mult))

                        @block.tensor
                        def _(pe):
                            pe.wait_ge(ready, 1)
                            for i, r in enumerate((MAG, COS, SIN, CR, CI)):
                                mm = nc.tensor.transpose(PS[:, 0, 32 * i:32 * i + 32], row[:, r], ident[0:TILES, 0:TILES])
                            mm.then_inc(turned, 1)
                            pe.wait_ge(padded, 1)
                            pe.wait_ge(c_loaded, 16 * 16)
                            for n in range(8):
                                if n >= 2:
                                    pe.wait_ge(copied, n - 1)
                                for i in range(2):
                                    nc.tensor.transpose(PS[:, 1 + n % 2, i * P:(i + 1) * P],
                                                        b_pad[:, i, 4 * n:4 * n + 4].rearrange("p t c -> p (t c)"), ident)
                                for i in range(2):
                                    mm = nc.tensor.transpose(PS[:, 1 + n % 2, (2 + i) * P:(3 + i) * P], c_in[:, i, n], ident)
                                mm.then_inc(turned, 1)

                with ExitStack() as run:
                    E = sbuf(run, "E", [P, 2, 2, 4, LEN])
                    bu = sbuf(run, "bu", [P, 2, 2, 4, LEN])
                    z = sbuf(run, "z", [P, 2, 4, LEN])
                    xs = sbuf(run, "xs", [P, 2, 4, LEN])
                    tmp = sbuf(run, "tmp", [P, 2, 4, P])
                    driven, drive_copied, tabled, rotated = (sem(f"ssm_{x}") for x in ("driven", "drive_copied", "tabled", "rotated"))
                    stated, summed, ykept, pstep = (sem(f"ssm_{x}") for x in ("stated", "summed", "ykept", "pstep"))
                    with nc.Block() as block:
                        @block.tensor
                        def _(pe):
                            def drive(j):
                                for part in range(2):
                                    n = 2 * j + part
                                    if n >= 1:
                                        pe.wait_ge(drive_copied, n)
                                    for q in range(4):
                                        r = slice(32 * q, 32 * q + 32)
                                        mm = nc.tensor.matmul(PS[:, q, 0:LEN], BT[r, j, part], uT[r, j], start=True, stop=True)
                                    mm.then_inc(driven, 1)

                            drive(0)
                            for j in range(UB):
                                if j + 1 < UB:
                                    drive(j + 1)
                                pe.wait_ge(stated, j + 1)
                                if j >= 2:
                                    pe.wait_ge(ykept, j - 1)
                                for q in range(4):
                                    r = slice(32 * q, 32 * q + 32)
                                    for part in range(2):
                                        mm = nc.tensor.matmul(PS[r, 4 + j % 2, 0:SEQ], CT[:, j, part, r], xs[:, part, q, META:LEN],
                                                              start=(part == 0), stop=(part == 1))
                                mm.then_inc(summed, 1)

                        @block.scalar
                        def _(a):
                            for j in range(UB):
                                for part in range(2):
                                    a.wait_ge(driven, 2 * j + part + 1)
                                    if j >= 2:
                                        a.wait_ge(rotated, j - 1)
                                    nc.scalar.copy(bu[:, j % 2, part], PS[:, 0:4, 0:LEN]).then_inc(drive_copied, 1)

                        @block.gpsimd
                        def _(g):
                            steps_done = 0

                            def link(instruction):
                                nonlocal steps_done
                                steps_done += 1
                                instruction.then_inc(pstep, 1)
                                g.wait_ge(pstep, steps_done)

                            for j in range(UB):
                                if j >= 2:
                                    g.wait_ge(stated, j - 1)
                                e = E[:, j % 2]
                                link(nc.gpsimd.memset(e[:, 0, :, 0:1], 1.0))
                                link(nc.gpsimd.memset(e[:, 1, :, 0:1], 0.0))
                                for k in range(9):
                                    L = 2 ** k
                                    m = min(L, LEN - L)
                                    pre, pim = (powers[:, i, k, 4 * j:4 * j + 4].unsqueeze(2).to_broadcast([P, 4, min(m, P)]) for i in range(2))
                                    for o in range(0, m, P):
                                        mm_ = min(P, m - o)
                                        pr, pi = pre[:, :, 0:mm_], pim[:, :, 0:mm_]
                                        lo_re, lo_im = e[:, 0, :, o:o + mm_], e[:, 1, :, o:o + mm_]
                                        hi_re, hi_im = e[:, 0, :, L + o:L + o + mm_], e[:, 1, :, L + o:L + o + mm_]
                                        ta, tb = tmp[:, 0, :, 0:mm_], tmp[:, 1, :, 0:mm_]
                                        link(nc.gpsimd.tensor_tensor(hi_re, lo_re, pr, ALU.mult))
                                        link(nc.gpsimd.tensor_tensor(ta, lo_im, pi, ALU.mult))
                                        link(nc.gpsimd.tensor_tensor(hi_re, hi_re, ta, ALU.subtract))
                                        link(nc.gpsimd.tensor_tensor(hi_im, lo_im, pr, ALU.mult))
                                        link(nc.gpsimd.tensor_tensor(tb, lo_re, pi, ALU.mult))
                                        link(nc.gpsimd.tensor_tensor(hi_im, hi_im, tb, ALU.add))
                                g.sem_inc(tabled, 1)

                        @block.vector
                        def _(dve):
                            def tt(o, i0, i1, op):
                                vec.tick(nc.vector.tensor_tensor(o, i0, i1, op))

                            def link():
                                dve.wait_ge(vec.sem, vec.value)

                            for j in range(UB):
                                dve.wait_ge(drive_copied, 2 * j + 2)
                                dve.wait_ge(tabled, j + 1)
                                cs, sn = E[:, j % 2, 0], E[:, j % 2, 1]
                                bre, bim = bu[:, j % 2, 0], bu[:, j % 2, 1]
                                if j >= 1:
                                    dve.wait_ge(summed, j)
                                tt(z[:, 0], cs, bre, ALU.mult)
                                tt(xs[:, 0], sn, bim, ALU.mult)
                                tt(z[:, 1], cs, bim, ALU.mult)
                                tt(xs[:, 1], sn, bre, ALU.mult)
                                link()
                                tt(z[:, 0], z[:, 0], xs[:, 0], ALU.add)
                                tt(z[:, 1], z[:, 1], xs[:, 1], ALU.subtract)
                                link()
                                dve.sem_inc(rotated, 1)
                                for part in range(2):
                                    for q in range(4):
                                        vec.tick(nc.vector.tensor_tensor_scan(
                                            xs[:, part, q], mag[:, 4 * j + q:4 * j + q + 1].to_broadcast([P, LEN]), z[:, part, q],
                                            0.0, ALU.mult, ALU.add))
                                link()
                                tt(z[:, 0], cs, xs[:, 0], ALU.mult)
                                tt(z[:, 1], sn, xs[:, 0], ALU.mult)
                                tt(bre, sn, xs[:, 1], ALU.mult)
                                tt(bim, cs, xs[:, 1], ALU.mult)
                                link()
                                tt(xs[:, 0], z[:, 0], bre, ALU.subtract)
                                tt(xs[:, 1], z[:, 1], bim, ALU.add)
                                link()
                                dve.sem_inc(stated, 1)
                                dve.wait_ge(summed, j + 1)
                                nc.vector.scalar_tensor_tensor(y[:, j], uT[:, j, META:LEN], col("ssm_d", j), PS[:, 4 + j % 2, 0:SEQ],
                                                               ALU.mult, ALU.add).then_inc(ykept, 1)
                with nc.Block() as block:
                    @block.scalar
                    def _(a):
                        act.tick(nc.scalar.activation(y, y, ACT.Gelu_apprx_tanh))

                ssm_out = sbuf(scope, "ssm_out", [P, DB, SEQ])
                gates = sbuf(scope, "gates", [P, 2, MB, SEQ])
                with ExitStack() as inner:
                    y_parts = sbuf(inner, "y_parts", [P, UB, 2, SEQ], F32R)
                    split_activations(y_parts, y, UB)

                    def glu_scalar(a, it, s, ready, taken):
                        if s % 2 == 0:
                            a.wait_ge(taken, it * 2 + s // 2 + 1)
                            nc.scalar.activation(gates[:, 0], PS[:, 0:4, 0:SEQ], ACT.Sigmoid).then_inc(ready, 1)
                            a.wait_ge(ready, it * 2 + s // 2 + 1)
                            a.sem_inc(banks_free[0], 1)

                    def glu_vector(dve, it, s, ready, taken):
                        if s % 2 == 1:
                            dve.wait_ge(ready, it * 2 + s // 2 + 1)
                            nc.vector.tensor_tensor(ssm_out[:, bass.ds(it * 8 + 4 * (s // 2), 4)], PS[:, 4:8, 0:SEQ], gates[:, 0],
                                                    ALU.mult).then_inc(taken, 1)
                            dve.wait_ge(taken, it * 2 + s // 2 + 2)
                            dve.sem_inc(banks_free[1], 1)
                    project_pair("glu", 2, lambda k: y_parts[:, k], glu_scalar, glu_vector, slabs=4)

                with ExitStack() as inner:
                    with ExitStack() as room:
                        inverse_rms(xT, DB, SEQ, sbuf(room, "squares", [P, DB, SEQ]))
                    nT = sbuf(inner, "nT", [P, DB, 2, SEQ], F32R)
                    scale_and_split(nT, xT, DB, SEQ, col("norm_mix", 0, DB))

                    def mix_scalar(a, it, s, ready, taken):
                        if s == 0:
                            a.wait_ge(taken, it + 1)
                        nc.scalar.activation(gates[:, s], PS[:, 4 * s:4 * s + 4, 0:SEQ], ACT.Sigmoid).then_inc(ready, 1)
                        a.wait_ge(ready, it * 2 + s + 1)
                        a.sem_inc(banks_free[s], 1)

                    def mix_vector(dve, it, s, ready, taken):
                        branch = (attn_out, ssm_out)[s][:, bass.ds(it * 4, 4)]
                        dve.wait_ge(ready, it * 2 + s + 1)
                        n = nc.vector.tensor_tensor(branch, branch, gates[:, s], ALU.mult).then_inc(mixed, 1)
                        if s == 1:
                            a_part = attn_out[:, bass.ds(it * 4, 4)]
                            dve.wait_ge(mixed, it * 2 + 2)
                            nc.vector.tensor_tensor(a_part, a_part, branch, ALU.add).then_inc(taken, 1)
                    mixed = sem("mixed")
                    project_pair("mix_gates", 4, lambda k: nT[:, k], mix_scalar, mix_vector)

            with ExitStack() as scope:
                mixed_parts = sbuf(scope, "mixed_parts", [P, DB, 2, SEQ], F32R)
                split_activations(mixed_parts, attn_out, DB)

                def residual(it, s, ps):
                    part = hT[:, bass.ds(it * 8 + 4 * s, 4), META:LEN]
                    return nc.vector.tensor_tensor(part, part, ps, ALU.add)
                project("w_out", 4, lambda k: mixed_parts[:, k], SEQ, residual)

        with ExitStack() as scope:
            with ExitStack() as room:
                inverse_rms(xT, DB, SEQ, sbuf(room, "squares", [P, DB, SEQ]))
            mT = sbuf(scope, "mT", [P, DB, 2, SEQ], F32R)
            scale_and_split(mT, xT, DB, SEQ, col("norm_ffn", 0, DB))
            hid = sbuf(scope, "hid", [P, MB * FF_PARTS[0][1], 2, SEQ], F32R)
            gates = sbuf(scope, "gates", [P, 2, MB, SEQ])
            result = sbuf(scope, "result", [P, MB, SEQ])
            for part, (first, n_slabs) in enumerate(FF_PARTS):
                made, parted = sem(f"hidden_made{part}"), sem(f"hidden_parted{part}")

                def ffn_scalar(a, it, s, ready, taken):
                    if s == 0:
                        a.wait_ge(taken, it + 1)
                        nc.scalar.activation(gates[:, 0], PS[:, 0:4, 0:SEQ], ACT.Sigmoid).then_inc(ready, 1)

                def ffn_vector(dve, it, s, ready, taken):
                    if s == 0:
                        dve.wait_ge(ready, it + 1)
                        nc.vector.tensor_tensor(gates[:, 1], PS[:, 0:4, 0:SEQ], gates[:, 0], ALU.mult).then_inc(banks_free[0], 1)
                        dve.wait_ge(banks_free[0], freed[0] + it + 1)
                        dve.sem_inc(taken, 1)
                    else:
                        dve.wait_ge(parted, 2 * it + 1)
                        nc.vector.tensor_tensor(result[:], PS[:, 4:8, 0:SEQ], gates[:, 1], ALU.mult).then_inc(banks_free[1], 1)
                        dve.wait_ge(banks_free[1], freed[1] + it + 1)
                        dve.sem_inc(made, 1)

                def ffn_parts(g, it, taken):
                    g.wait_ge(made, it + 1)
                    dst = hid[:, bass.ds(it * MB, MB)]
                    nc.gpsimd.tensor_copy(dst[:, :, 0], result[:]).then_inc(parted, 1)
                    g.wait_ge(parted, 2 * it + 2)
                    nc.gpsimd.tensor_tensor(dst[:, :, 1], result[:], dst[:, :, 0].bitcast(F32), ALU.subtract).then_inc(parted, 1)

                with nc.Block() as block:
                    @block.gpsimd
                    def _(g):
                        g.sem_inc(parted, 1)
                project_pair(f"ffn_up{part}", 4, lambda k: mT[:, k], ffn_scalar, ffn_vector, on_pool=ffn_parts)

                ph_down = phases[f"ffn_down{part}"]
                with nc.Block() as block:
                    @block.sync
                    def _(sp):
                        stream(sp, ph_down)

                    @block.tensor
                    def _(pe):
                        for j in range(ph_down.upi):
                            for kt in range(KT):
                                wait_parts(pe, ph_down, 0, j, kt)
                                x = hid[:, (j // 4) * KT + kt]
                                for m in range(MB):
                                    M = 4 * (j % 4) + m
                                    mm = three_products(PS[:, M // 2, (M % 2) * SEQ:(M % 2 + 1) * SEQ], j % 2, kt,
                                                        slice(m * P, (m + 1) * P), x,
                                                        j < 4 and kt == 0 and M % 2 == 0, j >= ph_down.upi - 4 and kt == KT - 1)
                                release_parts(mm, j, kt)

                    @block.scalar
                    def _(a):
                        split_round(a, split_hi, ph_down, 0, ph_down.upi, None, False)

                    @block.vector
                    def _(dve):
                        def evacuate(it, s):
                            wait_slab(dve, ph_down, 0, 0, ph_down.upi)
                            vec.tick(nc.vector.tensor_tensor(xT, xT, PS[:, :, :].rearrange("p b (m t) -> p (b m) t", m=2), ALU.add))
                        split_round(dve, split_lo, ph_down, 0, ph_down.upi, evacuate, False)

        with ExitStack() as room:
            inverse_rms(xT, DB, SEQ, sbuf(room, "squares", [P, DB, SEQ]))
            scale_tokens(xT, xT, DB, SEQ, col("norm_final", 0, DB))

        with ExitStack() as two:
            gains = sbuf(two, "gains", [P, DB])

            def modulated(dst, gain, mod):
                small_ops([lambda: nc.vector.scalar_tensor_tensor(gains[:], mod[:, DB:2 * DB], 1.0, gain, ALU.add, ALU.mult)])
                scale_and_split(dst, xT, DB, SEQ, gains, mod[:, 0:DB])

            def post_norm(y_out, gain, gate, squares):
                inverse_rms(y_out, DB, SEQ, squares)
                small_ops([lambda: nc.vector.tensor_tensor(gains[:], gain, gate, ALU.mult)])
                scale_tokens(y_out, y_out, DB, SEQ, gains)
                small_ops([lambda: nc.vector.tensor_tensor(xT, xT, y_out, ALU.add)])

            with ExitStack() as scope:
                qk = sbuf(scope, "qk", [P, 2 * A_QK // P, SEQ])
                heads_view = qk[:].rearrange("p (r h e) t -> p r h e t", r=2, e=2)
                with ExitStack() as inner:
                    hn = sbuf(inner, "hn", [P, DB, 2, SEQ], F32R)
                    with ExitStack() as proj:
                        pick = mod_room[0:A_HEADS].rearrange("p a b -> p (a b)")
                        va = sbuf(proj, "va", [P, 2, A_INNER])
                        inverse_rms(xT, DB, SEQ, qk)
                        modulated(hn, col("g_pre_2", 0, DB), mods[:, 0:3 * DB])

                        project("a_qk", 4, lambda k: hn[:, k], SEQ,
                                lambda it, s, ps: nc.vector.tensor_copy(qk[:, bass.ds(it * 8 + 4 * s, 4)], ps))

                        ph_v = phases["a_v"]
                        conv_step = sem("conv_step")
                        with ExitStack() as conv:
                            acc = sbuf(conv, "acc", [P, MB, SEQ])
                            term = sbuf(conv, "term", [P, MB, SEQ])
                            with nc.Block() as block:
                                @block.sync
                                def _(sp):
                                    stream(sp, ph_v)

                                values_by_token(ph_v, block, hn, va)

                                @block.vector
                                def _(dve):
                                    def convolve(it, j):
                                        j -= 1
                                        quarter = (j - 1) % 4
                                        b = it * 2 + (j - 1) // 4
                                        part = qk[:, bass.ds(b * MB, MB)]
                                        bias = cols[:, bass.ds(b * MB + 3 * P, MB)].unsqueeze(2).to_broadcast([P, MB, SEQ])

                                        def step(i, out_, in0, in1, op):
                                            dve.wait_ge(conv_step, it * 18 + (j - 1) // 4 * 9 + i + 1)
                                            nc.vector.tensor_tensor(out_, in0, in1, op).then_inc(conv_step, 1)

                                        def tapped(out_, back):
                                            n = SEQ - back
                                            weight = cols[:, bass.ds(b * MB + 32 * (CONV - 1 - back), MB)].unsqueeze(2)
                                            return out_[:, :, 0:n], part[:, :, 0:n], weight.to_broadcast([P, MB, n]), ALU.mult

                                        if quarter == 0:
                                            step(0, *tapped(acc, 0))
                                            step(1, acc[:], acc[:], bias, ALU.add)
                                        else:
                                            step(2 * quarter, *tapped(term, quarter))
                                            late = slice(quarter, SEQ)
                                            dst = acc if quarter < CONV - 1 else part
                                            step(2 * quarter + 1, dst[:, :, late], acc[:, :, late], term[:, :, 0:SEQ - quarter], ALU.add)
                                        if quarter == CONV - 1:
                                            dve.wait_ge(conv_step, it * 18 + (j - 1) // 4 * 9 + 9)
                                            nc.vector.tensor_scalar(part[:, :, 0:CONV - 1], acc[:, :, 0:CONV - 1], 1.0, None,
                                                                    ALU.mult).then_inc(conv_step, 1)

                                    dve.sem_inc(conv_step, 1)
                                    with dve.Fori(0, ph_v.iters) as it:
                                        split_round(dve, split_lo, ph_v, it, 4, None, False, convolve)
                            for s in range(2):
                                freed[s] += ph_v.iters
                            with nc.Block() as block:
                                base_a, base_v = act.value, vec.value

                                @block.scalar
                                def _(a):
                                    for b in range(8):
                                        if b >= 2:
                                            a.wait_ge(vec.sem, base_v + b - 1)
                                        act.tick(nc.scalar.activation((acc, term)[b % 2][:], qk[:, b * MB:(b + 1) * MB], ACT.Sigmoid))

                                @block.vector
                                def _(dve):
                                    for b in range(8):
                                        dve.wait_ge(act.sem, base_a + b + 1)
                                        part = qk[:, b * MB:(b + 1) * MB]
                                        vec.tick(nc.vector.tensor_tensor(part, part, (acc, term)[b % 2][:], ALU.mult))

                        gate_rows = sbuf(proj, "gate_rows", [A_HEADS, 5, SEQ])
                        with ExitStack() as gate_room, nc.Block() as block:
                            w_g = sbuf(gate_room, "w_g", [P, DB, 2 * A_HEADS])
                            b_g = sbuf(gate_room, "b_g", [A_HEADS, 2])
                            gates_in = small[0] + 48
                            gated = ten.value + 1
                            a0, v0 = act.value, vec.value

                            @block.sync
                            def _(sp):
                                load_small(sp, w_g[:], w["a_w_in_2"][:, A_G0:A_G0 + 2 * A_HEADS].rearrange("(k p) n -> p k n", p=P))
                                load_small(sp, pick, w["head_pick"])
                                load_small(sp, b_g[:], w["a_gate_b_2"])

                            @block.tensor
                            def _(pe):
                                pe.wait_ge(small_loaded, gates_in)
                                for g in range(2):
                                    for k in range(DB):
                                        for part in range(2):
                                            mm = nc.tensor.matmul(PS[0:A_HEADS, g, 0:SEQ], w_g[:, k, g * A_HEADS:(g + 1) * A_HEADS],
                                                                  hn[:, k, part].bitcast(F32), start=(k == 0 and part == 0),
                                                                  stop=(k == DB - 1 and part == 1))
                                ten.tick(mm)


                            @block.scalar
                            def _(a):
                                a.wait_ge(vec.sem, v0 + 2)
                                for fn, dst, src, kw in ((ACT.Abs, ABS, FG_, {}), (ACT.Exp, ABS, ABS, {"scale": -1.0}),
                                                         (ACT.Ln, ABS, ABS, {"bias": ones[0:A_HEADS, 0:1]})):
                                    n = act.tick(nc.scalar.activation(gate_rows[:, dst], gate_rows[:, src], fn, **kw))
                                    a.wait_ge(act.sem, n)
                                a.wait_ge(vec.sem, v0 + 9)
                                act.tick(nc.scalar.activation(gate_rows[:, EN], gate_rows[:, EN], ACT.Exp, scale=-1.0))

                            @block.vector
                            def _(dve):
                                def link(instruction):
                                    dve.wait_ge(vec.sem, vec.tick(instruction))
                                dve.wait_ge(ten.sem, gated)
                                link(nc.vector.tensor_scalar(gate_rows[:, I], PS[0:A_HEADS, 0, 0:SEQ], b_g[:, 0:1], None, ALU.add))
                                link(nc.vector.tensor_scalar(gate_rows[:, FG_], PS[0:A_HEADS, 1, 0:SEQ], b_g[:, 1:2], None, ALU.add))
                                dve.wait_ge(act.sem, a0 + 3)
                                link(nc.vector.tensor_scalar(gate_rows[:, FG_], gate_rows[:, FG_], 0.0, None, ALU.min))
                                link(nc.vector.tensor_tensor(gate_rows[:, FG_], gate_rows[:, FG_], gate_rows[:, ABS], ALU.subtract))
                                link(nc.vector.tensor_tensor_scan(gate_rows[:, CUM], ones[0:A_HEADS, 0:1].to_broadcast([A_HEADS, SEQ]),
                                                                  gate_rows[:, FG_], 0.0, ALU.mult, ALU.add))
                                link(nc.vector.tensor_tensor(gate_rows[:, A_], gate_rows[:, I], gate_rows[:, CUM], ALU.subtract))
                                link(nc.vector.memset(gate_rows[:, ZERO], 0.0))
                                link(nc.vector.tensor_tensor_scan(gate_rows[:, MM], gate_rows[:, A_], gate_rows[:, ZERO], 0.0, ALU.max, ALU.max))
                                link(nc.vector.tensor_tensor(gate_rows[:, EN], gate_rows[:, CUM], gate_rows[:, MM], ALU.add))

                        mlstm_heads(nc, sem, sbuf, PS, gate_rows, qk, va, ident, ones, after, pick)

                    with ExitStack() as hs:
                        rms_head = sbuf(hs, "rms_head", [P, A_HEADS, SEQ])
                        sq = sbuf(hs, "sq", [P, 2, 4, SEQ])
                        squared, hsum, sq_used = sem("head_squared"), sem("head_summed"), sem("head_rooted")
                        with nc.Block() as block:
                            @block.gpsimd
                            def _(g):
                                for h in range(A_HEADS):
                                    if h >= 2:
                                        g.wait_ge(hsum, h - 1)
                                    for r in range(2):
                                        src = heads_view[:, r, h]
                                        last = nc.gpsimd.tensor_tensor(sq[:, h % 2, 2 * r:2 * r + 2], src, src, ALU.mult)
                                        last.then_inc(squared, 1)

                            @block.tensor
                            def _(pe):
                                for h in range(A_HEADS):
                                    pe.wait_ge(squared, 2 * h + 2)
                                    if h >= 4:
                                        pe.wait_ge(sq_used, h - 3)
                                    for e in range(4):
                                        mm = nc.tensor.matmul(PS[:, h % 4, 0:SEQ], ones[:], sq[:, h % 2, e], start=(e == 0), stop=(e == 3))
                                    mm.then_inc(hsum, 1)

                            @block.scalar
                            def _(a):
                                for h in range(A_HEADS):
                                    a.wait_ge(hsum, h + 1)
                                    nc.scalar.activation(rms_head[:, h], PS[:, h % 4, 0:SEQ], ACT.Sqrt, scale=1.0 / A_DV,
                                                         bias=eps[:, 0:1]).then_inc(sq_used, 1)

                            @block.vector
                            def _(dve):
                                def link():
                                    dve.wait_ge(vec.sem, vec.value)
                                for h in range(A_HEADS):
                                    dve.wait_ge(sq_used, h + 1)
                                    vec.tick(nc.vector.reciprocal(rms_head[:, h], rms_head[:, h]))
                                    link()
                                    for e in range(4):
                                        ht = heads_view[:, e // 2, h, e % 2]
                                        vec.tick(nc.vector.scalar_tensor_tensor(ht, ht, col("a_g_head_2", 4 * h + e), rms_head[:, h], ALU.mult, ALU.mult))

                    gates = sbuf(inner, "gates", [P, 2, MB, SEQ])

                    def oz_scalar(a, it, s, ready, taken):
                        if s == 0:
                            a.wait_ge(taken, it + 1)
                        nc.scalar.activation(gates[:, s], PS[:, 4 * s:4 * s + 4, 0:SEQ], ACT.Sigmoid).then_inc(ready, 1)
                        if s == 0:
                            a.wait_ge(ready, it * 2 + 1)
                            a.sem_inc(banks_free[0], 1)

                    def oz_vector(dve, it, s, ready, taken):
                        if s == 0:
                            return
                        dve.wait_ge(ready, it * 2 + 2)
                        nc.vector.tensor_tensor(gates[:, 1], PS[:, 4:8, 0:SEQ], gates[:, 1], ALU.mult).then_inc(banks_free[1], 1)
                        dve.wait_ge(banks_free[1], freed[1] + it + 1)
                        nc.vector.tensor_tensor(gates[:, 0], gates[:, 0], gates[:, 1], ALU.mult).then_inc(gated_twice, 1)

                    def oz_apply(g, it, taken):
                        g.wait_ge(gated_twice, it + 1)
                        ht = qk[:].rearrange("p (r b) t -> p r b t", r=2)[:, :, bass.ds(it * 2, 2)]
                        nc.gpsimd.tensor_tensor(ht, ht, gates[:, 0].rearrange("p (r e) t -> p r e t", r=2), ALU.mult).then_inc(taken, 1)
                    gated_twice = sem("gated_twice")
                    project_pair("a_oz", 4, lambda k: hn[:, k], oz_scalar, oz_vector, on_pool=oz_apply)
                y_parts = sbuf(scope, "y_parts", [P, A_INNER // P, 2, SEQ], F32R)
                split_activations(y_parts, qk, A_INNER // P)
                y_out, room = qk[:, 0:DB], qk[:, DB:2 * DB]
                project("a_out", 8, lambda k: y_parts[:, k % 4 // 2 * DB + k // 4 * 2 + k % 2], SEQ,
                        lambda it, s, ps: nc.vector.tensor_copy(qk[:, bass.ds(it * 8 + 4 * s, 4)], ps))
                post_norm(y_out, col("g_post_2", 0, DB), mods[:, 2 * DB:3 * DB], room)

            with ExitStack() as scope:
                kb = sbuf(scope, "kb", [P, DB, SEQ])
                vb = sbuf(scope, "vb", [P, 2, D])
                qb = sbuf(scope, "qb", [P, DB, SEQ])
                zb = sbuf(scope, "zb", [P, DB, SEQ])
                with ExitStack() as inner:
                    hn = sbuf(inner, "hn", [P, DB, 2, SEQ], F32R)
                    inverse_rms(xT, DB, SEQ, kb)
                    modulated(hn, col("kv_g_2", 0, DB), mods[:, 6 * DB:8 * DB])
                    project("b_k", 4, lambda k: hn[:, k], SEQ,
                            lambda it, s, ps: nc.vector.tensor_copy(kb[:, bass.ds(it * 8 + 4 * s, 4)], ps))
                    ph_v = phases["b_v"]
                    with nc.Block() as block:
                        @block.sync
                        def _(sp):
                            stream(sp, ph_v)

                        values_by_token(ph_v, block, hn, vb)

                        @block.vector
                        def _(dve):
                            with dve.Fori(0, ph_v.iters) as it:
                                split_round(dve, split_lo, ph_v, it, 4, None, False)
                    for s in range(2):
                        freed[s] += ph_v.iters
                    modulated(hn, col("g_pre_2", DB, DB), mods[:, 3 * DB:6 * DB])
                    project("b_q", 4, lambda k: hn[:, k], SEQ,
                            lambda it, s, ps: nc.vector.tensor_copy(qb[:, bass.ds(it * 8 + 4 * s, 4)], ps))
                    project("b_z", 4, lambda k: hn[:, k], SEQ,
                            lambda it, s, ps: nc.vector.tensor_copy(zb[:, bass.ds(it * 8 + 4 * s, 4)], ps))

                with ExitStack() as inner:
                    bias = sbuf(inner, "bias", [P, HEADS, SEQ])
                    rel = sbuf(inner, "rel", [HEADS, 2 * MAX_REL + 1])
                    drawn = sbuf(inner, "drawn", [HEADS, 3 * P])
                    with nc.Block() as block:
                        rel_loaded, made = small[0] + 16, vec.value + 2
                        spread_done = small[0] + 48

                        @block.sync
                        def _(sp):
                            load_small(sp, rel[:], w["b_rel_2"])
                            sp.wait_ge(vec.sem, made)
                            load_small(sp, w["rel_scratch"], drawn[:])
                            sp.wait_ge(small_loaded, rel_loaded + 16)
                            scratch = w["rel_scratch"]
                            load_small(sp, bias[:], bass.AP(tensor=scratch.tensor, offset=scratch.offset,
                                                            ap=[[1, P], [3 * P, HEADS], [1, SEQ]]))

                        @block.vector
                        def _(dve):
                            dve.wait_ge(small_loaded, rel_loaded)
                            vec.tick(nc.vector.tensor_copy(drawn[:, 2 * P:3 * P], rel[:, 2 * MAX_REL:2 * MAX_REL + 1].to_broadcast([HEADS, P])))
                            vec.tick(nc.vector.tensor_copy(drawn[:, 0:2 * P], rel[:, 1:2 * MAX_REL + 1]))
                            dve.wait_ge(small_loaded, spread_done)
                            vec.tick(nc.vector.memset(bias[0:CHUNK, :, 0:CHUNK], NEG))

                    def band_keys(n):
                        return P * (n % 2 + 1)

                    attention("band", HEADS, lambda n: [(qb[:, n // 2, (n % 2) * P:(n % 2 + 1) * P], kb[:, n // 2, 0:band_keys(n)])],
                              band_keys, lambda n: bias[:, n // 2, 0:band_keys(n)][:, ::-1], P ** -0.5, vb, qb)
                with nc.Block() as block:
                    base_a = act.value

                    @block.scalar
                    def _(a):
                        act.tick(nc.scalar.activation(kb[:], zb[:], ACT.Sigmoid))

                    @block.vector
                    def _(dve):
                        n = vec.tick(nc.vector.tensor_tensor(qb[:], qb[:], zb[:], ALU.mult))
                        dve.wait_ge(vec.sem, n)
                        dve.wait_ge(act.sem, base_a + 1)
                        vec.tick(nc.vector.tensor_tensor(qb[:], qb[:], kb[:], ALU.mult))
                with ExitStack() as inner:
                    y_parts = sbuf(inner, "y_parts", [P, DB, 2, SEQ], F32R)
                    split_activations(y_parts, qb, DB)
                    project("b_out", 4, lambda k: y_parts[:, k], SEQ,
                            lambda it, s, ps: nc.vector.tensor_copy(kb[:, it * 8 + 4 * s:it * 8 + 4 * s + 4], ps), static=True, follows=False)
                post_norm(kb[:], col("g_post_2", DB, DB), mods[:, 5 * DB:6 * DB], qb)

        with ExitStack() as scope:
            rows_out = sbuf(scope, "rows_out", [P, 2, D])
            turned, copied = sem("output_turned"), sem("output_copied")
            with nc.Block() as block:
                @block.tensor
                def _(pe):
                    for n in range(8):
                        if n >= 4:
                            pe.wait_ge(copied, n - 3)
                        for q in range(4):
                            k, t = (n % 4) * 4 + q, n // 4
                            mm = nc.tensor.transpose(PS[:, n % 4, q * P:(q + 1) * P], xT[:, k, t * P:(t + 1) * P], ident)
                        mm.then_inc(turned, 1)

                @block.vector
                def _(dve):
                    for n in range(8):
                        dve.wait_ge(turned, n + 1)
                        nc.vector.tensor_copy(rows_out[:, n // 4, (n % 4) * COLS:(n % 4 + 1) * COLS], PS[:, n % 4, :]).then_inc(copied, 1)

                @block.sync
                def _(sp):
                    for t in range(2):
                        sp.wait_ge(copied, 4 * t + 4)
                        sp.dma_start(out[t * P:(t + 1) * P, :], rows_out[:, t]).then_inc(stored, 16)
                    sp.wait_ge(stored, 32)


def mlstm_heads(nc, sem, sbuf, PS, gate_rows, qk, va, ident, ones, after, head_pick):
    QB = A_DK // P
    W0 = SEQ + P
    with ExitStack() as scope:
        a_cols = sbuf(scope, "a_cols", [P, 2, A_HEADS])
        wt = sbuf(scope, "wt", [P, 2, W0])
        st = sbuf(scope, "st", [P, 2, W0])
        den = sbuf(scope, "den", [P, 2, SEQ])
        spread, scored, a_turned, a_kept = (sem(f"mlstm_{x}") for x in ("spread", "scored", "a_turned", "a_kept"))
        masked, exped, weighted, valued = (sem(f"mlstm_{x}") for x in ("masked", "exped", "weighted", "valued"))
        den_summed, absed, kept, dstep = (sem(f"mlstm_{x}") for x in ("den_summed", "absed", "kept", "dstep"))
        spread_bank = (0, 1, 7)
        with nc.Block() as block:
            @block.tensor
            def _(pe):
                for b in range(2):
                    mm = nc.tensor.transpose(PS[:, 7, 8 * b:8 * b + 8], gate_rows[:, A_, b * P:(b + 1) * P], ident[0:A_HEADS, 0:A_HEADS])
                mm.then_inc(a_turned, 1)

                def front(h):
                    if h == 2:
                        pe.wait_ge(a_kept, 1)
                    if h >= 3:
                        pe.wait_ge(kept, h - 2)
                    for i, r in enumerate((MM, EN)):
                        mm = nc.tensor.matmul(PS[:, spread_bank[h % 3], i * SEQ:(i + 1) * SEQ], head_pick[0:A_HEADS, h * P:(h + 1) * P],
                                              gate_rows[:, r], start=True, stop=True)
                    mm.then_inc(spread, 1)
                    if h >= 2:
                        pe.wait_ge(weighted, h - 1)
                    for b in range(2):
                        dst = PS[:, 2 + h % 2, b * SEQ:b * SEQ + SEQ - b * P]
                        for i in range(QB):
                            mm = nc.tensor.matmul(dst, qk[:, A_QK // P + QB * h + i, b * P:(b + 1) * P], qk[:, QB * h + i, b * P:SEQ],
                                                  start=(i == 0), stop=(i == QB - 1))
                    mm.then_inc(scored, 1)

                front(0)
                front(1)
                for h in range(A_HEADS):
                    pe.wait_ge(weighted, h + 1)
                    if h >= 1:
                        pe.wait_ge(kept, h)
                    for e in (4, 0, 1, 2, 3):
                        dst = PS[:, 4 + e // 2, (e % 2) * SEQ:(e % 2 + 1) * SEQ]
                        for b in range(2):
                            lhsT = va[:, b, h * A_DV + e * P:h * A_DV + (e + 1) * P] if e < 4 else ones[:]
                            mm = nc.tensor.matmul(dst[:, b * P:SEQ], lhsT, st[:, h % 2, b * SEQ:b * SEQ + SEQ - b * P],
                                                  start=(b == 0), stop=(b == 1))
                        if e == 4:
                            mm.then_inc(den_summed, 1)
                    mm.then_inc(valued, 1)
                    if h + 2 < A_HEADS:
                        front(h + 2)

            @block.scalar
            def _(a):
                def weight_exp(h):
                    a.wait_ge(masked, h + 1)
                    nc.scalar.activation(wt[:, h % 2, 0:SEQ], wt[:, h % 2, 0:SEQ], ACT.Exp, scale=-1.0, bias=a_cols[:, 0, h:h + 1])
                    nc.scalar.activation(wt[:, h % 2, SEQ:W0], wt[:, h % 2, SEQ:W0], ACT.Exp, scale=-1.0,
                                         bias=a_cols[:, 1, h:h + 1]).then_inc(exped, 1)

                a.wait_ge(a_kept, 1)
                weight_exp(0)
                weight_exp(1)
                for h in range(A_HEADS):
                    denominator(nc, a, h, den_summed, absed, den, PS)
                    if h + 2 < A_HEADS:
                        weight_exp(h + 2)

            @block.vector
            def _(dve):
                steps = 0

                def link(instruction):
                    nonlocal steps
                    steps += 1
                    instruction.then_inc(dstep, 1)
                    dve.wait_ge(dstep, steps)

                def mask(h):
                    dve.wait_ge(spread, h + 1)
                    b, bank = h % 2, spread_bank[h % 3]
                    if h >= 2:
                        dve.wait_ge(weighted, h - 1)
                    nc.vector.tensor_tensor(wt[:, b, 0:SEQ], PS[:, bank, 0:SEQ], after, ALU.add)
                    nc.vector.tensor_tensor(wt[:, b, SEQ:W0], PS[:, bank, P:SEQ], after[:, 0:P], ALU.add).then_inc(masked, 1)

                def weigh(h):
                    b = h % 2
                    dve.wait_ge(scored, h + 1)
                    dve.wait_ge(exped, h + 1)
                    if h >= 2:
                        dve.wait_ge(valued, h - 1)
                    nc.vector.scalar_tensor_tensor(st[:, b], PS[:, 2 + b, 0:W0], A_DK ** -0.5, wt[:, b], ALU.mult, ALU.mult).then_inc(weighted, 1)

                dve.wait_ge(a_turned, 1)
                nc.vector.tensor_copy(a_cols[:], PS[:, 7, 0:16].rearrange("p (b h) -> p b h", b=2)).then_inc(a_kept, 1)
                mask(0)
                mask(1)
                weigh(0)
                for h in range(A_HEADS):
                    b = h % 2
                    if h + 1 < A_HEADS:
                        weigh(h + 1)
                    dve.wait_ge(absed, h + 1)
                    link(nc.vector.tensor_tensor(den[:, b], den[:, b], PS[:, spread_bank[h % 3], SEQ:2 * SEQ], ALU.max))
                    link(nc.vector.reciprocal(den[:, b], den[:, b]))
                    dve.wait_ge(valued, h + 1)
                    for r in range(2):
                        dst = qk[:, r * (A_QK // P) + QB * h:r * (A_QK // P) + QB * h + QB]
                        last = nc.vector.tensor_tensor(dst, PS[:, 4 + r, :].rearrange("p (e t) -> p e t", e=2),
                                                       den[:, b].unsqueeze(1).to_broadcast([P, 2, SEQ]), ALU.mult)
                    last.then_inc(kept, 1)
                    if h + 2 < A_HEADS:
                        mask(h + 2)


def denominator(nc, a, h, den_summed, absed, den, PS):
    a.wait_ge(den_summed, h + 1)
    nc.scalar.activation(den[:, h % 2], PS[:, 6, 0:SEQ], ACT.Abs).then_inc(absed, 1)


def shape_constants():
    import numpy as np
    a = np.zeros((P, CONST_COLS), np.float32)
    one = np.zeros((P, 3 * LEN), np.float32)

    def put(name, value):
        dst, (first, n) = (a, CONST[name]) if name in CONST else (one, CONST_ONE[name])
        dst[:, first:first + n] = value

    put("identity", np.eye(P, dtype=np.float32))
    half = ROPE // 2
    freqs = np.float32(10000.0) ** (-np.arange(half, dtype=np.float32) / np.float32(half))
    ang = np.arange(LEN, dtype=np.float32)[None, :] * freqs[:, None]
    put("cos", np.tile(np.cos(ang), (4, 1)))
    put("sin", np.tile(np.concatenate([-np.sin(ang), np.sin(ang)]), (2, 1)))
    p = np.arange(P)[:, None]
    put("causal", np.where(np.arange(LEN)[None, :] <= P + META + p, 0.0, NEG))
    put("after", np.where(np.arange(SEQ)[None, :] < p, -NEG, 0.0))
    return a, one


_MATRICES = ["w_in", "w_kv_up", "w_attn_proj", "w_glu_val", "w_glu_gate", "w_out", "w_ffn_gate", "w_ffn_up",
             "w_ffn_down", "a_w_in_2", "a_w_out_2", "b_w_in_2", "b_w_out_2"]


def kernel(**inputs):
    import numpy as np
    import concourse.bacc as bacc
    from concourse.bass_utils import run_bass_kernel_spmd as run

    nc = bacc.Bacc("TRN2", target_bir_lowering=False, num_devices=1)
    arrays, w = {}, {}

    def give(name, a):
        a = np.ascontiguousarray(a)
        arrays[f"in_{name}"] = a
        w[name] = nc.dram_tensor(f"in_{name}", a.shape, F32, kind="ExternalInput").ap()

    for name in _MATRICES:
        give(name, np.asarray(inputs[name])[0])
    q_up = np.asarray(inputs["w_q_up"])[0].reshape(LORA, HEADS // 2, 2, NOPE + ROPE)
    give("w_q_up", np.concatenate([q_up[..., :NOPE].reshape(LORA, HEADS // 2, -1),
                                   q_up[..., NOPE:].reshape(LORA, HEADS // 2, -1)], axis=2).reshape(LORA, -1))
    ada = np.asarray(inputs["ada_w_2"])
    give("ada_all", np.concatenate([ada[0], ada[1], np.asarray(inputs["kv_ada_w_2"])], axis=1))
    for name in ("kv_w_2", "meta_tokens"):
        give(name, inputs[name])
    for name in ("ssm_lambda_re", "ssm_lambda_im", "ssm_log_step", "ssm_b_re", "ssm_b_im", "ssm_c_re", "ssm_c_im",
                 "b_rel_2", "x"):
        give(name, np.asarray(inputs[name])[0])
    give("a_gate_b_2", np.asarray(inputs["a_gate_b_2"])[0].reshape(2, A_HEADS).T)
    for name in VECTOR_ROWS:
        give(name + "_rows", np.asarray(inputs[name]).reshape(-1, P))
    for name, value in zip(("shape_constants", "shape_constants_one"), shape_constants()):
        give(name, value)
    give("head_pick", np.kron(np.eye(A_HEADS), np.ones((1, P))).astype(np.float32))
    w["rel_scratch"] = nc.dram_tensor("rel_scratch", (HEADS, 3 * P), F32, kind="Internal").ap()
    out = nc.dram_tensor("out_x", (SEQ, D), F32, kind="ExternalOutput").ap()
    build(nc, w, out)
    r = run(nc, [arrays], core_ids=[0])
    return r.results[0]["out_x"].reshape(1, SEQ, D)
```

```python
from contextlib import ExitStack

import concourse.bass as bass
from concourse import mybir

F32 = mybir.dt.float32
F32R = mybir.dt.float32r
I32 = mybir.dt.int32
ALU = mybir.AluOpType
ACT = mybir.ActivationFunctionType
AX = mybir.AxisListType.X

P = 128
D = 2048
DB = D // P
SEQ = 256
META = 16
LEN = SEQ + META
EPS = 1e-6
NEG = -1e30

SLOTS = 4
KT = 4
COLS = 512
MB = COLS // P

HEADS = 16
LORA = 512
NOPE, ROPE = 128, 64
G, N, C = 64, 64, 16
SSM_W = G * C
OFF_KR = 2 * LORA
OFF_U = OFF_KR + ROPE
OFF_G = OFF_U + SSM_W

FF_PARTS = ((0, 6), (6, 5))

A_INNER, A_QK, A_HEADS, CONV = 4096, 2048, 8, 4
A_DK, A_DV = A_QK // A_HEADS, A_INNER // A_HEADS
I, FG_, ABS, CUM, MM = range(5)
A_, ZERO, EN = I, FG_, ABS
A_V0, A_O0, A_Z0, A_G0 = 2 * A_QK, 2 * A_QK + A_INNER, 2 * A_QK + 2 * A_INNER, 2 * A_QK + 3 * A_INNER
CHUNK, MAX_REL = 64, 128

VECTOR_ROWS = {
    "a_conv_w_2": (0, 0, 128),
    "ada_b_2": (1, 0, 96), "kv_ada_b_2": (1, 96, 32),
    "g_pre_2": (2, 0, 32), "g_post_2": (2, 32, 32), "norm_mix": (2, 64, 16), "norm_ffn": (2, 80, 16),
    "norm_final": (2, 96, 16), "kv_g_2": (2, 112, 16),
    "a_conv_b_2": (3, 0, 32), "a_g_head_2": (3, 32, 32), "c_2": (3, 64, 16), "norm_q": (3, 80, 4),
    "norm_kv": (3, 84, 4), "ssm_d": (3, 88, 8),
}
VECTOR_TILE_ROWS = (128, 128, 128, 96)

CONST = {"identity": (0, 128), "after": (128, SEQ)}
CONST_COLS = 128 + SEQ
CONST_ONE = {"cos": (0, LEN), "sin": (LEN, LEN), "causal": (2 * LEN, LEN)}


class Phase:

    def __init__(self, base, iters, upi, source, extra, splits):
        self.base, self.iters, self.upi, self.source, self.extra, self.splits = base, iters, upi, source, extra, splits
        self.raw = upi + upi // 2 if extra is not None else upi
        assert iters == 1 or self.raw % SLOTS == 0
        self.end = base + iters * self.raw

    def place(self, j):
        return j + j // 2 if self.extra is not None else j

    def slot_at(self, r):
        return (self.base + r) % SLOTS

    def uses_at(self, it, r):
        return (self.base + r) // SLOTS + it * (self.raw // SLOTS) + 1

    def slot(self, j):
        return self.slot_at(self.place(j))

    def uses(self, it, j):
        return self.uses_at(it, self.place(j))

    def fills(self, it, j):
        return (self.splits + j) // 2 + it * (self.upi // 2) + 1


def plan_units(w):
    phases, flat = {}, []

    def block(m, row, col, cols=COLS):
        rows = m[bass.ds(row, KT * P), :] if not isinstance(row, int) else m[row:row + KT * P, :]
        part = rows[:, bass.ds(col, cols)] if not isinstance(col, int) else rows[:, col:col + cols]
        return part.rearrange("(k p) n -> p k n", p=P)

    splits = [0]

    def add(name, iters, upi, source, extra=None, split=True):
        ph = phases[name] = Phase(len(flat), iters, upi, source, extra, splits[0] if split else None)
        for it in range(iters):
            for r in range(ph.raw):
                flat.append((lambda it, r, ph=ph: round_unit(ph, it, r), it, r))
        assert len(flat) == ph.end
        if split:
            splits[0] += iters * upi

    def round_unit(ph, it, r):
        if ph.extra is None:
            return ph.source(it, r)
        if r % 3 == 2:
            return block(w["ada_all"], (r // 3) % 4 * KT * P, (it + ph.extra + r // 12) * COLS)
        return ph.source(it, r - r // 3)

    def slabs(m, first, k_units, per=2):
        return lambda it, j: block(m, (j % k_units) * KT * P, first + it * per * COLS + (j // k_units) * COLS)

    def pair(m0, c0, m1, c1, k_units, per=1):
        def source(it, j):
            s = j // k_units
            m, c = ((m0, c0), (m1, c1))[s % 2]
            return block(m, (j % k_units) * KT * P, c + it * per * COLS + (s // 2) * COLS)
        return source

    add("latents", 1, 8, slabs(w["w_in"], 0, 4))
    add("u", 1, 8, slabs(w["w_in"], OFF_U, 4), extra=0)
    add("q_up", 1, 8, lambda it, j: block(w["w_q_up"], 0, j * 2 * (NOPE + ROPE), 2 * (NOPE + ROPE)))
    add("kv_up", 1, 8, lambda it, j: block(w["w_kv_up"], 0, j * COLS))
    add("attn_proj", 2, 8, slabs(w["w_attn_proj"], 0, 4), extra=1)
    add("glu", 2, 8, pair(w["w_glu_gate"], 0, w["w_glu_val"], 0, 2, 2))
    add("mix_gates", 4, 8, pair(w["w_in"], OFF_G, w["w_in"], OFF_G + D, 4), extra=3)
    add("w_out", 2, 8, slabs(w["w_out"], 0, 4), extra=7)
    for part, (first, n) in enumerate(FF_PARTS):
        add(f"ffn_up{part}", n, 8, pair(w["w_ffn_gate"], first * COLS, w["w_ffn_up"], first * COLS, 4), extra=9 + first)
        add(f"ffn_down{part}", 1, 4 * n,
            lambda it, j, first=first: block(w["w_ffn_down"], (first + j // 4) * KT * P, (j % 4) * COLS))
    add("a_qk", 4, 8, slabs(w["a_w_in_2"], 0, 4), extra=20)
    add("a_v", 4, 8, slabs(w["a_w_in_2"], A_V0, 4))
    add("a_oz", 8, 8, pair(w["a_w_in_2"], A_O0, w["a_w_in_2"], A_Z0, 4), extra=24)
    add("a_out", 2, 16, slabs(w["a_w_out_2"], 0, 8))
    add("b_k", 2, 8, slabs(w["kv_w_2"], 0, 4))
    add("b_v", 2, 8, slabs(w["kv_w_2"], D, 4))
    add("b_q", 2, 8, slabs(w["b_w_in_2"], 0, 4))
    add("b_z", 2, 8, slabs(w["b_w_in_2"], D, 4))
    add("b_out", 2, 8, slabs(w["b_w_out_2"], 0, 4))
    return phases, flat, round_unit


class Feed:

    def __init__(self, vector, scalar, pool, wait):
        self.vector, self.scalar, self.pool, self.wait = vector, scalar, pool, wait


class Step:

    def __init__(self, sem):
        self.sem, self.value = sem, 0

    def tick(self, instruction):
        self.value += 1
        instruction.then_inc(self.sem, 1)
        return self.value


def build(nc, w, out):
    with ExitStack() as ctx:
        names = [0]

        def sem(name):
            return ctx.enter_context(nc.semaphore(name))

        def sbuf(stack, name, shape, dtype=F32):
            names[0] += 1
            return stack.enter_context(nc.sbuf_tensor(f"{name}_{names[0]}", shape, dtype))

        phases, flat, round_unit = plan_units(w)

        ring = sbuf(ctx, "ring", [P, SLOTS, KT, COLS])
        w_hi = sbuf(ctx, "w_hi", [P, 2, KT, COLS], F32R)
        w_lo = sbuf(ctx, "w_lo", [P, 2, KT, COLS], F32R)
        hT = sbuf(ctx, "hT", [P, DB, LEN])
        xT = hT[:, :, META:LEN]
        cols = sbuf(ctx, "cols", [P, 4 * P])
        const = sbuf(ctx, "const", [P, CONST_COLS])
        ones = sbuf(ctx, "ones", [P, P])
        eps = sbuf(ctx, "eps", [P, 1])
        mods = sbuf(ctx, "mods", [P, P])
        c_silu = sbuf(ctx, "c_silu", [P, DB])
        mod_room = sbuf(ctx, "mod_room", [P, 2, COLS])
        mod_acc, mod_sum = mod_room[:, 0], mod_room[:, 1]
        rms = sbuf(ctx, "rms", [P, LEN])
        PS = ctx.enter_context(nc.psum_tensor("PS", [P, 8, 512], F32))

        unit_loaded = [sem(f"unit_loaded{i}") for i in range(SLOTS)]
        slot_read = [sem(f"slot_read{i}") for i in range(SLOTS)]
        hi_ready = [sem(f"hi_ready{i}") for i in range(4)]
        parts_read = [sem(f"parts_read{i}") for i in range(4)]
        mod_step = sem("mod_step")
        mod_reduced = sem("mod_reduced")
        mod_seen = sem("mod_seen")
        mod_kept = sem("mod_kept")
        banks_free = [sem(f"banks_free{i}") for i in range(2)]
        freed = [0, 0]
        vec = Step(sem("vector_step"))
        act = Step(sem("scalar_step"))
        ten = Step(sem("tensor_step"))
        pool = Step(sem("pool_step"))
        whole_made = sem("whole_made")
        high_made = sem("high_made")
        low_made = [sem(f"low_made{i}") for i in range(2)]
        fed = [0, 0, 0, 0]
        small_loaded = sem("small_loaded")
        small = [0]
        stored = sem("stored")

        def const_of(name):
            first, n = CONST[name]
            return const[:, first:first + n]

        ident, after = const_of("identity"), const_of("after")

        def col(name, i, n=1):
            tile, row, rows = VECTOR_ROWS[name]
            assert i + n <= rows
            return cols[:, tile * P + row + i:tile * P + row + i + n]

        def load_small(eng, dst, src):
            small[0] += 16
            eng.dma_start(dst, src).then_inc(small_loaded, 16)

        def load_unit(sp, n):
            source, it, j = flat[n]
            if n >= SLOTS:
                sp.wait_ge(slot_read[n % SLOTS], 2 * (n // SLOTS))
            src = source(it, j)
            sp.dma_start(ring[:, n % SLOTS, :, 0:src.shape[2]], src).then_inc(unit_loaded[n % SLOTS], 16)

        def stream(sp, ph):
            first = ph.base + SLOTS
            if ph.iters > 1:
                for n in range(first, ph.base + ph.raw):
                    load_unit(sp, n)
                with sp.Fori(1, ph.iters) as it:
                    for r in range(ph.raw):
                        s = ph.slot_at(r)
                        sp.wait_ge(slot_read[s], 2 * ph.uses_at(it, r) - 2)
                        sp.dma_start(ring[:, s], round_unit(ph, it, r)).then_inc(unit_loaded[s], 16)
                first = ph.end
            for n in range(first, min(ph.end + SLOTS, len(flat))):
                load_unit(sp, n)

        def split_hi(a, ph, it, j):
            slot, b = ph.slot(j), j % 2
            a.wait_ge(unit_loaded[slot], 16 * ph.uses(it, j))
            for half in range(2):
                if not isinstance(it, int) or ph.fills(it, j) > 1:
                    a.wait_ge(parts_read[2 * b + half], ph.fills(it, j) - 1)
                k = slice(half * KT // 2, (half + 1) * KT // 2)
                nc.scalar.copy(w_hi[:, b, k], ring[:, slot, k]).then_inc(hi_ready[2 * b + half], 1)

        def split_lo(dve, ph, it, j):
            slot, b = ph.slot(j), j % 2
            for half in range(2):
                dve.wait_ge(hi_ready[2 * b + half], ph.fills(it, j))
                k = slice(half * KT // 2, (half + 1) * KT // 2)
                nc.vector.tensor_tensor(w_lo[:, b, k], ring[:, slot, k], w_hi[:, b, k].bitcast(F32), ALU.subtract).then_inc(slot_read[slot], 1)

        def wait_parts(pe, ph, it, j, kt):
            if kt % 2 == 0:
                pe.wait_ge(slot_read[ph.slot(j)], 2 * ph.uses(it, j) - 1 + kt // 2)

        def release_parts(mm, j, kt):
            if kt % 2 == 1:
                mm.then_inc(parts_read[2 * (j % 2) + kt // 2], 1)

        def prime(ph):
            with nc.Block() as block:
                @block.scalar
                def _(a):
                    for j in range(2):
                        split_hi(a, ph, 0, j)

                @block.vector
                def _(dve):
                    for j in range(2):
                        split_lo(dve, ph, 0, j)

        def mod_unit(dve, ph, it, i):
            r = 3 * i + 2
            slot = ph.slot_at(r)
            done = 16 * (it + ph.extra)
            dve.wait_ge(unit_loaded[slot], 16 * ph.uses_at(it, r))
            for kt in range(KT):
                k = i * KT + kt
                if k == 0:
                    if ph.extra > 0:
                        dve.wait_ge(mod_reduced, it + ph.extra)
                    last = nc.vector.tensor_scalar(mod_acc, ring[:, slot, kt], c_silu[:, k:k + 1], None, ALU.mult)
                else:
                    dve.wait_ge(mod_step, done + k)
                    last = nc.vector.scalar_tensor_tensor(mod_acc, ring[:, slot, kt], c_silu[:, k:k + 1], mod_acc,
                                                          ALU.mult, ALU.add)
                last.then_inc(mod_step, 1)
            dve.wait_ge(mod_step, done + (i + 1) * KT)
            dve.sem_inc(slot_read[slot], 2)

        def mod_reduce(g, ph, it):
            m = it + ph.extra
            g.wait_ge(mod_step, 16 * m + 16)
            if ph.extra > 0:
                g.wait_ge(mod_kept, 3 * m)
            g.sem_inc(mod_seen, 1)
            nc.gpsimd.partition_all_reduce(mod_sum, mod_acc, P, bass.bass_isa.ReduceOp.add).then_inc(mod_reduced, 1)

        def mod_keep(dve, ph, it):
            m = it + ph.extra
            dve.wait_ge(mod_reduced, m + 1)
            picked = mod_sum.rearrange("p (i c) -> p i c", i=MB)
            nc.vector.tensor_tensor(picked, picked, ident.unsqueeze(1).to_broadcast([P, MB, P]), ALU.mult).then_inc(mod_kept, 1)
            dve.wait_ge(mod_kept, 3 * m + 1)
            part = mods[:, m * MB:(m + 1) * MB] if isinstance(m, int) else mods[:, bass.ds(m * MB, MB)]
            nc.vector.reduce_sum(part, picked, AX).then_inc(mod_kept, 1)
            dve.wait_ge(mod_kept, 3 * m + 2)
            bias = cols[:, P + m * MB:P + (m + 1) * MB] if isinstance(m, int) else cols[:, bass.ds(m * MB + P, MB)]
            nc.vector.tensor_tensor(part, part, bias, ALU.add).then_inc(mod_kept, 1)

        def modulation_part(dve, ph, it, j):
            if ph.extra is not None and j % 2 == 0:
                mod_unit(dve, ph, it, j // 2 - 1)
            if ph.extra is not None and j == ph.upi + 1:
                mod_keep(dve, ph, it)

        def three_products(dst, b, kt, cols_of, x, start, stop):
            for i, (part, xi) in enumerate(((w_hi, 0), (w_hi, 1), (w_lo, 0))):
                mm = nc.tensor.matmul(dst, part[:, b, kt, cols_of], x[:, xi], start=(start and i == 0),
                                      stop=(stop and i == 2), skip_group_check=True)
            return mm

        def multiply(pe, ph, it, k_units, moving, free_per_slab, slabs, feed=None):
            for s in range(slabs):
                half = s % 2
                need = freed[half] + free_per_slab * (it * (slabs // 2) + s // 2)
                if not isinstance(it, int) or need > 0:
                    pe.wait_ge(banks_free[half], need)
                for ku in range(k_units):
                    j = s * k_units + ku
                    if feed is not None and s == 0:
                        feed.wait(pe, ku)
                    for kt in range(KT):
                        wait_parts(pe, ph, it, j, kt)
                        x = moving(ku * KT + kt)
                        for m in range(MB):
                            mm = three_products(PS[:, 4 * half + m, 0:x.shape[2]], j % 2, kt, slice(m * P, (m + 1) * P), x,
                                                ku == 0 and kt == 0, ku == k_units - 1 and kt == KT - 1)
                        release_parts(mm, j, kt)

        def wait_slab(eng, ph, it, s, k_units):
            j = (s + 1) * k_units - 1
            eng.wait_ge(parts_read[2 * (j % 2) + 1], ph.fills(it, j))

        def rounds(eng, ph, body, static=False):
            if ph.iters == 1 or static:
                for it in range(ph.iters):
                    body(it)
            else:
                with eng.Fori(0, ph.iters) as it:
                    body(it)

        def split_round(eng, split, ph, it, k_units, evacuate, last, between=None):
            for j in range(2, ph.upi + 2):
                if between is not None:
                    between(it, j)
                if j < ph.upi or not last:
                    split(eng, ph, it, j)
                if (j - 1) % k_units == 0 and evacuate is not None:
                    evacuate(it, (j - 1) // k_units - 1)

        def project(name, k_units, moving, width, on_vector, slabs=2, static=False, follows=True, feed=None):
            ph = phases[name]

            def ends(it):
                return not follows and it == ph.iters - 1

            with nc.Block() as block:
                @block.sync
                def _(sp):
                    stream(sp, ph)

                @block.tensor
                def _(pe):
                    rounds(pe, ph, lambda it: multiply(pe, ph, it, k_units, moving, 1, slabs, feed), static)

                @block.scalar
                def _(a):
                    if feed is not None:
                        feed.scalar(a)
                    rounds(a, ph, lambda it: split_round(a, split_hi, ph, it, k_units, None, ends(it)), static)

                @block.vector
                def _(dve):
                    def evacuate(it, s):
                        wait_slab(dve, ph, it, s, k_units)
                        half = s % 2
                        on_vector(it, s, PS[:, 4 * half:4 * half + 4, 0:width]).then_inc(banks_free[half], 1)

                    def between(it, j):
                        modulation_part(dve, ph, it, j)

                    def body(it):
                        split_round(dve, split_lo, ph, it, k_units, evacuate, ends(it), between)
                    if feed is not None:
                        feed.vector(dve)
                    rounds(dve, ph, body, static)

                @block.gpsimd
                def _(g):
                    if feed is not None:
                        feed.pool(g)
                    if ph.extra is not None:
                        rounds(g, ph, lambda it: mod_reduce(g, ph, it), static)
            for half in range(2):
                freed[half] += ph.iters * slabs // 2

        def project_pair(name, k_units, moving, on_scalar, on_vector, slabs=2, on_pool=None, feed=None):
            ph = phases[name]
            ready, taken = sem(f"{name}_ready"), sem(f"{name}_taken")
            with nc.Block() as block:
                @block.sync
                def _(sp):
                    stream(sp, ph)

                @block.tensor
                def _(pe):
                    rounds(pe, ph, lambda it: multiply(pe, ph, it, k_units, moving, 1, slabs, feed))

                @block.scalar
                def _(a):
                    if feed is not None:
                        feed.scalar(a)
                    a.sem_inc(taken, 1)
                    def evacuate(it, s):
                        wait_slab(a, ph, it, s, k_units)
                        on_scalar(a, it, s, ready, taken)
                    rounds(a, ph, lambda it: split_round(a, split_hi, ph, it, k_units, evacuate, False))

                @block.vector
                def _(dve):
                    def evacuate(it, s):
                        wait_slab(dve, ph, it, s, k_units)
                        on_vector(dve, it, s, ready, taken)

                    def between(it, j):
                        modulation_part(dve, ph, it, j)

                    def body(it):
                        split_round(dve, split_lo, ph, it, k_units, evacuate, False, between)
                    if feed is not None:
                        feed.vector(dve)
                    rounds(dve, ph, body)

                @block.gpsimd
                def _(g):
                    def body(it):
                        if ph.extra is not None:
                            mod_reduce(g, ph, it)
                        if on_pool is not None:
                            on_pool(g, it, taken)
                    if feed is not None:
                        feed.pool(g)
                    if on_pool is not None or ph.extra is not None:
                        rounds(g, ph, body)
            for half in range(2):
                freed[half] += ph.iters * slabs // 2

        def values_by_token(ph, block, x, v):
            @block.tensor
            def _(pe):
                with pe.Fori(0, ph.iters) as it:
                    for s in range(2):
                        pe.wait_ge(banks_free[s], freed[s] + it)
                        for ku in range(4):
                            j = 4 * s + ku
                            for kt in range(KT):
                                wait_parts(pe, ph, it, j, kt)
                                k = ku * KT + kt
                                for t in range(2):
                                    for i, (xi, part) in enumerate(((0, w_hi), (0, w_lo), (1, w_hi))):
                                        mm = nc.tensor.matmul(PS[:, 4 * s + t, :], x[:, k, xi, t * P:(t + 1) * P], part[:, j % 2, kt],
                                                              start=(k == 0 and i == 0), stop=(k == DB - 1 and i == 2))
                                release_parts(mm, j, kt)

            @block.scalar
            def _(a):
                with a.Fori(0, ph.iters) as it:
                    def evacuate(it, s):
                        wait_slab(a, ph, it, s, 4)
                        nc.scalar.copy(v[:, :, bass.ds(it * 2 * COLS + s * COLS, COLS)], PS[:, 4 * s:4 * s + 2, :]).then_inc(banks_free[s], 1)
                    split_round(a, split_hi, ph, it, 4, evacuate, False)

        def inverse_rms(src, blocks, width, squares):
            quarter = blocks // 4
            groups = [slice(q * quarter, (q + 1) * quarter) for q in range(4)]
            by_scalar = groups[:2]
            with nc.Block() as block:
                a0, v0, summed = act.value, vec.value, ten.value + 1

                @block.scalar
                def _(a):
                    for k in by_scalar:
                        act.tick(nc.scalar.activation(squares[:, k, 0:width], src[:, k], ACT.Square))
                    a.wait_ge(ten.sem, summed)
                    act.tick(nc.scalar.activation(rms[:, 0:width], PS[:, 0, 0:width], ACT.Sqrt,
                                                  scale=1.0 / (blocks * P), bias=eps[:, 0:1]))

                @block.tensor
                def _(pe):
                    for i, k in enumerate(by_scalar):
                        pe.wait_ge(vec.sem, v0 + 2 * i + 2)
                        for kk in range(k.start, k.stop):
                            mm = nc.tensor.matmul(PS[:, 0, 0:width], ones[:], squares[:, kk, 0:width],
                                                  start=(kk == 0), stop=(kk == by_scalar[-1].stop - 1))
                    ten.tick(mm)

                @block.vector
                def _(dve):
                    for i, (k, far) in enumerate(zip(by_scalar, groups[2:])):
                        n = vec.tick(nc.vector.tensor_tensor(squares[:, far, 0:width], src[:, far], src[:, far], ALU.mult))
                        dve.wait_ge(vec.sem, n)
                        dve.wait_ge(act.sem, a0 + i + 1)
                        vec.tick(nc.vector.tensor_tensor(squares[:, k, 0:width], squares[:, k, 0:width],
                                                         squares[:, far, 0:width], ALU.add))
                    dve.wait_ge(act.sem, a0 + len(by_scalar) + 1)
                    vec.tick(nc.vector.reciprocal(rms[:, 0:width], rms[:, 0:width]))

        def scale_tokens(dst, src, blocks, width, gain):
            with nc.Block() as block:
                @block.vector
                def _(dve):
                    for k in range(blocks):
                        vec.tick(nc.vector.scalar_tensor_tensor(dst[:, k], src[:, k], gain[:, k:k + 1], rms[:, 0:width],
                                                                ALU.mult, ALU.mult))

        def feed_parts(groups, make=None, prologue=()):
            whole0, high0, low0 = fed[0], fed[1], (fed[2], fed[3])

            def low(eng, engine, q):
                hi, lo, src = groups[q]
                eng.wait_ge(high_made, high0 + q + 1)
                engine.tensor_tensor(lo, src, hi.bitcast(F32), ALU.subtract).then_inc(low_made[q % 2], 1)

            def wait_low(eng, q):
                eng.wait_ge(low_made[q % 2], low0[q % 2] + q // 2 + 1)

            def vector(dve):
                for op in prologue:
                    dve.wait_ge(vec.sem, vec.tick(op()))
                for q in range(len(groups)):
                    if make is not None:
                        if q >= 2:
                            wait_low(dve, q - 2)
                        make(dve, q).then_inc(whole_made, 1)
                    if q % 2 == 1:
                        low(dve, nc.vector, q - 1)
                if len(groups) % 2 == 1:
                    low(dve, nc.vector, len(groups) - 1)

            def scalar(a):
                for q, (hi, lo, src) in enumerate(groups):
                    if make is not None:
                        a.wait_ge(whole_made, whole0 + q + 1)
                    nc.scalar.copy(hi, src).then_inc(high_made, 1)

            def pool_part(g):
                for q in range(1, len(groups), 2):
                    low(g, nc.gpsimd, q)

            if make is not None:
                fed[0] += len(groups)
            fed[1] += len(groups)
            fed[2] += (len(groups) + 1) // 2
            fed[3] += len(groups) // 2
            return Feed(vector, scalar, pool_part, wait_low)

        def feed_scaled(dst, src, blocks, width, gain, room, shift=None, prologue=()):
            whole = room.rearrange("p (b i) t -> p b i t", b=2)

            def make(dve, q):
                for i in range(MB):
                    k = q * MB + i
                    last = nc.vector.scalar_tensor_tensor(whole[:, q % 2, i, 0:width], src[:, k], gain[:, k:k + 1],
                                                          rms[:, 0:width], ALU.mult, ALU.mult)
                    if shift is not None:
                        vec.tick(last)
                if shift is None:
                    return last
                dve.wait_ge(vec.sem, vec.value)
                return nc.vector.tensor_tensor(whole[:, q % 2, :, 0:width], whole[:, q % 2, :, 0:width],
                                               shift[:, q * MB:(q + 1) * MB].unsqueeze(2).to_broadcast([P, MB, width]), ALU.add)

            groups = []
            for q in range(blocks // MB):
                part = dst[:, q * MB:(q + 1) * MB]
                groups.append((part[:, :, 0], part[:, :, 1], whole[:, q % 2, :, 0:width]))
            return feed_parts(groups, make, prologue)

        def feed_split(dst, src, blocks):
            return feed_parts([(dst[:, k:k + KT, 0], dst[:, k:k + KT, 1], src[:, k:k + KT]) for k in range(0, blocks, KT)])

        def small_ops(ops):
            with nc.Block() as block:
                @block.vector
                def _(dve):
                    for op in ops:
                        dve.wait_ge(vec.sem, vec.tick(op()))

        def attention(name, heads, scores_of, keys_of, bias_of, scale, v, o):
            items = 2 * heads
            TURN, VALUE, KEEP = 2, 3, 4
            scored, turned, valued = (sem(f"{name}_{x}") for x in ("scored", "turned", "valued"))
            biased, shifted, exped, normed = (sem(f"{name}_{x}") for x in ("biased", "shifted", "exped", "normed"))
            copied, kept, maxed, inverted = (sem(f"{name}_{x}") for x in ("copied", "kept", "maxed", "inverted"))
            with ExitStack() as scope:
                S = sbuf(scope, "S", [P, 2, LEN])
                Pr = sbuf(scope, "Pr", [P, 3, LEN])
                PT = sbuf(scope, "PT", [P, 2, 3, P])
                mx = sbuf(scope, "mx", [P, 3, 4])
                with nc.Block() as block:
                    @block.tensor
                    def _(pe):
                        for n in range(items + VALUE):
                            if n < items:
                                if n >= 3:
                                    pe.wait_ge(biased, n - 2)
                                pairs = scores_of(n)
                                for i, (lhsT, rhs) in enumerate(pairs):
                                    mm = nc.tensor.matmul(PS[:, n % 3, 0:keys_of(n)], lhsT, rhs,
                                                          start=(i == 0), stop=(i == len(pairs) - 1))
                                mm.then_inc(scored, 1)
                            t = n - TURN
                            if 0 <= t < items:
                                pe.wait_ge(normed, t + 1)
                                if t >= 2:
                                    pe.wait_ge(copied, t - 1)
                                for k0 in range(0, keys_of(t), P):
                                    kn = min(P, keys_of(t) - k0)
                                    mm = nc.tensor.transpose(PS[0:kn, 3 + t % 2, k0:k0 + P], Pr[:, t % 3, k0:k0 + kn], ident)
                                mm.then_inc(turned, 1)
                            r = n - VALUE
                            if 0 <= r < items:
                                pe.wait_ge(copied, r + 1)
                                if r >= 2:
                                    pe.wait_ge(kept, r - 1)
                                kts = -(-keys_of(r) // P)
                                for kt in range(kts):
                                    kn = min(P, keys_of(r) - kt * P)
                                    mm = nc.tensor.matmul(PS[:, 5 + r % 2, 0:P], v[0:kn, kt, (r // 2) * P:(r // 2 + 1) * P],
                                                          PT[0:kn, r % 2, kt], start=(kt == 0), stop=(kt == kts - 1))
                                mm.then_inc(valued, 1)

                    @block.vector
                    def _(dve):
                        for n in range(items + KEEP):
                            t, r = n - 1, n - KEEP
                            front, back = n < items, 0 <= t < items
                            b, c = n % 3, t % 3
                            if front:
                                nk = keys_of(n)
                                dve.wait_ge(scored, n + 1)
                                if n >= 2:
                                    dve.wait_ge(exped, n - 1)
                                nc.vector.scalar_tensor_tensor(S[:, n % 2, 0:nk], PS[:, n % 3, 0:nk], scale, bias_of(n),
                                                               ALU.mult, ALU.add).then_inc(biased, 1)
                            if back:
                                dve.wait_ge(exped, t + 1)
                                nc.vector.reciprocal(mx[:, c, 3:4], mx[:, c, 2:3]).then_inc(inverted, 1)
                            if front:
                                dve.wait_ge(biased, n + 1)
                                if n >= 3:
                                    dve.wait_ge(normed, n - 2)
                                nc.vector.reduce_max(mx[:, b, 0:1], S[:, n % 2, 0:nk], AX).then_inc(maxed, 1)
                            if back:
                                dve.wait_ge(inverted, t + 1)
                                nc.vector.tensor_scalar(Pr[:, c, 0:keys_of(t)], Pr[:, c, 0:keys_of(t)], mx[:, c, 3:4], None,
                                                        ALU.mult).then_inc(normed, 1)
                            if front:
                                dve.wait_ge(maxed, n + 1)
                                nc.vector.tensor_scalar(mx[:, b, 1:2], mx[:, b, 0:1], -1.0, None, ALU.mult).then_inc(shifted, 1)
                            if 0 <= r < items:
                                dve.wait_ge(valued, r + 1)
                                nc.vector.tensor_copy(o[:, r // 2, (r % 2) * P:(r % 2 + 1) * P],
                                                      PS[:, 5 + r % 2, 0:P]).then_inc(kept, 1)

                    @block.scalar
                    def _(a):
                        for n in range(items + TURN):
                            t = n - TURN
                            if 0 <= t < items:
                                a.wait_ge(turned, t + 1)
                                if t >= 2:
                                    a.wait_ge(valued, t - 1)
                                nk, b = keys_of(t), t % 2
                                full, rest = nk // P, nk % P
                                last = nc.scalar.copy(PT[:, b, 0:full], PS[:, 3 + b, 0:full * P].rearrange("p (k q) -> p k q", q=P))
                                if rest:
                                    last = nc.scalar.copy(PT[0:rest, b, full], PS[0:rest, 3 + b, full * P:(full + 1) * P])
                                last.then_inc(copied, 1)
                            if n < items:
                                nk, b = keys_of(n), n % 3
                                a.wait_ge(shifted, n + 1)
                                if n >= 3:
                                    a.wait_ge(turned, n - 2)
                                nc.scalar.activation(Pr[:, b, 0:nk], S[:, n % 2, 0:nk], ACT.Exp, bias=mx[:, b, 1:2],
                                                     accum_out=mx[:, b, 2:3]).then_inc(exped, 1)

        with ExitStack() as scope:
            x_rows = sbuf(scope, "x_rows", [P, 2, D])
            meta_rows = sbuf(scope, "meta_rows", [META, D])
            vec_rows = sbuf(scope, "vec_rows", [P, 4, P])
            with nc.Block() as block:
                turned, copied, vectors_loaded = sem("input_turned"), sem("input_copied"), sem("vectors_loaded")

                @block.sync
                def _(sp):
                    load_small(sp, const[:], w["shape_constants"])
                    load_small(sp, x_rows[:], w["x"].rearrange("(t p) d -> p t d", p=P))
                    load_small(sp, meta_rows[:], w["meta_tokens"])
                    for n in range(SLOTS):
                        load_unit(sp, n)

                @block.gpsimd
                def _(g):
                    nc.gpsimd.memset(ones[:], 1.0)
                    nc.gpsimd.memset(eps[:], EPS)

                @block.scalar
                def _(a):
                    for name, (tile, row, rows) in VECTOR_ROWS.items():
                        a.dma_start(vec_rows[row:row + rows, tile], w[name + "_rows"]).then_inc(vectors_loaded, 16)
                    a.wait_ge(copied, 10)
                    n = act.tick(nc.scalar.activation(c_silu[:], col("c_2", 0, DB), ACT.Sigmoid))

                groups = [("x", i) for i in range(8)] + [("meta", None), ("vector", None)]

                @block.tensor
                def _(pe):
                    pe.wait_ge(small_loaded, 16 * 3)
                    for n, (kind, i) in enumerate(groups):
                        if n >= 4:
                            pe.wait_ge(copied, n - 3)
                        if kind == "vector":
                            pe.wait_ge(vectors_loaded, 16 * len(VECTOR_ROWS))
                            for t in range(4):
                                r = VECTOR_TILE_ROWS[t]
                                mm = nc.tensor.transpose(PS[:, n % 4, t * P:t * P + r], vec_rows[0:r, t], ident[0:r, 0:r])
                        elif kind == "x":
                            for q in range(4):
                                k = (i % 4) * 4 + q
                                mm = nc.tensor.transpose(PS[:, n % 4, q * P:(q + 1) * P],
                                                         x_rows[:, i // 4, k * P:(k + 1) * P], ident)
                        else:
                            for k in range(DB):
                                mm = nc.tensor.transpose(PS[:, n % 4, k * META:(k + 1) * META],
                                                         meta_rows[:, k * P:(k + 1) * P], ident[0:META, 0:META])
                        mm.then_inc(turned, 1)

                @block.vector
                def _(dve):
                    for n, (kind, i) in enumerate(groups):
                        dve.wait_ge(turned, n + 1)
                        if kind == "vector":
                            nc.vector.tensor_copy(cols[:, 0:480], PS[:, n % 4, 0:480]).then_inc(copied, 1)
                        elif kind == "x":
                            nc.vector.tensor_copy(
                                hT[:, (i % 4) * 4:(i % 4) * 4 + 4, META + (i // 4) * P:META + (i // 4 + 1) * P],
                                PS[:, n % 4, :].rearrange("p (k t) -> p k t", k=4)).then_inc(copied, 1)
                        else:
                            nc.vector.tensor_copy(hT[:, :, 0:META],
                                                  PS[:, n % 4, 0:DB * META].rearrange("p (k t) -> p k t", k=DB)).then_inc(copied, 1)

        small_ops([lambda: nc.vector.tensor_tensor(c_silu[:], c_silu[:], col("c_2", 0, DB), ALU.mult)])
        prime(phases["latents"])

        with ExitStack() as one:
            kT = sbuf(one, "kT", [P, HEADS, LEN])
            attn_out = kT[:, :, 0:SEQ]
            uT = sbuf(one, "uT", [P, SSM_W // P, LEN])
            with ExitStack() as scope:
                const_one = sbuf(scope, "const_one", [P, 3 * LEN])
                cosT, sinT, causal = (const_one[:, first:first + n] for first, n in CONST_ONE.values())
                latent = sbuf(scope, "latent", [P, 8, LEN])
                k_rope = sbuf(scope, "k_rope", [P, LEN])
                qT = sbuf(scope, "qT", [P, HEADS, SEQ])
                swapped = sbuf(scope, "swapped", [P, 2, LEN])
                with nc.Block() as block:
                    @block.sync
                    def _(sp):
                        load_small(sp, const_one[:], w["shape_constants_one"])

                def rotate(dve, dst, ps, first, width):
                    for q, r in ((0, 1), (1, 0), (2, 3), (3, 2)):
                        last = nc.vector.tensor_copy(swapped[32 * q:32 * q + 32, 0, 0:width], ps[32 * r:32 * r + 32])
                        vec.tick(last)
                    dve.wait_ge(vec.sem, vec.value)
                    vec.tick(nc.vector.tensor_tensor(swapped[:, 0, 0:width], swapped[:, 0, 0:width],
                                                     sinT[:, first:first + width], ALU.mult))
                    last = nc.vector.tensor_tensor(swapped[:, 1, 0:width], ps, cosT[:, first:first + width], ALU.mult)
                    dve.wait_ge(vec.sem, vec.tick(last))
                    last = nc.vector.tensor_tensor(dst, swapped[:, 0, 0:width], swapped[:, 1, 0:width], ALU.add)
                    dve.wait_ge(vec.sem, vec.tick(last))

                with ExitStack() as normed:
                    nT = sbuf(normed, "nT", [P, DB, 2, LEN], F32R)
                    kr_whole = qT[:, 0:DB // 2, :].rearrange("p k t -> p (k t)").rearrange("p (k a b) -> p k a b", k=DB, a=2)
                    kr_hi = sbuf(normed, "kr_hi", [P, DB, 2 * ROPE], F32R)
                    kr_lo = sbuf(normed, "kr_lo", [P, DB, 2 * ROPE], F32R)
                    with nc.Block() as block:
                        @block.sync
                        def _(sp):
                            for half in range(2):
                                load_small(sp, kr_whole[:, :, half], w["w_in"][:, OFF_KR:OFF_U].rearrange("(k p) n -> p k n", p=P))
                    inverse_rms(hT, DB, LEN, kT)
                    project("latents", 4, lambda k: nT[:, k], LEN,
                            lambda it, s, ps: nc.vector.tensor_copy(latent[:, 4 * s:4 * s + 4], ps),
                            feed=feed_scaled(nT, hT, DB, LEN, col("norm_mix", 0, DB), kT[:, 0:8]))
                    project("u", 4, lambda k: nT[:, k], LEN,
                            lambda it, s, ps: nc.vector.tensor_copy(uT[:, 4 * s:4 * s + 4], ps))

                    with nc.Block() as block:
                        @block.sync
                        def _(sp):
                            sp.wait_ge(small_loaded, small[0])
                    with nc.Block() as block:
                        kr_done, a0, v0 = ten.value + 1, act.value, vec.value
                        flat_kr = kr_whole.rearrange("p k a b -> p k (a b)")

                        @block.scalar
                        def _(a):
                            act.tick(nc.scalar.copy(kr_hi[:], flat_kr))

                        @block.tensor
                        def _(pe):
                            pe.wait_ge(vec.sem, v0 + 1)
                            for k in range(DB):
                                for i, (part, xi) in enumerate(((kr_hi, 0), (kr_hi, 1), (kr_lo, 0))):
                                    mm = nc.tensor.matmul(PS[:, 0, 0:LEN], part[:, k], nT[:, k, xi],
                                                          start=(k == 0 and i == 0), stop=(k == DB - 1 and i == 2))
                            ten.tick(mm)

                        @block.vector
                        def _(dve):
                            dve.wait_ge(act.sem, a0 + 1)
                            vec.tick(nc.vector.tensor_tensor(kr_lo[:], flat_kr, kr_hi[:].bitcast(F32), ALU.subtract))
                            dve.wait_ge(ten.sem, kr_done)
                            rotate(dve, k_rope[:], PS[:, 0, 0:LEN], 0, LEN)

                heads_done = scope.enter_context(ExitStack())
                q_rope = sbuf(heads_done, "q_rope", [P, HEADS // 2, SEQ])
                v = sbuf(heads_done, "v", [P, 3, D])
                with ExitStack() as inner:
                    q_parts = sbuf(inner, "q_parts", [P, 4, 2, SEQ], F32R)
                    kv_parts = sbuf(inner, "kv_parts", [P, 4, 2, 3 * P], F32R)
                    rms_latent = sbuf(inner, "rms_latent", [P, 2, LEN])
                    with nc.Block() as block:
                        a0, v0, t0, pad = act.value, vec.value, ten.value, 3 * P - LEN
                        halves = tuple(latent[:, 4 * i:4 * i + 4] for i in range(2))
                        pieces = ((q_parts, slice(0, SEQ), halves[0][:, :, META:LEN], 0),
                                  (kv_parts, slice(0, LEN), halves[1], 1),
                                  (kv_parts, slice(LEN, 3 * P), halves[1][:, :, 0:pad], 1))

                        @block.scalar
                        def _(a):
                            for i in range(2):
                                act.tick(nc.scalar.activation(kT[:, 4 * i:4 * i + 4], halves[i], ACT.Square))
                            for i in range(2):
                                a.wait_ge(ten.sem, t0 + i + 1)
                                act.tick(nc.scalar.activation(rms_latent[:, i], PS[:, i, 0:LEN], ACT.Sqrt,
                                                              scale=1.0 / LORA, bias=eps[:, 0:1]))
                            for dst, t, src, i in pieces:
                                a.wait_ge(vec.sem, v0 + 5 * (i + 1))
                                act.tick(nc.scalar.copy(dst[:, :, 0, t], src))

                        @block.tensor
                        def _(pe):
                            for i in range(2):
                                pe.wait_ge(act.sem, a0 + i + 1)
                                for k in range(4):
                                    mm = nc.tensor.matmul(PS[:, i, 0:LEN], ones[:], kT[:, 4 * i + k], start=(k == 0), stop=(k == 3))
                                ten.tick(mm)

                        @block.vector
                        def _(dve):
                            for i, gain in enumerate(("norm_q", "norm_kv")):
                                dve.wait_ge(act.sem, a0 + 3 + i)
                                dve.wait_ge(vec.sem, vec.tick(nc.vector.reciprocal(rms_latent[:, i], rms_latent[:, i])))
                                for k in range(4):
                                    vec.tick(nc.vector.scalar_tensor_tensor(halves[i][:, k], halves[i][:, k], col(gain, k), rms_latent[:, i],
                                                                            ALU.mult, ALU.mult))
                            dve.wait_ge(vec.sem, vec.value)
                            for n, (dst, t, src, i) in enumerate(pieces):
                                dve.wait_ge(act.sem, a0 + 5 + n)
                                vec.tick(nc.vector.tensor_tensor(dst[:, :, 1, t], src, dst[:, :, 0, t].bitcast(F32), ALU.subtract))

                    ph = phases["q_up"]
                    with nc.Block() as block:
                        q_free, q_rope_free = sem("q_free"), sem("q_rope_free")

                        @block.sync
                        def _(sp):
                            stream(sp, ph)

                        @block.tensor
                        def _(pe):
                            for j in range(8):
                                if j >= 4:
                                    pe.wait_ge(q_free, j - 3)
                                    pe.wait_ge(q_rope_free, j - 3)
                                for kt in range(KT):
                                    wait_parts(pe, ph, 0, j, kt)
                                    for m in range(3):
                                        mm = three_products(PS[:, 2 * (j % 4) + m // 2, (m % 2) * SEQ:(m % 2 + 1) * SEQ],
                                                            j % 2, kt, slice(m * P, (m + 1) * P), q_parts[:, kt],
                                                            kt == 0 and m != 1, kt == KT - 1)
                                    release_parts(mm, j, kt)

                        @block.scalar
                        def _(a):
                            def evacuate(it, j):
                                wait_slab(a, ph, 0, j, 1)
                                nc.scalar.copy(qT[:, 2 * j:2 * j + 2], PS[:, 2 * (j % 4), :].rearrange("p (m t) -> p m t", m=2)).then_inc(q_free, 1)
                            split_round(a, split_hi, ph, 0, 1, evacuate, False)

                        @block.vector
                        def _(dve):
                            def evacuate(it, j):
                                wait_slab(dve, ph, 0, j, 1)
                                rotate(dve, q_rope[:, j], PS[:, 2 * (j % 4) + 1, 0:SEQ], META, SEQ)
                                dve.sem_inc(q_rope_free, 1)
                            split_round(dve, split_lo, ph, 0, 1, evacuate, False)

                    ph_kv = phases["kv_up"]
                    with nc.Block() as block:
                        k_free, v_free = sem("k_free"), sem("v_free")

                        @block.sync
                        def _(sp):
                            stream(sp, ph_kv)

                        @block.tensor
                        def _(pe):
                            for j in range(8):
                                bank = 4 * (j % 2)
                                if j >= 2:
                                    pe.wait_ge(k_free, j - 1)
                                    pe.wait_ge(v_free, j - 1)
                                for kt in range(KT):
                                    wait_parts(pe, ph_kv, 0, j, kt)
                                    for m in range(2):
                                        three_products(PS[:, bank + m, 0:LEN], j % 2, kt, slice(2 * m * P, (2 * m + 1) * P),
                                                       kv_parts[:, kt, :, 0:LEN], kt == 0, kt == KT - 1)
                                    for t in range(3):
                                        for i, (xi, part) in enumerate(((0, w_hi), (0, w_lo), (1, w_hi))):
                                            both = part[:, j % 2, kt].rearrange("p (h c) -> p h c", h=2)[:, :, NOPE:]
                                            mm = nc.tensor.matmul(
                                                PS[:, bank + 2 + t // 2, (t % 2) * 256:(t % 2) * 256 + 256],
                                                kv_parts[:, kt, xi, t * P:(t + 1) * P], both,
                                                start=(kt == 0 and i == 0 and t % 2 == 0), stop=(kt == KT - 1 and i == 2),
                                                skip_group_check=True)
                                    release_parts(mm, j, kt)

                        @block.scalar
                        def _(a):
                            def evacuate(it, j):
                                wait_slab(a, ph_kv, 0, j, 1)
                                nc.scalar.copy(kT[:, 2 * j:2 * j + 2], PS[:, 4 * (j % 2):4 * (j % 2) + 2, 0:LEN]).then_inc(k_free, 1)
                            split_round(a, split_hi, ph_kv, 0, 1, evacuate, False)

                        @block.vector
                        def _(dve):
                            def evacuate(it, j):
                                bank = 4 * (j % 2)
                                wait_slab(dve, ph_kv, 0, j, 1)
                                nc.vector.tensor_copy(v[0:META, 2, j * 256:(j + 1) * 256], PS[0:META, bank + 3, 0:256])
                                nc.vector.tensor_copy(v[:, 0:2, j * 256:(j + 1) * 256],
                                                      PS[:, bank + 2, :].rearrange("p (t c) -> p t c", t=2)).then_inc(v_free, 1)
                            split_round(dve, split_lo, ph_kv, 0, 1, evacuate, False)

                def mla_keys(n):
                    return META + P * (n % 2 + 1)

                def mla_scores(n):
                    h, b = n // 2, n % 2
                    r = 64 * (h % 2)
                    nk = mla_keys(n)
                    return [(qT[:, h, b * P:(b + 1) * P], kT[:, h, 0:nk]),
                            (q_rope[r:r + 64, h // 2, b * P:(b + 1) * P], k_rope[r:r + 64, 0:nk])]

                attention("mla", HEADS, mla_scores, mla_keys, lambda n: causal[:, LEN - mla_keys(n):LEN],
                          (NOPE + ROPE) ** -0.5, v, qT)
                heads_done.close()
                o_parts = sbuf(scope, "o_parts", [P, HEADS, 2, SEQ], F32R)
                project("attn_proj", 4, lambda k: o_parts[:, k], SEQ,
                        lambda it, s, ps: nc.vector.tensor_copy(attn_out[:, bass.ds(it * 8 + 4 * s, 4)], ps),
                        feed=feed_split(o_parts, qT, HEADS))

            TILES = G // 2
            UB = SSM_W // P
            SPAN = LEN // 4
            LEVELS = 7
            assert 2 ** (LEVELS - 1) < SPAN <= 2 ** LEVELS and SPAN == 64 + 4
            with ExitStack() as scope:
                y = uT[:, :, META:LEN]
                BT = sbuf(scope, "BT", [P, UB, 2, P])
                CT = sbuf(scope, "CT", [P, UB, 2, P])
                mag = sbuf(scope, "mag", [P, TILES])
                powers = sbuf(scope, "powers", [P, 2, LEVELS, TILES])
                carry = sbuf(scope, "carry", [P, 3, TILES])
                with ExitStack() as prep:
                    row = sbuf(prep, "row", [TILES, 16, P])
                    steps = sbuf(prep, "steps", [TILES, 2])
                    turns = sbuf(prep, "turns", [TILES, P], I32)
                    b_in = sbuf(prep, "b_in", [P, 2, TILES, C])
                    c_in = sbuf(prep, "c_in", [P, 2, UB, P])
                    coef = sbuf(prep, "coef", [P, 2, TILES])
                    prod = sbuf(prep, "prod", [P, 4, TILES, C])
                    b_pad = sbuf(prep, "b_pad", [P, 2, TILES, 2 * C])
                    LR, LI, ST, ANG, MAG, SIN, COS, NR, T0, T1, DEN, CR, CI, HALF = range(14)
                    two_pi_hi, two_pi_lo = 6.28125, 0.0019353071795864769
                    with nc.Block() as block:
                        base = small[0]
                        c_loaded = sem("ssm_c_loaded")
                        zeroed = pool.value + 2

                        @block.gpsimd
                        def _(g):
                            pool.tick(nc.gpsimd.memset(c_in[:], 0.0))
                            pool.tick(nc.gpsimd.memset(b_pad[:], 0.0))

                        @block.sync
                        def _(sp):
                            load_small(sp, row[:, LR], w["ssm_lambda_re"].rearrange("(r c) n -> r (c n)", c=2))
                            load_small(sp, row[:, LI], w["ssm_lambda_im"].rearrange("(r c) n -> r (c n)", c=2))
                            load_small(sp, steps[:], w["ssm_log_step"].rearrange("(r c) -> r c", c=2))
                            for i, name in enumerate(("ssm_b_re", "ssm_b_im")):
                                load_small(sp, b_in[:, i], w[name].rearrange("(t c) n p -> (c n) t p", c=2))
                            sp.wait_ge(pool.sem, zeroed)
                            for i, name in enumerate(("ssm_c_re", "ssm_c_im")):
                                src = w[name].rearrange("(j g) p n -> g p j n", g=8)
                                for g8 in range(8):
                                    sp.dma_start(c_in[16 * g8:16 * g8 + 16, i, :, 64 * (g8 % 2):64 * (g8 % 2) + 64],
                                                 src[g8]).then_inc(c_loaded, 16)
                        in_loaded = base + 16 * 5
                        stepped, phased, ready = sem("ssm_stepped"), sem("ssm_phased"), sem("ssm_ready")
                        turned, copied, padded = sem("ssm_turned"), sem("ssm_copied"), sem("ssm_padded")

                        @block.scalar
                        def _(a):
                            a.wait_ge(small_loaded, in_loaded)
                            nc.scalar.activation(steps[:], steps[:], ACT.Exp).then_inc(stepped, 1)
                            a.wait_ge(phased, 1)
                            act.tick(nc.scalar.activation(row[:, MAG], row[:, T0], ACT.Exp))
                            act.tick(nc.scalar.activation(row[:, SIN], row[:, ANG], ACT.Sin))
                            nc.scalar.activation(row[:, HALF], row[:, ANG], ACT.Sin, scale=0.5).then_inc(stepped, 1)
                            for n in range(8):
                                a.wait_ge(turned, 2 + n)
                                src = PS[:, 1 + n % 2, :]
                                nc.scalar.copy(BT[:, n], src[:, 0:256].rearrange("p (a b) -> p a b", a=2))
                                nc.scalar.copy(CT[:, n, 0], src[:, 256:384])
                                nc.scalar.mul(CT[:, n, 1], src[:, 384:512], -1.0).then_inc(copied, 1)

                        @block.vector
                        def _(dve):
                            def link(instruction):
                                dve.wait_ge(vec.sem, vec.tick(instruction))

                            def tt(o, i0, i1, op):
                                link(nc.vector.tensor_tensor(o, i0, i1, op))

                            dve.wait_ge(stepped, 1)
                            for c2 in range(2):
                                link(nc.vector.tensor_copy(row[:, ST, c2 * N:(c2 + 1) * N], steps[:, c2:c2 + 1].to_broadcast([TILES, N])))
                            tt(row[:, T0], row[:, LR], row[:, ST], ALU.mult)
                            tt(row[:, ANG], row[:, LI], row[:, ST], ALU.mult)
                            link(nc.vector.tensor_scalar(turns[:], row[:, ANG], 1.0 / 6.283185307179586, None, ALU.mult))
                            link(nc.vector.tensor_copy(row[:, T1], turns[:]))
                            for part in (two_pi_hi, two_pi_lo):
                                link(nc.vector.scalar_tensor_tensor(row[:, ANG], row[:, T1], -part, row[:, ANG], ALU.mult, ALU.add))
                            link(nc.vector.tensor_scalar(row[:, T1], row[:, ANG], 3.1415925, 6.283185307179586, ALU.is_gt, ALU.mult))
                            tt(row[:, ANG], row[:, ANG], row[:, T1], ALU.subtract)
                            link(nc.vector.tensor_scalar(row[:, T1], row[:, ANG], -3.1415925, 6.283185307179586, ALU.is_lt, ALU.mult))
                            tt(row[:, ANG], row[:, ANG], row[:, T1], ALU.add)
                            link(nc.vector.tensor_scalar(row[:, ANG], row[:, ANG], 3.1415925, -3.1415925, ALU.min, ALU.max))
                            dve.sem_inc(phased, 1)
                            dve.wait_ge(stepped, 2)
                            tt(row[:, T1], row[:, HALF], row[:, HALF], ALU.mult)
                            link(nc.vector.tensor_scalar(row[:, COS], row[:, T1], -2.0, 1.0, ALU.mult, ALU.add))
                            tt(row[:, T0], row[:, MAG], row[:, COS], ALU.mult)
                            link(nc.vector.tensor_scalar(row[:, NR], row[:, T0], -1.0, None, ALU.add))
                            tt(row[:, T0], row[:, MAG], row[:, SIN], ALU.mult)
                            tt(row[:, T1], row[:, LR], row[:, LR], ALU.mult)
                            tt(row[:, DEN], row[:, LI], row[:, LI], ALU.mult)
                            tt(row[:, DEN], row[:, DEN], row[:, T1], ALU.add)
                            link(nc.vector.reciprocal(row[:, DEN], row[:, DEN]))
                            tt(row[:, CR], row[:, NR], row[:, LR], ALU.mult)
                            tt(row[:, T1], row[:, T0], row[:, LI], ALU.mult)
                            tt(row[:, CR], row[:, CR], row[:, T1], ALU.add)
                            tt(row[:, CR], row[:, CR], row[:, DEN], ALU.mult)
                            tt(row[:, CI], row[:, T0], row[:, LR], ALU.mult)
                            tt(row[:, T1], row[:, NR], row[:, LI], ALU.mult)
                            tt(row[:, CI], row[:, CI], row[:, T1], ALU.subtract)
                            tt(row[:, CI], row[:, CI], row[:, DEN], ALU.mult)
                            dve.sem_inc(ready, 1)
                            dve.wait_ge(turned, 1)
                            vec.tick(nc.vector.tensor_copy(mag[:], PS[:, 0, 0:32]))
                            vec.tick(nc.vector.tensor_copy(powers[:, :, 0], PS[:, 0, 32:96].rearrange("p (a t) -> p a t", a=2)))
                            link(nc.vector.tensor_copy(coef[:], PS[:, 0, 96:160].rearrange("p (a t) -> p a t", a=2)))
                            bc = [coef[:, i].unsqueeze(2).to_broadcast([P, TILES, C]) for i in range(2)]
                            tt(prod[:, 0], b_in[:, 0], bc[0], ALU.mult)
                            tt(prod[:, 1], b_in[:, 1], bc[1], ALU.mult)
                            tt(prod[:, 2], b_in[:, 1], bc[0], ALU.mult)
                            tt(prod[:, 3], b_in[:, 0], bc[1], ALU.mult)
                            dve.wait_ge(pool.sem, zeroed)
                            for hf in range(2):
                                r = slice(64 * hf, 64 * hf + 64)
                                c = slice(C * hf, C * hf + C)
                                vec.tick(nc.vector.tensor_tensor(b_pad[r, 0, :, c], prod[r, 0], prod[r, 1], ALU.subtract))
                                link(nc.vector.tensor_tensor(b_pad[r, 1, :, c], prod[r, 2], prod[r, 3], ALU.add))
                            dve.sem_inc(padded, 1)
                            for k in range(LEVELS - 1):
                                re, im = powers[:, 0, k], powers[:, 1, k]
                                re2, im2 = powers[:, 0, k + 1], powers[:, 1, k + 1]
                                t0, t1 = prod[:, 0, :, 0], prod[:, 0, :, 1]
                                tt(t0, re, re, ALU.mult)
                                tt(t1, im, im, ALU.mult)
                                tt(re2, t0, t1, ALU.subtract)
                                tt(t0, re, im, ALU.mult)
                                link(nc.vector.tensor_scalar(im2, t0, 2.0, None, ALU.mult))
                            (re4, im4), (re64, im64) = ((powers[:, 0, k], powers[:, 1, k]) for k in (2, 6))
                            tt(t0, re4, re64, ALU.mult)
                            tt(t1, im4, im64, ALU.mult)
                            tt(carry[:, 0], t0, t1, ALU.subtract)
                            tt(carry[:, 0], carry[:, 0], mag[:], ALU.mult)
                            tt(t0, re4, im64, ALU.mult)
                            tt(t1, im4, re64, ALU.mult)
                            tt(carry[:, 2], t0, t1, ALU.add)
                            tt(carry[:, 2], carry[:, 2], mag[:], ALU.mult)
                            link(nc.vector.tensor_scalar(carry[:, 1], carry[:, 2], -1.0, None, ALU.mult))

                        @block.tensor
                        def _(pe):
                            pe.wait_ge(ready, 1)
                            for i, r in enumerate((MAG, COS, SIN, CR, CI)):
                                mm = nc.tensor.transpose(PS[:, 0, 32 * i:32 * i + 32], row[:, r], ident[0:TILES, 0:TILES])
                            mm.then_inc(turned, 1)
                            pe.wait_ge(padded, 1)
                            pe.wait_ge(c_loaded, 16 * 16)
                            for n in range(8):
                                if n >= 2:
                                    pe.wait_ge(copied, n - 1)
                                for i in range(2):
                                    nc.tensor.transpose(PS[:, 1 + n % 2, i * P:(i + 1) * P],
                                                        b_pad[:, i, 4 * n:4 * n + 4].rearrange("p t c -> p (t c)"), ident)
                                for i in range(2):
                                    mm = nc.tensor.transpose(PS[:, 1 + n % 2, (2 + i) * P:(3 + i) * P], c_in[:, i, n], ident)
                                mm.then_inc(turned, 1)

                with ExitStack() as run:
                    E = sbuf(run, "E", [P, 2, TILES, SPAN])
                    bu = sbuf(run, "bu", [P, 3, 2, 4, LEN])
                    z = sbuf(run, "z", [P, 2, 2, 4, LEN])
                    tmp = sbuf(run, "tmp", [P, 4 * LEN])
                    ends = sbuf(run, "ends", [P, 2, 2, 4])
                    driven, drive_copied, low_tabled, high_tabled = (
                        sem(f"ssm_{x}") for x in ("driven", "drive_copied", "low_tabled", "high_tabled"))
                    sine_made, imag_made, added = (sem(f"ssm_{x}") for x in ("sine_made", "imag_made", "added"))
                    stated, summed, ykept, pstep = (sem(f"ssm_{x}") for x in ("stated", "summed", "ykept", "pstep"))
                    LOW = 4

                    def make_table(eng, link, first, n, room):
                        e = E[:, :, first:first + n]
                        link(eng.memset(e[:, 0, :, 0:1], 1.0))
                        link(eng.memset(e[:, 1, :, 0:1], 0.0))
                        for k in range(LEVELS):
                            L = 2 ** k
                            m = min(L, SPAN - L)
                            pr, pi = (powers[:, i, k, first:first + n].unsqueeze(2).to_broadcast([P, n, m]) for i in range(2))
                            t = room[:, 0:n * m].rearrange("p (a b) -> p a b", b=m)
                            for part, other, op in ((0, 1, ALU.subtract), (1, 0, ALU.add)):
                                dst = e[:, part, :, L:L + m]
                                link(eng.tensor_tensor(dst, e[:, part, :, 0:m], pr, ALU.mult))
                                link(eng.tensor_tensor(t, e[:, other, :, 0:m], pi, ALU.mult))
                                link(eng.tensor_tensor(dst, dst, t, op))

                    def by_span(x):
                        return x.rearrange("p q (c t) -> p q c t", t=SPAN)

                    def turn(j, part):
                        return E[:, part, 4 * j:4 * j + 4].unsqueeze(2).to_broadcast([P, 4, LEN // SPAN, SPAN])

                    with nc.Block() as block:
                        @block.tensor
                        def _(pe):
                            def drive(j):
                                for i, part in enumerate((1, 0)):
                                    n = 2 * j + i
                                    if n >= 1:
                                        pe.wait_ge(drive_copied, n)
                                    for q in range(4):
                                        r = slice(32 * q, 32 * q + 32)
                                        mm = nc.tensor.matmul(PS[:, q, 0:LEN], BT[r, j, part], uT[r, j], start=True, stop=True)
                                    mm.then_inc(driven, 1)

                            for j in range(3):
                                drive(j)
                            for j in range(UB):
                                pe.wait_ge(stated, j + 1)
                                if j >= 2:
                                    pe.wait_ge(ykept, j - 1)
                                for q in range(4):
                                    r = slice(32 * q, 32 * q + 32)
                                    for i in range(4):
                                        x = (bu[:, j % 3, i // 2, q, META:LEN], z[:, j % 2, i // 2, q, META:LEN])[i % 2]
                                        mm = nc.tensor.matmul(PS[r, 4 + j % 2, 0:SEQ], CT[:, j, i // 2, r], x,
                                                              start=(i == 0), stop=(i == 3))
                                mm.then_inc(summed, 1)
                                if j + 3 < UB:
                                    drive(j + 3)

                        @block.scalar
                        def _(a):
                            for j in range(UB):
                                for i, part in enumerate((1, 0)):
                                    a.wait_ge(driven, 2 * j + i + 1)
                                    if j >= 3:
                                        a.wait_ge(summed, j - 2)
                                    nc.scalar.copy(bu[:, j % 3, part], PS[:, 0:4, 0:LEN]).then_inc(drive_copied, 1)

                        @block.gpsimd
                        def _(g):
                            steps_done = 0

                            def link(instruction):
                                nonlocal steps_done
                                steps_done += 1
                                instruction.then_inc(pstep, 1)
                                g.wait_ge(pstep, steps_done)

                            make_table(nc.gpsimd, link, 0, LOW, tmp)
                            g.sem_inc(low_tabled, 1)
                            t = by_span(tmp[:].rearrange("p (q t) -> p q t", q=4))
                            for j in range(UB):
                                b = j % 2
                                re, im = (by_span(bu[:, j % 3, part]) for part in range(2))
                                z_re, z_im = (by_span(z[:, b, part]) for part in range(2))
                                g.wait_ge(drive_copied, 2 * j + 1)
                                if j == 1:
                                    g.wait_ge(high_tabled, 1)
                                if j >= 2:
                                    g.wait_ge(summed, j - 1)
                                nc.gpsimd.tensor_tensor(z_im, turn(j, 0), im, ALU.mult).then_inc(pstep, 1)
                                g.wait_ge(drive_copied, 2 * j + 2)
                                if j >= 1:
                                    g.wait_ge(added, j)
                                nc.gpsimd.tensor_tensor(t, turn(j, 1), re, ALU.mult).then_inc(pstep, 1)
                                steps_done += 2
                                g.wait_ge(pstep, steps_done)
                                nc.gpsimd.tensor_tensor(z_im, z_im, t, ALU.subtract).then_inc(imag_made, 1)
                                nc.gpsimd.tensor_tensor(z_re, turn(j, 0), re, ALU.mult).then_inc(pstep, 1)
                                steps_done += 1
                                g.wait_ge(imag_made, j + 1)
                                nc.gpsimd.tensor_tensor(t, turn(j, 1), im, ALU.mult).then_inc(sine_made, 1)

                        @block.vector
                        def _(dve):
                            def link(instruction=None):
                                if instruction is not None:
                                    vec.tick(instruction)
                                dve.wait_ge(vec.sem, vec.value)

                            def keep(j):
                                dve.wait_ge(summed, j + 1)
                                nc.vector.scalar_tensor_tensor(y[:, j], uT[:, j, META:LEN], col("ssm_d", j), PS[:, 4 + j % 2, 0:SEQ],
                                                               ALU.mult, ALU.add).then_inc(ykept, 1)

                            make_table(nc.vector, link, LOW, TILES - LOW, z[:, 1].rearrange("p a q t -> p (a q t)"))
                            dve.sem_inc(high_tabled, 1)
                            dve.wait_ge(low_tabled, 1)
                            for j in range(UB):
                                b = j % 2
                                states = z[:, b].rearrange("p a q (c t) -> p a q c t", t=SPAN)
                                dve.wait_ge(sine_made, j + 1)
                                nc.vector.tensor_tensor(z[:, b, 0], z[:, b, 0], tmp[:].rearrange("p (q t) -> p q t", q=4),
                                                        ALU.add).then_inc(added, 1)
                                if j >= 1:
                                    keep(j - 1)
                                dve.wait_ge(added, j + 1)
                                dve.wait_ge(imag_made, j + 1)
                                for c in range(LEN // SPAN):
                                    if c >= 1:
                                        last = states[:, :, :, c - 1, SPAN - 1]
                                        first = states[:, :, :, c, 0]
                                        vec.tick(nc.vector.tensor_tensor(
                                            ends[:, 0], last, carry[:, 0:1, 4 * j:4 * j + 4].to_broadcast([P, 2, 4]), ALU.mult))
                                        link(nc.vector.tensor_tensor(ends[:, 1], last[:, ::-1], carry[:, 1:3, 4 * j:4 * j + 4], ALU.mult))
                                        link(nc.vector.tensor_tensor(first, first, ends[:, 0], ALU.add))
                                        link(nc.vector.tensor_tensor(first, first, ends[:, 1], ALU.add))
                                    for part in range(2):
                                        for q in range(4):
                                            at = states[:, part, q, c]
                                            vec.tick(nc.vector.tensor_tensor_scan(
                                                at, mag[:, 4 * j + q:4 * j + q + 1].to_broadcast([P, SPAN]), at,
                                                0.0, ALU.mult, ALU.add))
                                    link()
                                re, im = by_span(z[:, b, 0]), by_span(z[:, b, 1])
                                vec.tick(nc.vector.tensor_tensor(by_span(bu[:, j % 3, 0]), turn(j, 0), re, ALU.mult))
                                link(nc.vector.tensor_tensor(by_span(bu[:, j % 3, 1]), turn(j, 1), re, ALU.mult))
                                for q in range(4):
                                    vec.tick(nc.vector.scalar_tensor_tensor(re[:, q], turn(j, 1)[:, q], -1.0, im[:, q], ALU.mult, ALU.mult))
                                link()
                                nc.vector.tensor_tensor(im, turn(j, 0), im, ALU.mult).then_inc(stated, 1)
                            keep(UB - 1)
                with nc.Block() as block:
                    @block.scalar
                    def _(a):
                        act.tick(nc.scalar.activation(y, y, ACT.Gelu_apprx_tanh))

                ssm_out = sbuf(scope, "ssm_out", [P, DB, SEQ])
                gates = sbuf(scope, "gates", [P, 2, MB, SEQ])
                with ExitStack() as inner:
                    y_parts = sbuf(inner, "y_parts", [P, UB, 2, SEQ], F32R)

                    def glu_scalar(a, it, s, ready, taken):
                        if s % 2 == 0:
                            a.wait_ge(taken, it * 2 + s // 2 + 1)
                            nc.scalar.activation(gates[:, 0], PS[:, 0:4, 0:SEQ], ACT.Sigmoid).then_inc(ready, 1)
                            a.wait_ge(ready, it * 2 + s // 2 + 1)
                            a.sem_inc(banks_free[0], 1)

                    def glu_vector(dve, it, s, ready, taken):
                        if s % 2 == 1:
                            dve.wait_ge(ready, it * 2 + s // 2 + 1)
                            nc.vector.tensor_tensor(ssm_out[:, bass.ds(it * 8 + 4 * (s // 2), 4)], PS[:, 4:8, 0:SEQ], gates[:, 0],
                                                    ALU.mult).then_inc(taken, 1)
                            dve.wait_ge(taken, it * 2 + s // 2 + 2)
                            dve.sem_inc(banks_free[1], 1)
                    project_pair("glu", 2, lambda k: y_parts[:, k], glu_scalar, glu_vector, slabs=4,
                                 feed=feed_split(y_parts, y, UB))

                with ExitStack() as inner:
                    with ExitStack() as room:
                        inverse_rms(xT, DB, SEQ, sbuf(room, "squares", [P, DB, SEQ]))
                    nT = sbuf(inner, "nT", [P, DB, 2, SEQ], F32R)

                    def mix_scalar(a, it, s, ready, taken):
                        if s == 0:
                            a.wait_ge(taken, it + 1)
                        nc.scalar.activation(gates[:, s], PS[:, 4 * s:4 * s + 4, 0:SEQ], ACT.Sigmoid).then_inc(ready, 1)
                        a.wait_ge(ready, it * 2 + s + 1)
                        a.sem_inc(banks_free[s], 1)

                    def mix_vector(dve, it, s, ready, taken):
                        branch = (attn_out, ssm_out)[s][:, bass.ds(it * 4, 4)]
                        dve.wait_ge(ready, it * 2 + s + 1)
                        n = nc.vector.tensor_tensor(branch, branch, gates[:, s], ALU.mult).then_inc(mixed, 1)
                        if s == 1:
                            a_part = attn_out[:, bass.ds(it * 4, 4)]
                            dve.wait_ge(mixed, it * 2 + 2)
                            nc.vector.tensor_tensor(a_part, a_part, branch, ALU.add).then_inc(taken, 1)
                    mixed = sem("mixed")
                    project_pair("mix_gates", 4, lambda k: nT[:, k], mix_scalar, mix_vector,
                                 feed=feed_scaled(nT, xT, DB, SEQ, col("norm_mix", 0, DB), gates[:].rearrange("p a b t -> p (a b) t")))

            with ExitStack() as scope:
                mixed_parts = sbuf(scope, "mixed_parts", [P, DB, 2, SEQ], F32R)

                def residual(it, s, ps):
                    part = hT[:, bass.ds(it * 8 + 4 * s, 4), META:LEN]
                    return nc.vector.tensor_tensor(part, part, ps, ALU.add)
                project("w_out", 4, lambda k: mixed_parts[:, k], SEQ, residual,
                        feed=feed_split(mixed_parts, attn_out, DB))

        with ExitStack() as scope:
            with ExitStack() as room:
                inverse_rms(xT, DB, SEQ, sbuf(room, "squares", [P, DB, SEQ]))
            mT = sbuf(scope, "mT", [P, DB, 2, SEQ], F32R)
            hid = sbuf(scope, "hid", [P, MB * FF_PARTS[0][1], 2, SEQ], F32R)
            gates = sbuf(scope, "gates", [P, 2, MB, SEQ])
            result = sbuf(scope, "result", [P, MB, SEQ])
            for part, (first, n_slabs) in enumerate(FF_PARTS):
                made, parted = sem(f"hidden_made{part}"), sem(f"hidden_parted{part}")

                def ffn_scalar(a, it, s, ready, taken):
                    if s == 0:
                        a.wait_ge(taken, it + 1)
                        nc.scalar.activation(gates[:, 0], PS[:, 0:4, 0:SEQ], ACT.Sigmoid).then_inc(ready, 1)

                def ffn_vector(dve, it, s, ready, taken):
                    if s == 0:
                        dve.wait_ge(ready, it + 1)
                        nc.vector.tensor_tensor(gates[:, 1], PS[:, 0:4, 0:SEQ], gates[:, 0], ALU.mult).then_inc(banks_free[0], 1)
                        dve.wait_ge(banks_free[0], freed[0] + it + 1)
                        dve.sem_inc(taken, 1)
                    else:
                        dve.wait_ge(parted, 2 * it + 1)
                        nc.vector.tensor_tensor(result[:], PS[:, 4:8, 0:SEQ], gates[:, 1], ALU.mult).then_inc(banks_free[1], 1)
                        dve.wait_ge(banks_free[1], freed[1] + it + 1)
                        dve.sem_inc(made, 1)

                def ffn_parts(g, it, taken):
                    g.wait_ge(made, it + 1)
                    dst = hid[:, bass.ds(it * MB, MB)]
                    nc.gpsimd.tensor_copy(dst[:, :, 0], result[:]).then_inc(parted, 1)
                    g.wait_ge(parted, 2 * it + 2)
                    nc.gpsimd.tensor_tensor(dst[:, :, 1], result[:], dst[:, :, 0].bitcast(F32), ALU.subtract).then_inc(parted, 1)

                with nc.Block() as block:
                    @block.gpsimd
                    def _(g):
                        g.sem_inc(parted, 1)
                project_pair(f"ffn_up{part}", 4, lambda k: mT[:, k], ffn_scalar, ffn_vector, on_pool=ffn_parts,
                             feed=None if part else feed_scaled(mT, xT, DB, SEQ, col("norm_ffn", 0, DB),
                                                                gates[:].rearrange("p a b t -> p (a b) t")))

                ph_down = phases[f"ffn_down{part}"]
                with nc.Block() as block:
                    @block.sync
                    def _(sp):
                        stream(sp, ph_down)

                    @block.tensor
                    def _(pe):
                        for j in range(ph_down.upi):
                            for kt in range(KT):
                                wait_parts(pe, ph_down, 0, j, kt)
                                x = hid[:, (j // 4) * KT + kt]
                                for m in range(MB):
                                    M = 4 * (j % 4) + m
                                    mm = three_products(PS[:, M // 2, (M % 2) * SEQ:(M % 2 + 1) * SEQ], j % 2, kt,
                                                        slice(m * P, (m + 1) * P), x,
                                                        j < 4 and kt == 0 and M % 2 == 0, j >= ph_down.upi - 4 and kt == KT - 1)
                                release_parts(mm, j, kt)

                    @block.scalar
                    def _(a):
                        split_round(a, split_hi, ph_down, 0, ph_down.upi, None, False)

                    @block.vector
                    def _(dve):
                        def evacuate(it, s):
                            wait_slab(dve, ph_down, 0, 0, ph_down.upi)
                            vec.tick(nc.vector.tensor_tensor(xT, xT, PS[:, :, :].rearrange("p b (m t) -> p (b m) t", m=2), ALU.add))
                        split_round(dve, split_lo, ph_down, 0, ph_down.upi, evacuate, False)

        with ExitStack() as room:
            inverse_rms(xT, DB, SEQ, sbuf(room, "squares", [P, DB, SEQ]))
            scale_tokens(xT, xT, DB, SEQ, col("norm_final", 0, DB))

        with ExitStack() as two:
            gains = sbuf(two, "gains", [P, DB])

            def modulated(dst, gain, mod, room):
                return feed_scaled(dst, xT, DB, SEQ, gains, room, mod[:, 0:DB], prologue=(
                    lambda: nc.vector.scalar_tensor_tensor(gains[:], mod[:, DB:2 * DB], 1.0, gain, ALU.add, ALU.mult),))

            def post_norm(y_out, gain, gate, squares):
                inverse_rms(y_out, DB, SEQ, squares)
                with nc.Block() as block:
                    v0 = vec.value

                    @block.vector
                    def _(dve):
                        dve.wait_ge(vec.sem, vec.tick(nc.vector.tensor_tensor(gains[:], gain, gate, ALU.mult)))
                        for k in range(DB):
                            vec.tick(nc.vector.scalar_tensor_tensor(y_out[:, k], y_out[:, k], gains[:, k:k + 1], rms[:, 0:SEQ],
                                                                    ALU.mult, ALU.mult))
                        dve.wait_ge(vec.sem, vec.value)
                        vec.tick(nc.vector.tensor_tensor(xT[:, DB // 2:], xT[:, DB // 2:], y_out[:, DB // 2:], ALU.add))

                    @block.gpsimd
                    def _(g):
                        for q in range(2):
                            k = slice(q * MB, (q + 1) * MB)
                            g.wait_ge(vec.sem, v0 + 1 + (q + 1) * MB)
                            pool.tick(nc.gpsimd.tensor_tensor(xT[:, k], xT[:, k], y_out[:, k], ALU.add))

            with ExitStack() as scope:
                qk = sbuf(scope, "qk", [P, 2 * A_QK // P, SEQ])
                heads_view = qk[:].rearrange("p (r h e) t -> p r h e t", r=2, e=2)
                with ExitStack() as inner:
                    hn = sbuf(inner, "hn", [P, DB, 2, SEQ], F32R)
                    with ExitStack() as proj:
                        pick = mod_room[0:A_HEADS].rearrange("p a b -> p (a b)")
                        va = sbuf(proj, "va", [P, 2, A_INNER])
                        inverse_rms(xT, DB, SEQ, qk)

                        project("a_qk", 4, lambda k: hn[:, k], SEQ,
                                lambda it, s, ps: nc.vector.tensor_copy(qk[:, bass.ds(it * 8 + 4 * s, 4)], ps),
                            feed=modulated(hn, col("g_pre_2", 0, DB), mods[:, 0:3 * DB], qk[:, 0:8]))

                        ph_v = phases["a_v"]
                        conv_step = sem("conv_step")
                        with ExitStack() as conv:
                            acc = sbuf(conv, "acc", [P, MB, SEQ])
                            term = sbuf(conv, "term", [P, MB, SEQ])
                            with nc.Block() as block:
                                @block.sync
                                def _(sp):
                                    stream(sp, ph_v)

                                values_by_token(ph_v, block, hn, va)

                                @block.vector
                                def _(dve):
                                    def convolve(it, j):
                                        j -= 1
                                        quarter = (j - 1) % 4
                                        b = it * 2 + (j - 1) // 4
                                        part = qk[:, bass.ds(b * MB, MB)]
                                        bias = cols[:, bass.ds(b * MB + 3 * P, MB)].unsqueeze(2).to_broadcast([P, MB, SEQ])

                                        def step(i, out_, in0, in1, op):
                                            dve.wait_ge(conv_step, it * 18 + (j - 1) // 4 * 9 + i + 1)
                                            nc.vector.tensor_tensor(out_, in0, in1, op).then_inc(conv_step, 1)

                                        def tapped(out_, back):
                                            n = SEQ - back
                                            weight = cols[:, bass.ds(b * MB + 32 * (CONV - 1 - back), MB)].unsqueeze(2)
                                            return out_[:, :, 0:n], part[:, :, 0:n], weight.to_broadcast([P, MB, n]), ALU.mult

                                        if quarter == 0:
                                            step(0, *tapped(acc, 0))
                                            step(1, acc[:], acc[:], bias, ALU.add)
                                        else:
                                            step(2 * quarter, *tapped(term, quarter))
                                            late = slice(quarter, SEQ)
                                            dst = acc if quarter < CONV - 1 else part
                                            step(2 * quarter + 1, dst[:, :, late], acc[:, :, late], term[:, :, 0:SEQ - quarter], ALU.add)
                                        if quarter == CONV - 1:
                                            dve.wait_ge(conv_step, it * 18 + (j - 1) // 4 * 9 + 9)
                                            nc.vector.tensor_scalar(part[:, :, 0:CONV - 1], acc[:, :, 0:CONV - 1], 1.0, None,
                                                                    ALU.mult).then_inc(conv_step, 1)

                                    dve.sem_inc(conv_step, 1)
                                    with dve.Fori(0, ph_v.iters) as it:
                                        split_round(dve, split_lo, ph_v, it, 4, None, False, convolve)
                            for s in range(2):
                                freed[s] += ph_v.iters
                            with nc.Block() as block:
                                base_a, base_v = act.value, vec.value

                                @block.scalar
                                def _(a):
                                    for b in range(8):
                                        if b >= 2:
                                            a.wait_ge(vec.sem, base_v + b - 1)
                                        act.tick(nc.scalar.activation((acc, term)[b % 2][:], qk[:, b * MB:(b + 1) * MB], ACT.Sigmoid))

                                @block.vector
                                def _(dve):
                                    for b in range(8):
                                        dve.wait_ge(act.sem, base_a + b + 1)
                                        part = qk[:, b * MB:(b + 1) * MB]
                                        vec.tick(nc.vector.tensor_tensor(part, part, (acc, term)[b % 2][:], ALU.mult))

                        gate_rows = sbuf(proj, "gate_rows", [A_HEADS, 5, SEQ])
                        FORGET = 32
                        with ExitStack() as gate_room, nc.Block() as block:
                            w_g = sbuf(gate_room, "w_g", [P, DB, FORGET + A_HEADS])
                            b_g = sbuf(gate_room, "b_g", [A_HEADS, 2])
                            gates_in = small[0] + 64
                            w_g_zeroed = pool.value + 1
                            gated = ten.value + 1
                            a0, v0 = act.value, vec.value

                            @block.sync
                            def _(sp):
                                sp.wait_ge(pool.sem, w_g_zeroed)
                                for g in range(2):
                                    first = A_G0 + g * A_HEADS
                                    load_small(sp, w_g[:, :, g * FORGET:g * FORGET + A_HEADS],
                                               w["a_w_in_2"][:, first:first + A_HEADS].rearrange("(k p) n -> p k n", p=P))
                                load_small(sp, pick, w["head_pick"])
                                load_small(sp, b_g[:], w["a_gate_b_2"])

                            @block.tensor
                            def _(pe):
                                pe.wait_ge(small_loaded, gates_in)
                                for k in range(DB):
                                    for part in range(2):
                                        mm = nc.tensor.matmul(PS[0:FORGET + A_HEADS, 0, 0:SEQ], w_g[:, k],
                                                              hn[:, k, part].bitcast(F32), start=(k == 0 and part == 0),
                                                              stop=(k == DB - 1 and part == 1))
                                ten.tick(mm)

                            @block.gpsimd
                            def _(g):
                                pool.tick(nc.gpsimd.memset(w_g[:], 0.0))

                            @block.scalar
                            def _(a):
                                a.wait_ge(vec.sem, v0 + 2)
                                for fn, dst, src, kw in ((ACT.Abs, ABS, FG_, {}), (ACT.Exp, ABS, ABS, {"scale": -1.0}),
                                                         (ACT.Ln, ABS, ABS, {"bias": ones[0:A_HEADS, 0:1]})):
                                    n = act.tick(nc.scalar.activation(gate_rows[:, dst], gate_rows[:, src], fn, **kw))
                                    a.wait_ge(act.sem, n)
                                a.wait_ge(vec.sem, v0 + 9)
                                act.tick(nc.scalar.activation(gate_rows[:, EN], gate_rows[:, EN], ACT.Exp, scale=-1.0))

                            @block.vector
                            def _(dve):
                                def link(instruction):
                                    dve.wait_ge(vec.sem, vec.tick(instruction))
                                dve.wait_ge(ten.sem, gated)
                                link(nc.vector.tensor_scalar(gate_rows[:, I], PS[0:A_HEADS, 0, 0:SEQ], b_g[:, 0:1], None, ALU.add))
                                link(nc.vector.tensor_scalar(gate_rows[:, FG_], PS[FORGET:FORGET + A_HEADS, 0, 0:SEQ], b_g[:, 1:2], None, ALU.add))
                                dve.wait_ge(act.sem, a0 + 3)
                                link(nc.vector.tensor_scalar(gate_rows[:, FG_], gate_rows[:, FG_], 0.0, None, ALU.min))
                                link(nc.vector.tensor_tensor(gate_rows[:, FG_], gate_rows[:, FG_], gate_rows[:, ABS], ALU.subtract))
                                link(nc.vector.tensor_tensor_scan(gate_rows[:, CUM], ones[0:A_HEADS, 0:1].to_broadcast([A_HEADS, SEQ]),
                                                                  gate_rows[:, FG_], 0.0, ALU.mult, ALU.add))
                                link(nc.vector.tensor_tensor(gate_rows[:, A_], gate_rows[:, I], gate_rows[:, CUM], ALU.subtract))
                                link(nc.vector.memset(gate_rows[:, ZERO], 0.0))
                                link(nc.vector.tensor_tensor_scan(gate_rows[:, MM], gate_rows[:, A_], gate_rows[:, ZERO], 0.0, ALU.max, ALU.max))
                                link(nc.vector.tensor_tensor(gate_rows[:, EN], gate_rows[:, CUM], gate_rows[:, MM], ALU.add))

                        mlstm_heads(nc, sem, sbuf, PS, gate_rows, qk, va, ident, ones, after, pick)

                    with ExitStack() as hs:
                        rms_head = sbuf(hs, "rms_head", [P, A_HEADS, SEQ])
                        sq = sbuf(hs, "sq", [P, 3, 4, SEQ])
                        halved = sem("head_halved")
                        squared, hsum, sq_used = sem("head_squared"), sem("head_summed"), sem("head_rooted")
                        with nc.Block() as block:
                            @block.gpsimd
                            def _(g):
                                for h in range(A_HEADS):
                                    g.wait_ge(squared, h + 1)
                                    nc.gpsimd.tensor_tensor(sq[:, h % 3, 0:2], sq[:, h % 3, 0:2], sq[:, h % 3, 2:4], ALU.add).then_inc(halved, 1)

                            @block.tensor
                            def _(pe):
                                for h in range(A_HEADS):
                                    pe.wait_ge(halved, h + 1)
                                    if h >= 4:
                                        pe.wait_ge(sq_used, h - 3)
                                    for e in range(2):
                                        mm = nc.tensor.matmul(PS[:, h % 4, 0:SEQ], ones[:], sq[:, h % 3, e], start=(e == 0), stop=(e == 1))
                                    mm.then_inc(hsum, 1)

                            @block.scalar
                            def _(a):
                                for h in range(A_HEADS + 2):
                                    if h < A_HEADS:
                                        if h >= 3:
                                            a.wait_ge(hsum, h - 2)
                                        nc.scalar.activation(sq[:, h % 3].rearrange("p (r e) t -> p r e t", r=2), heads_view[:, :, h],
                                                             ACT.Square).then_inc(squared, 1)
                                    n = h - 2
                                    if n >= 0:
                                        a.wait_ge(hsum, n + 1)
                                        nc.scalar.activation(rms_head[:, n], PS[:, n % 4, 0:SEQ], ACT.Sqrt, scale=1.0 / A_DV,
                                                             bias=eps[:, 0:1]).then_inc(sq_used, 1)

                            @block.vector
                            def _(dve):
                                def link():
                                    dve.wait_ge(vec.sem, vec.value)
                                for h in range(A_HEADS):
                                    dve.wait_ge(sq_used, h + 1)
                                    vec.tick(nc.vector.reciprocal(rms_head[:, h], rms_head[:, h]))
                                    link()
                                    for e in range(4):
                                        ht = heads_view[:, e // 2, h, e % 2]
                                        vec.tick(nc.vector.scalar_tensor_tensor(ht, ht, col("a_g_head_2", 4 * h + e), rms_head[:, h], ALU.mult, ALU.mult))

                    gates = sbuf(inner, "gates", [P, 2, MB, SEQ])

                    def oz_scalar(a, it, s, ready, taken):
                        if s == 0:
                            a.wait_ge(taken, it + 1)
                        nc.scalar.activation(gates[:, s], PS[:, 4 * s:4 * s + 4, 0:SEQ], ACT.Sigmoid).then_inc(ready, 1)
                        if s == 0:
                            a.wait_ge(ready, it * 2 + 1)
                            a.sem_inc(banks_free[0], 1)

                    def oz_vector(dve, it, s, ready, taken):
                        if s == 0:
                            return
                        dve.wait_ge(ready, it * 2 + 2)
                        nc.vector.tensor_tensor(gates[:, 1], PS[:, 4:8, 0:SEQ], gates[:, 1], ALU.mult).then_inc(banks_free[1], 1)
                        dve.wait_ge(banks_free[1], freed[1] + it + 1)
                        nc.vector.tensor_tensor(gates[:, 0], gates[:, 0], gates[:, 1], ALU.mult).then_inc(gated_twice, 1)

                    def oz_apply(g, it, taken):
                        g.wait_ge(gated_twice, it + 1)
                        ht = qk[:].rearrange("p (r b) t -> p r b t", r=2)[:, :, bass.ds(it * 2, 2)]
                        nc.gpsimd.tensor_tensor(ht, ht, gates[:, 0].rearrange("p (r e) t -> p r e t", r=2), ALU.mult).then_inc(taken, 1)
                    gated_twice = sem("gated_twice")
                    project_pair("a_oz", 4, lambda k: hn[:, k], oz_scalar, oz_vector, on_pool=oz_apply)
                y_parts = sbuf(scope, "y_parts", [P, A_INNER // P, 2, SEQ], F32R)
                in_halves = qk[:].rearrange("p (r b) t -> p r b t", r=2)
                parts_in_halves = y_parts[:].rearrange("p (r b) c t -> p r b c t", r=2)
                groups = [(parts_in_halves[:, :, 2 * q:2 * q + 2, 0], parts_in_halves[:, :, 2 * q:2 * q + 2, 1],
                           in_halves[:, :, 2 * q:2 * q + 2]) for q in range(8)]
                y_out, room = qk[:, 0:DB], qk[:, DB:2 * DB]
                project("a_out", 8, lambda k: y_parts[:, k % 4 // 2 * DB + k // 4 * 2 + k % 2], SEQ,
                        lambda it, s, ps: nc.vector.tensor_copy(qk[:, bass.ds(it * 8 + 4 * s, 4)], ps),
                        feed=feed_parts(groups))
                post_norm(y_out, col("g_post_2", 0, DB), mods[:, 2 * DB:3 * DB], room)

            with ExitStack() as scope:
                kb = sbuf(scope, "kb", [P, DB, SEQ])
                vb = sbuf(scope, "vb", [P, 2, D])
                qb = sbuf(scope, "qb", [P, DB, SEQ])
                zb = sbuf(scope, "zb", [P, DB, SEQ])
                rel_loaded, rel_stored = sem("rel_loaded"), sem("rel_stored")
                rel = sbuf(scope, "rel", [HEADS, 2 * MAX_REL + 1])
                drawn = sbuf(scope, "drawn", [HEADS, 3 * P])
                with ExitStack() as inner:
                    hn = sbuf(inner, "hn", [P, DB, 2, SEQ], F32R)
                    inverse_rms(xT, DB, SEQ, kb)
                    project("b_k", 4, lambda k: hn[:, k], SEQ,
                            lambda it, s, ps: nc.vector.tensor_copy(kb[:, bass.ds(it * 8 + 4 * s, 4)], ps),
                            feed=modulated(hn, col("kv_g_2", 0, DB), mods[:, 6 * DB:8 * DB], kb[:, 0:8]))
                    ph_v = phases["b_v"]
                    with nc.Block() as block:
                        @block.sync
                        def _(sp):
                            stream(sp, ph_v)

                        values_by_token(ph_v, block, hn, vb)

                        @block.gpsimd
                        def _(g):
                            g.dma_start(rel[:], w["b_rel_2"]).then_inc(rel_loaded, 16)
                            g.wait_ge(rel_loaded, 16)
                            pool.tick(nc.gpsimd.tensor_copy(drawn[:, 2 * P:3 * P], rel[:, 2 * MAX_REL:2 * MAX_REL + 1].to_broadcast([HEADS, P])))
                            n = pool.tick(nc.gpsimd.tensor_copy(drawn[:, 0:2 * P], rel[:, 1:2 * MAX_REL + 1]))
                            g.wait_ge(pool.sem, n)
                            g.dma_start(w["rel_scratch"], drawn[:]).then_inc(rel_stored, 16)
                            g.wait_ge(rel_stored, 16)

                        @block.vector
                        def _(dve):
                            with dve.Fori(0, ph_v.iters) as it:
                                split_round(dve, split_lo, ph_v, it, 4, None, False)
                    for s in range(2):
                        freed[s] += ph_v.iters
                    project("b_q", 4, lambda k: hn[:, k], SEQ,
                            lambda it, s, ps: nc.vector.tensor_copy(qb[:, bass.ds(it * 8 + 4 * s, 4)], ps),
                            feed=modulated(hn, col("g_pre_2", DB, DB), mods[:, 3 * DB:6 * DB], qb[:, 0:8]))
                    project("b_z", 4, lambda k: hn[:, k], SEQ,
                            lambda it, s, ps: nc.vector.tensor_copy(zb[:, bass.ds(it * 8 + 4 * s, 4)], ps))

                with ExitStack() as inner:
                    bias = sbuf(inner, "bias", [P, HEADS, SEQ])
                    with nc.Block() as block:
                        spread_done = small[0] + 16

                        @block.sync
                        def _(sp):
                            scratch = w["rel_scratch"]
                            load_small(sp, bias[:], bass.AP(tensor=scratch.tensor, offset=scratch.offset,
                                                            ap=[[1, P], [3 * P, HEADS], [1, SEQ]]))

                        @block.vector
                        def _(dve):
                            dve.wait_ge(small_loaded, spread_done)
                            vec.tick(nc.vector.memset(bias[0:CHUNK, :, 0:CHUNK], NEG))

                    def band_keys(n):
                        return P * (n % 2 + 1)

                    attention("band", HEADS, lambda n: [(qb[:, n // 2, (n % 2) * P:(n % 2 + 1) * P], kb[:, n // 2, 0:band_keys(n)])],
                              band_keys, lambda n: bias[:, n // 2, 0:band_keys(n)][:, ::-1], P ** -0.5, vb, qb)
                with nc.Block() as block:
                    base_a = act.value

                    @block.scalar
                    def _(a):
                        act.tick(nc.scalar.activation(kb[:], zb[:], ACT.Sigmoid))

                    @block.vector
                    def _(dve):
                        n = vec.tick(nc.vector.tensor_tensor(qb[:], qb[:], zb[:], ALU.mult))
                        dve.wait_ge(vec.sem, n)
                        dve.wait_ge(act.sem, base_a + 1)
                        vec.tick(nc.vector.tensor_tensor(qb[:], qb[:], kb[:], ALU.mult))
                with ExitStack() as inner:
                    y_parts = sbuf(inner, "y_parts", [P, DB, 2, SEQ], F32R)
                    project("b_out", 4, lambda k: y_parts[:, k], SEQ,
                            lambda it, s, ps: nc.vector.tensor_copy(kb[:, it * 8 + 4 * s:it * 8 + 4 * s + 4], ps), static=True, follows=False,
                            feed=feed_split(y_parts, qb, DB))
                post_norm(kb[:], col("g_post_2", DB, DB), mods[:, 5 * DB:6 * DB], qb)

        with ExitStack() as scope:
            rows_out = sbuf(scope, "rows_out", [P, 2, D])
            turned, copied = sem("output_turned"), sem("output_copied")
            with nc.Block() as block:
                @block.tensor
                def _(pe):
                    for n in range(8):
                        if n >= 4:
                            pe.wait_ge(copied, n - 3)
                        for q in range(4):
                            k, t = (n % 4) * 4 + q, n // 4
                            mm = nc.tensor.transpose(PS[:, n % 4, q * P:(q + 1) * P], xT[:, k, t * P:(t + 1) * P], ident)
                        mm.then_inc(turned, 1)

                @block.vector
                def _(dve):
                    for n in range(8):
                        dve.wait_ge(turned, n + 1)
                        nc.vector.tensor_copy(rows_out[:, n // 4, (n % 4) * COLS:(n % 4 + 1) * COLS], PS[:, n % 4, :]).then_inc(copied, 1)

                @block.sync
                def _(sp):
                    for t in range(2):
                        sp.wait_ge(copied, 4 * t + 4)
                        sp.dma_start(out[t * P:(t + 1) * P, :], rows_out[:, t]).then_inc(stored, 16)
                    sp.wait_ge(stored, 32)


def mlstm_heads(nc, sem, sbuf, PS, gate_rows, qk, va, ident, ones, after, head_pick):
    QB = A_DK // P
    W0 = SEQ + P
    with ExitStack() as scope:
        a_cols = sbuf(scope, "a_cols", [P, 2, A_HEADS])
        wt = sbuf(scope, "wt", [P, 2, W0])
        st = sbuf(scope, "st", [P, 2, W0])
        den = sbuf(scope, "den", [P, 2, SEQ])
        spread, scored, a_turned, a_kept = (sem(f"mlstm_{x}") for x in ("spread", "scored", "a_turned", "a_kept"))
        masked, exped, weighted, valued = (sem(f"mlstm_{x}") for x in ("masked", "exped", "weighted", "valued"))
        den_summed, absed, kept, dstep = (sem(f"mlstm_{x}") for x in ("den_summed", "absed", "kept", "dstep"))
        spread_bank = (0, 1, 7)
        with nc.Block() as block:
            @block.tensor
            def _(pe):
                for b in range(2):
                    mm = nc.tensor.transpose(PS[:, 7, 8 * b:8 * b + 8], gate_rows[:, A_, b * P:(b + 1) * P], ident[0:A_HEADS, 0:A_HEADS])
                mm.then_inc(a_turned, 1)

                def front(h):
                    if h == 2:
                        pe.wait_ge(a_kept, 1)
                    if h >= 3:
                        pe.wait_ge(kept, h - 2)
                    for i, r in enumerate((MM, EN)):
                        mm = nc.tensor.matmul(PS[:, spread_bank[h % 3], i * SEQ:(i + 1) * SEQ], head_pick[0:A_HEADS, h * P:(h + 1) * P],
                                              gate_rows[:, r], start=True, stop=True)
                    mm.then_inc(spread, 1)
                    if h >= 2:
                        pe.wait_ge(weighted, h - 1)
                    for b in range(2):
                        dst = PS[:, 2 + h % 2, b * SEQ:b * SEQ + SEQ - b * P]
                        for i in range(QB):
                            mm = nc.tensor.matmul(dst, qk[:, A_QK // P + QB * h + i, b * P:(b + 1) * P], qk[:, QB * h + i, b * P:SEQ],
                                                  start=(i == 0), stop=(i == QB - 1))
                    mm.then_inc(scored, 1)

                front(0)
                front(1)
                for h in range(A_HEADS):
                    pe.wait_ge(weighted, h + 1)
                    if h >= 1:
                        pe.wait_ge(kept, h)
                    for e in (4, 0, 1, 2, 3):
                        dst = PS[:, 4 + e // 2, (e % 2) * SEQ:(e % 2 + 1) * SEQ]
                        for b in range(2):
                            lhsT = va[:, b, h * A_DV + e * P:h * A_DV + (e + 1) * P] if e < 4 else ones[:]
                            mm = nc.tensor.matmul(dst[:, b * P:SEQ], lhsT, st[:, h % 2, b * SEQ:b * SEQ + SEQ - b * P],
                                                  start=(b == 0), stop=(b == 1))
                        if e == 4:
                            mm.then_inc(den_summed, 1)
                    mm.then_inc(valued, 1)
                    if h + 2 < A_HEADS:
                        front(h + 2)

            @block.scalar
            def _(a):
                def weight_exp(h):
                    a.wait_ge(masked, h + 1)
                    nc.scalar.activation(wt[:, h % 2, 0:SEQ], wt[:, h % 2, 0:SEQ], ACT.Exp, scale=-1.0, bias=a_cols[:, 0, h:h + 1])
                    nc.scalar.activation(wt[:, h % 2, SEQ:W0], wt[:, h % 2, SEQ:W0], ACT.Exp, scale=-1.0,
                                         bias=a_cols[:, 1, h:h + 1]).then_inc(exped, 1)

                a.wait_ge(a_kept, 1)
                weight_exp(0)
                weight_exp(1)
                for h in range(A_HEADS):
                    denominator(nc, a, h, den_summed, absed, den, PS)
                    if h + 2 < A_HEADS:
                        weight_exp(h + 2)

            @block.vector
            def _(dve):
                steps = 0

                def link(instruction):
                    nonlocal steps
                    steps += 1
                    instruction.then_inc(dstep, 1)
                    dve.wait_ge(dstep, steps)

                def mask(h):
                    dve.wait_ge(spread, h + 1)
                    b, bank = h % 2, spread_bank[h % 3]
                    if h >= 2:
                        dve.wait_ge(weighted, h - 1)
                    nc.vector.tensor_tensor(wt[:, b, 0:SEQ], PS[:, bank, 0:SEQ], after, ALU.add)
                    nc.vector.tensor_tensor(wt[:, b, SEQ:W0], PS[:, bank, P:SEQ], after[:, 0:P], ALU.add).then_inc(masked, 1)

                def weigh(h):
                    b = h % 2
                    dve.wait_ge(scored, h + 1)
                    dve.wait_ge(exped, h + 1)
                    if h >= 2:
                        dve.wait_ge(valued, h - 1)
                    nc.vector.scalar_tensor_tensor(st[:, b], PS[:, 2 + b, 0:W0], A_DK ** -0.5, wt[:, b], ALU.mult, ALU.mult).then_inc(weighted, 1)

                dve.wait_ge(a_turned, 1)
                nc.vector.tensor_copy(a_cols[:], PS[:, 7, 0:16].rearrange("p (b h) -> p b h", b=2)).then_inc(a_kept, 1)
                mask(0)
                mask(1)
                weigh(0)
                for h in range(A_HEADS):
                    b = h % 2
                    if h + 1 < A_HEADS:
                        weigh(h + 1)
                    dve.wait_ge(absed, h + 1)
                    link(nc.vector.tensor_tensor(den[:, b], den[:, b], PS[:, spread_bank[h % 3], SEQ:2 * SEQ], ALU.max))
                    link(nc.vector.reciprocal(den[:, b], den[:, b]))
                    dve.wait_ge(valued, h + 1)
                    for r in range(2):
                        dst = qk[:, r * (A_QK // P) + QB * h:r * (A_QK // P) + QB * h + QB]
                        last = nc.vector.tensor_tensor(dst, PS[:, 4 + r, :].rearrange("p (e t) -> p e t", e=2),
                                                       den[:, b].unsqueeze(1).to_broadcast([P, 2, SEQ]), ALU.mult)
                    last.then_inc(kept, 1)
                    if h + 2 < A_HEADS:
                        mask(h + 2)


def denominator(nc, a, h, den_summed, absed, den, PS):
    a.wait_ge(den_summed, h + 1)
    nc.scalar.activation(den[:, h % 2], PS[:, 6, 0:SEQ], ACT.Abs).then_inc(absed, 1)


def shape_constants():
    import numpy as np
    a = np.zeros((P, CONST_COLS), np.float32)
    one = np.zeros((P, 3 * LEN), np.float32)

    def put(name, value):
        dst, (first, n) = (a, CONST[name]) if name in CONST else (one, CONST_ONE[name])
        dst[:, first:first + n] = value

    put("identity", np.eye(P, dtype=np.float32))
    half = ROPE // 2
    freqs = np.float32(10000.0) ** (-np.arange(half, dtype=np.float32) / np.float32(half))
    ang = np.arange(LEN, dtype=np.float32)[None, :] * freqs[:, None]
    put("cos", np.tile(np.cos(ang), (4, 1)))
    put("sin", np.tile(np.concatenate([-np.sin(ang), np.sin(ang)]), (2, 1)))
    p = np.arange(P)[:, None]
    put("causal", np.where(np.arange(LEN)[None, :] <= P + META + p, 0.0, NEG))
    put("after", np.where(np.arange(SEQ)[None, :] < p, -NEG, 0.0))
    return a, one


_MATRICES = ["w_in", "w_kv_up", "w_attn_proj", "w_glu_val", "w_glu_gate", "w_out", "w_ffn_gate", "w_ffn_up",
             "w_ffn_down", "a_w_in_2", "a_w_out_2", "b_w_in_2", "b_w_out_2"]


def kernel(**inputs):
    import numpy as np
    import concourse.bacc as bacc
    from concourse.bass_utils import run_bass_kernel_spmd as run

    nc = bacc.Bacc("TRN2", target_bir_lowering=False, num_devices=1)
    arrays, w = {}, {}

    def give(name, a):
        a = np.ascontiguousarray(a)
        arrays[f"in_{name}"] = a
        w[name] = nc.dram_tensor(f"in_{name}", a.shape, F32, kind="ExternalInput").ap()

    for name in _MATRICES:
        give(name, np.asarray(inputs[name])[0])
    q_up = np.asarray(inputs["w_q_up"])[0].reshape(LORA, HEADS // 2, 2, NOPE + ROPE)
    give("w_q_up", np.concatenate([q_up[..., :NOPE].reshape(LORA, HEADS // 2, -1),
                                   q_up[..., NOPE:].reshape(LORA, HEADS // 2, -1)], axis=2).reshape(LORA, -1))
    ada = np.asarray(inputs["ada_w_2"])
    give("ada_all", np.concatenate([ada[0], ada[1], np.asarray(inputs["kv_ada_w_2"])], axis=1))
    for name in ("kv_w_2", "meta_tokens"):
        give(name, inputs[name])
    for name in ("ssm_lambda_re", "ssm_lambda_im", "ssm_log_step", "ssm_b_re", "ssm_b_im", "ssm_c_re", "ssm_c_im",
                 "b_rel_2", "x"):
        give(name, np.asarray(inputs[name])[0])
    give("a_gate_b_2", np.asarray(inputs["a_gate_b_2"])[0].reshape(2, A_HEADS).T)
    for name in VECTOR_ROWS:
        give(name + "_rows", np.asarray(inputs[name]).reshape(-1, P))
    for name, value in zip(("shape_constants", "shape_constants_one"), shape_constants()):
        give(name, value)
    give("head_pick", np.kron(np.eye(A_HEADS), np.ones((1, P))).astype(np.float32))
    w["rel_scratch"] = nc.dram_tensor("rel_scratch", (HEADS, 3 * P), F32, kind="Internal").ap()
    out = nc.dram_tensor("out_x", (SEQ, D), F32, kind="ExternalOutput").ap()
    build(nc, w, out)
    r = run(nc, [arrays], core_ids=[0])
    return r.results[0]["out_x"].reshape(1, SEQ, D)
```
